# Optimizing a Trainium2 kernel written in Bass

```python
import math
import numpy as np
import jax
import jax.numpy as jnp
from jax import lax

D_MODEL = 2048
BATCH = 1
SEQ = 256
DEPTH = 1
DEC_BATCH = 8
DEC_SEQ = 1
PAST_LEN = 1024
PAGE_SIZE = 128

HEAD_DIM = 128
NSA_HEADS = 8
NSA_KV = 2
NSA_REP = NSA_HEADS // NSA_KV
CMP_STRIDE = 16
CMP_LEN = 2 * CMP_STRIDE
SLC_LEN = 64
SLC_TOPN = 16
WINDOW = 512
SLC_QBLOCK = 64
WIN_QBLOCK = 128
DN_HEADS = 8
DN_DK = 128
DN_DV = 128
DN_QKV = DN_HEADS * (2 * DN_DK + DN_DV)
DN_CONV = 4
DN_CHUNK = 64
PEER_HEADS = 8
PEER_NKEYS = 128
PEER_EXPERTS = PEER_NKEYS * PEER_NKEYS
PEER_DKEY = 256
PEER_TOPK = 16
PEER_TBLOCK = 128
ROPE_THETA = 10000.0
EPS = 1e-6
NEG = -1e30
IN_SPLITS = (NSA_HEADS * HEAD_DIM, 6 * NSA_KV * HEAD_DIM, NSA_HEADS * 3, DN_QKV, DN_HEADS, DN_HEADS, DN_HEADS * DN_DV, 2 * D_MODEL)
IN_WIDTH = sum(IN_SPLITS)
F32 = jnp.float32

kernel_name = 'nsa_gdn_peer_hybrid_step'

def _split_cols(a, sizes):
    return jnp.split(a, [int(s) for s in np.cumsum(sizes)[:-1]], axis=-1)

def _rmsnorm(x, w):
    xf = x.astype(F32)
    return xf * lax.rsqrt(jnp.mean(xf * xf, axis=-1, keepdims=True) + EPS) * w.astype(F32)

def _l2norm(x):
    xf = x.astype(F32)
    return xf * lax.rsqrt(jnp.sum(xf * xf, axis=-1, keepdims=True) + EPS)

def _rope(x, pos):
    half = HEAD_DIM // 2
    inv = ROPE_THETA ** (-jnp.arange(half, dtype=F32) / half)
    ang = jnp.asarray(pos, F32)[:, None] * inv
    cos = jnp.cos(ang)[:, None, :]
    sin = jnp.sin(ang)[:, None, :]
    x1 = x[..., :half].astype(F32)
    x2 = x[..., half:].astype(F32)
    return jnp.concatenate([x1 * cos - x2 * sin, x1 * sin + x2 * cos], axis=-1)

def _compress(rows, w, b):
    B, L = rows.shape[:2]
    n_cmp = (L - CMP_LEN) // CMP_STRIDE + 1
    n_chunk = -(-L // CMP_STRIDE)
    rows = jnp.pad(rows, ((0, 0), (0, n_chunk * CMP_STRIDE - L), (0, 0), (0, 0)))
    ch = rows.reshape(B, n_chunk, CMP_STRIDE, NSA_KV, HEAD_DIM)
    first = jnp.einsum('bnjgd,jd->bngd', ch, w[:CMP_STRIDE])
    second = jnp.einsum('bnjgd,jd->bngd', ch, w[CMP_STRIDE:])
    return first[:, :n_cmp] + second[:, 1:n_cmp + 1] + b

def _overlap(n_cmp, n_slc):
    cs = np.arange(n_cmp)[:, None] * CMP_STRIDE
    ss = np.arange(n_slc)[None, :] * SLC_LEN
    return ((cs < ss + SLC_LEN) & (cs + CMP_LEN > ss)).astype(np.float32)

def _nsa(q, kc, vc, ks, vs, kw, vw, gate, q_off, w_off, P):
    B, Tq = q.shape[:2]
    L = kc.shape[1]
    scale = HEAD_DIM ** -0.5
    qpos = q_off + np.arange(Tq)
    qg = q.astype(F32).reshape(B, Tq, NSA_KV, NSA_REP, HEAD_DIM)

    n_cmp = (L - CMP_LEN) // CMP_STRIDE + 1
    cpos = np.arange(n_cmp) * CMP_STRIDE + CMP_LEN - 1
    ck = _rope(_compress(kc, P['w_cmp_k'], P['b_cmp_k']), cpos)
    cv = _compress(vc, P['w_cmp_v'], P['b_cmp_v']).astype(F32)
    cmask = cpos[None, :] <= qpos[:, None]
    s = jnp.einsum('bqgrd,bngd->bgrqn', qg, ck) * scale
    p_cmp = jax.nn.softmax(jnp.where(cmask, s, NEG), axis=-1) * cmask
    o_cmp = jnp.einsum('bgrqn,bngd->bqgrd', p_cmp, cv)

    n_slc = -(-L // SLC_LEN)
    n_sel = min(SLC_TOPN, n_slc)
    imp = jnp.einsum('bgrqn,ns->bgqs', p_cmp, _overlap(n_cmp, n_slc))
    blk = np.arange(n_slc)[None, :]
    cur = (qpos // SLC_LEN)[:, None]
    visible = blk <= cur
    forced = (blk == 0) | (blk == cur) | (blk == cur - 1)
    score = jnp.where(forced, 1e9, jnp.where(visible, imp, -1e9))
    top_s, idx = lax.top_k(score, n_sel)
    valid = top_s > -1e8

    pad_l = n_slc * SLC_LEN - L

    def blocks(a):
        a = jnp.pad(a.astype(F32), ((0, 0), (0, pad_l), (0, 0), (0, 0)))
        return a.reshape(B, n_slc, SLC_LEN, NSA_KV, HEAD_DIM).transpose(0, 3, 1, 2, 4)

    ksb, vsb = blocks(ks), blocks(vs)
    qb_len = min(SLC_QBLOCK, Tq)
    nqb = -(-Tq // qb_len)
    pq = nqb * qb_len - Tq
    q_blk = jnp.pad(qg, ((0, 0), (0, pq), (0, 0), (0, 0), (0, 0))).reshape(
        B, nqb, qb_len, NSA_KV, NSA_REP, HEAD_DIM).transpose(1, 0, 2, 3, 4, 5)

    def per_qblock(a, fill):
        a = jnp.pad(a, ((0, 0), (0, 0), (0, pq), (0, 0)), constant_values=fill)
        return a.reshape(B, NSA_KV, nqb, qb_len, n_sel).transpose(2, 0, 1, 3, 4)

    idx_blk = per_qblock(idx, 0)
    val_blk = per_qblock(valid, False)
    pos_blk = jnp.asarray(np.pad(qpos, (0, pq), mode='edge').reshape(nqb, qb_len), jnp.int32)
    gather = jax.vmap(jax.vmap(lambda tab, ix: tab[ix]))

    def sel_attend(args):
        qx, ix, vl, ps = args
        kg = gather(ksb, ix)
        vg = gather(vsb, ix)
        kpos = ix[..., None] * SLC_LEN + jnp.arange(SLC_LEN)
        mask = vl[..., None] & (kpos <= ps[None, None, :, None, None])
        sc = jnp.einsum('bqgrd,bgqnsd->bgrqns', qx, kg) * scale
        sc = jnp.where(mask[:, :, None], sc, NEG)
        shp = sc.shape
        pr = jax.nn.softmax(sc.reshape(shp[:4] + (-1,)), axis=-1).reshape(shp)
        return jnp.einsum('bgrqns,bgqnsd->bqgrd', pr, vg)

    o_slc = lax.map(sel_attend, (q_blk, idx_blk, val_blk, pos_blk))
    o_slc = o_slc.transpose(1, 0, 2, 3, 4, 5).reshape(B, nqb * qb_len, NSA_KV, NSA_REP, HEAD_DIM)[:, :Tq]

    wq_len = min(WIN_QBLOCK, Tq)
    nwb = -(-Tq // wq_len)
    pw = nwb * wq_len - Tq
    span = WINDOW + wq_len
    widx = (q_off - w_off) + np.arange(nwb)[:, None] * wq_len + np.arange(span)[None, :]
    kpos = widx - WINDOW + w_off
    qposw = (q_off + np.arange(nwb * wq_len)).reshape(nwb, wq_len)
    wmask = ((kpos[:, None, :] <= qposw[:, :, None]) & (kpos[:, None, :] >= qposw[:, :, None] - WINDOW)
             & (kpos[:, None, :] >= w_off))

    def band(a):
        return jnp.pad(a.astype(F32), ((0, 0), (WINDOW, pw), (0, 0), (0, 0)))[:, widx]

    kwb, vwb = band(kw), band(vw)
    q_w = jnp.pad(qg, ((0, 0), (0, pw), (0, 0), (0, 0), (0, 0))).reshape(
        B, nwb, wq_len, NSA_KV, NSA_REP, HEAD_DIM)
    s = jnp.einsum('bnqgrd,bnkgd->bngrqk', q_w, kwb) * scale
    p = jax.nn.softmax(jnp.where(wmask[None, :, None, None], s, NEG), axis=-1)
    o_win = jnp.einsum('bngrqk,bnkgd->bnqgrd', p, vwb).reshape(
        B, nwb * wq_len, NSA_KV, NSA_REP, HEAD_DIM)[:, :Tq]

    g = jax.nn.sigmoid(gate.astype(F32)).reshape(B, Tq, NSA_KV, NSA_REP, 3)
    o = g[..., 0:1] * o_cmp + g[..., 1:2] * o_slc + g[..., 2:3] * o_win
    return o.reshape(B, Tq, NSA_HEADS * HEAD_DIM)

def _gated_delta(q, k, v, g, beta, S0):
    B, T, H, DK = q.shape
    DV = v.shape[-1]
    C = min(DN_CHUNK, T)
    n = -(-T // C)
    pad = n * C - T

    def chunks(a):
        a = jnp.pad(a.astype(F32), [(0, 0), (0, pad)] + [(0, 0)] * (a.ndim - 2))
        a = a.reshape((B, n, C) + a.shape[2:])
        return a.transpose((1, 0, 3, 2) + tuple(range(4, a.ndim)))

    qc = chunks(q) * DK ** -0.5
    kc, vc, gc, bc = chunks(k), chunks(v), chunks(g), chunks(beta)
    G = jnp.cumsum(gc, axis=-1)
    tril = np.tril(np.ones((C, C), bool))
    strict = np.tril(np.ones((C, C), bool), -1)
    diff = G[..., :, None] - G[..., None, :]
    decay = jnp.where(tril, jnp.exp(jnp.where(tril, diff, 0.0)), 0.0)
    kb = kc * bc[..., None]
    M = jnp.where(strict, jnp.einsum('nbhid,nbhjd->nbhij', kb, kc) * decay, 0.0)
    rhs = jnp.concatenate([vc * bc[..., None], kb * jnp.exp(G)[..., None]], axis=-1)
    sol = lax.linalg.triangular_solve(M + jnp.eye(C, dtype=F32), rhs, left_side=True, lower=True,
                                      unit_diagonal=True)
    u, w = sol[..., :DV], sol[..., DV:]
    a_qk = jnp.where(tril, jnp.einsum('nbhid,nbhjd->nbhij', qc, kc) * decay, 0.0)

    def step(S, inp):
        q_i, k_i, u_i, w_i, a_i, G_i = inp
        v_new = u_i - jnp.einsum('bhck,bhkv->bhcv', w_i, S)
        o_i = (jnp.einsum('bhck,bhkv->bhcv', q_i * jnp.exp(G_i)[..., None], S)
               + jnp.einsum('bhij,bhjv->bhiv', a_i, v_new))
        G_last = G_i[..., -1]
        S = (S * jnp.exp(G_last)[..., None, None]
             + jnp.einsum('bhck,bhcv->bhkv', k_i * jnp.exp(G_last[..., None] - G_i)[..., None], v_new))
        return S, o_i

    S, o = lax.scan(step, S0.astype(F32), (qc, kc, u, w, a_qk, G))
    o = o.transpose(1, 0, 3, 2, 4).reshape(B, n * C, H, DV)[:, :T]
    return o, S

def _deltanet(qkv, a, b, z, conv_hist, S0, P):
    B, T, _ = qkv.shape
    xx = jnp.concatenate([conv_hist.astype(F32), qkv.astype(F32)], axis=1)
    y = xx[:, 0:T] * P['dn_conv_w'][0]
    for j in range(1, DN_CONV):
        y = y + xx[:, j:j + T] * P['dn_conv_w'][j]
    y = jax.nn.silu(y)
    q, k, v = _split_cols(y, (DN_HEADS * DN_DK, DN_HEADS * DN_DK, DN_HEADS * DN_DV))
    q = _l2norm(q.reshape(B, T, DN_HEADS, DN_DK))
    k = _l2norm(k.reshape(B, T, DN_HEADS, DN_DK))
    v = v.reshape(B, T, DN_HEADS, DN_DV)
    beta = jax.nn.sigmoid(b.astype(F32))
    g = -jnp.exp(P['dn_A_log']) * jax.nn.softplus(a.astype(F32) + P['dn_dt_bias'])
    o, S = _gated_delta(q, k, v, g, beta, S0)
    o = _rmsnorm(o, P['dn_norm_w']) * jax.nn.silu(z.astype(F32).reshape(B, T, DN_HEADS, DN_DV))
    return o.reshape(B, T, DN_HEADS * DN_DV), xx[:, -(DN_CONV - 1):], S

def _peer(h, P):
    B, T, D = h.shape
    N = B * T
    TB = min(PEER_TBLOCK, N)
    nb = -(-N // TB)
    hb = jnp.pad(h.reshape(N, D), ((0, nb * TB - N), (0, 0))).reshape(nb, TB, D)
    half = PEER_DKEY // 2

    def block(xb):
        qh = jnp.einsum('td,hdk->thk', xb, P['w_peer_q'])
        s1 = jnp.einsum('thk,hnk->thn', qh[..., :half], P['w_peer_keys'][:, 0])
        s2 = jnp.einsum('thk,hnk->thn', qh[..., half:], P['w_peer_keys'][:, 1])
        v1, i1 = lax.top_k(s1, PEER_TOPK)
        v2, i2 = lax.top_k(s2, PEER_TOPK)
        cand = (v1[..., :, None] + v2[..., None, :]).reshape(TB, PEER_HEADS, PEER_TOPK * PEER_TOPK)
        cidx = (i1[..., :, None] * PEER_NKEYS + i2[..., None, :]).reshape(TB, PEER_HEADS, PEER_TOPK * PEER_TOPK)
        best, sel = lax.top_k(cand, PEER_TOPK)
        eidx = jnp.take_along_axis(cidx, sel, axis=-1)
        wts = jax.nn.softmax(best.astype(F32), axis=-1)
        act = jax.nn.gelu(jnp.einsum('thkd,td->thk', P['w_peer_u'][eidx], xb))
        return jnp.einsum('thk,thkd->td', wts * act, P['w_peer_v'][eidx])

    return lax.map(block, hb).reshape(nb * TB, D)[:N].reshape(B, T, D)

def _layer(x, c, past, P):
    B, T, _ = x.shape
    q_off = 0 if past is None else past[0].shape[1]
    pos = q_off + np.arange(T)
    ada = jnp.einsum('bd,de->be', c, P['w_ada']) + P['b_ada']
    sh1, sc1, gt1, sh2, sc2, gt2 = jnp.split(ada[:, None, :].astype(F32), 6, axis=-1)

    h = _rmsnorm(x, P['norm1_w']) * (1.0 + sc1) + sh1
    proj = jnp.einsum('btd,de->bte', h, P['w_in'])
    q, kv, nsa_gate, dn_qkv, dn_a, dn_b, dn_z, merge = _split_cols(proj, IN_SPLITS)
    kc, vc, ksl, vsl, kw, vw = [a.reshape(B, T, NSA_KV, HEAD_DIM) for a in jnp.split(kv, 6, axis=-1)]
    q = _rope(_rmsnorm(q.reshape(B, T, NSA_HEADS, HEAD_DIM), P['q_norm_w']), pos)
    kc = _rmsnorm(kc, P['k_norm_w'][0])
    ksl = _rope(_rmsnorm(ksl, P['k_norm_w'][1]), pos)
    kw = _rope(_rmsnorm(kw, P['k_norm_w'][2]), pos)
    if past is None:
        kc_all, vc_all, ks_all, vs_all, kw_all, vw_all = kc, vc, ksl, vsl, kw, vw
        win_keep = min(WINDOW, T)
        w_off = 0
        conv_hist = jnp.zeros((B, DN_CONV - 1, DN_QKV), F32)
        S0 = jnp.zeros((B, DN_HEADS, DN_DK, DN_DV), F32)
    else:
        pkc, pvc, pks, pvs, bwk, bwv, conv_hist, S0 = past

        def cat(a, b):
            return jnp.concatenate([a.astype(F32), b.astype(F32)], axis=1)

        kc_all, vc_all, ks_all, vs_all = cat(pkc, kc), cat(pvc, vc), cat(pks, ksl), cat(pvs, vsl)
        kw_all, vw_all = cat(bwk, kw), cat(bwv, vw)
        win_keep = bwk.shape[1]
        w_off = q_off - win_keep
    o_nsa = _nsa(q, kc_all, vc_all, ks_all, vs_all, kw_all, vw_all, nsa_gate, q_off, w_off, P)
    o_dn, conv_new, S_new = _deltanet(dn_qkv, dn_a, dn_b, dn_z, conv_hist, S0, P)
    g_nsa, g_dn = jnp.split(jax.nn.sigmoid(merge.astype(F32)), 2, axis=-1)
    mixed = (g_nsa * jnp.einsum('bte,ed->btd', o_nsa, P['w_br_a'])
             + g_dn * jnp.einsum('bte,ed->btd', o_dn, P['w_br_b']))
    x = x + gt1 * jnp.einsum('btd,de->bte', mixed, P['w_out'])

    h2 = _rmsnorm(x, P['norm2_w']) * (1.0 + sc2) + sh2
    x = x + gt2 * _peer(h2, P)
    return (x, kc, vc, ksl, vsl, kw_all[:, -win_keep:], vw_all[:, -win_keep:], conv_new, S_new)

def setup_inputs(seed: int = 0) -> dict:
    key = jax.random.key(seed)
    keys = iter(jax.random.split(key, 64))

    def nrm(shape, scale=1.0):
        return jax.random.normal(next(keys), shape, F32) * scale

    def gain(shape):
        return 1.0 + nrm(shape, 0.02)

    n_pages = PAST_LEN // PAGE_SIZE
    n_used = DEC_BATCH * n_pages
    n_pool = n_used + -(-n_used // 4)
    page_table = jax.random.permutation(next(keys), n_pool)[:n_used].reshape(DEC_BATCH, n_pages).astype(jnp.int32)
    win_buf = min(WINDOW, PAST_LEN)
    pool = (DEPTH, n_pool, PAGE_SIZE, NSA_KV, HEAD_DIM)
    dt = jnp.exp(jax.random.uniform(next(keys), (DEPTH, DN_HEADS), F32, math.log(1e-3), math.log(1e-1)))
    a_log = jnp.log(jax.random.uniform(next(keys), (DEPTH, DN_HEADS), F32, 1.0, 16.0))
    return {
        'x_prompt': nrm((BATCH, SEQ, D_MODEL)),
        'x_sample': nrm((DEC_BATCH, DEC_SEQ, D_MODEL)),
        'cache_cmp_k': nrm(pool),
        'cache_cmp_v': nrm(pool),
        'cache_slc_k': nrm(pool),
        'cache_slc_v': nrm(pool),
        'state_win_k': nrm((DEPTH, DEC_BATCH, win_buf, NSA_KV, HEAD_DIM)),
        'state_win_v': nrm((DEPTH, DEC_BATCH, win_buf, NSA_KV, HEAD_DIM)),
        'state_conv': nrm((DEPTH, DEC_BATCH, DN_CONV - 1, DN_QKV)),
        'state_delta': nrm((DEPTH, DEC_BATCH, DN_HEADS, DN_DK, DN_DV), 0.05),
        'page_table': page_table,
        'c_prompt': nrm((BATCH, D_MODEL)),
        'c_sample': nrm((DEC_BATCH, D_MODEL)),
        'w_ada': nrm((DEPTH, D_MODEL, 6 * D_MODEL), 0.5 * D_MODEL ** -0.5),
        'b_ada': nrm((DEPTH, 6 * D_MODEL), 0.02),
        'norm1_w': gain((DEPTH, D_MODEL)),
        'norm2_w': gain((DEPTH, D_MODEL)),
        'w_in': nrm((DEPTH, D_MODEL, IN_WIDTH), D_MODEL ** -0.5),
        'q_norm_w': gain((DEPTH, HEAD_DIM)),
        'k_norm_w': gain((DEPTH, 3, HEAD_DIM)),
        'w_cmp_k': 1.0 / CMP_LEN + nrm((DEPTH, CMP_LEN, HEAD_DIM), CMP_LEN ** -0.5),
        'b_cmp_k': nrm((DEPTH, HEAD_DIM), 0.02),
        'w_cmp_v': 1.0 / CMP_LEN + nrm((DEPTH, CMP_LEN, HEAD_DIM), CMP_LEN ** -0.5),
        'b_cmp_v': nrm((DEPTH, HEAD_DIM), 0.02),
        'dn_conv_w': nrm((DEPTH, DN_CONV, DN_QKV), DN_CONV ** -0.5),
        'dn_A_log': a_log,
        'dn_dt_bias': dt + jnp.log(-jnp.expm1(-dt)),
        'dn_norm_w': gain((DEPTH, DN_DV)),
        'w_br_a': nrm((DEPTH, NSA_HEADS * HEAD_DIM, D_MODEL), (NSA_HEADS * HEAD_DIM) ** -0.5),
        'w_br_b': nrm((DEPTH, DN_HEADS * DN_DV, D_MODEL), (DN_HEADS * DN_DV) ** -0.5),
        'w_out': nrm((DEPTH, D_MODEL, D_MODEL), D_MODEL ** -0.5),
        'w_peer_q': nrm((DEPTH, PEER_HEADS, D_MODEL, PEER_DKEY), D_MODEL ** -0.5),
        'w_peer_keys': nrm((DEPTH, PEER_HEADS, 2, PEER_NKEYS, PEER_DKEY // 2), (PEER_DKEY // 2) ** -0.5),
        'w_peer_u': nrm((DEPTH, PEER_EXPERTS, D_MODEL), D_MODEL ** -0.5),
        'w_peer_v': nrm((DEPTH, PEER_EXPERTS, D_MODEL), PEER_HEADS ** -0.5),
    }

def reference(x_prompt, x_sample, cache_cmp_k, cache_cmp_v, cache_slc_k, cache_slc_v,
              state_win_k, state_win_v, state_conv, state_delta, page_table, c_prompt, c_sample,
              w_ada, b_ada, norm1_w, norm2_w, w_in, q_norm_w, k_norm_w, w_cmp_k, b_cmp_k, w_cmp_v, b_cmp_v,
              dn_conv_w, dn_A_log, dn_dt_bias, dn_norm_w, w_br_a, w_br_b, w_out,
              w_peer_q, w_peer_keys, w_peer_u, w_peer_v):
    n_pages = page_table.shape[1]

    def paged(cache):
        rows = cache[page_table]
        return rows.reshape((rows.shape[0], n_pages * rows.shape[2]) + rows.shape[3:])

    yp, ys = x_prompt, x_sample
    p_hist, s_hist = [], []
    for l in range(DEPTH):
        P = {'w_ada': w_ada[l], 'b_ada': b_ada[l], 'norm1_w': norm1_w[l], 'norm2_w': norm2_w[l],
             'w_in': w_in[l], 'q_norm_w': q_norm_w[l], 'k_norm_w': k_norm_w[l],
             'w_cmp_k': w_cmp_k[l], 'b_cmp_k': b_cmp_k[l], 'w_cmp_v': w_cmp_v[l], 'b_cmp_v': b_cmp_v[l],
             'dn_conv_w': dn_conv_w[l], 'dn_A_log': dn_A_log[l], 'dn_dt_bias': dn_dt_bias[l],
             'dn_norm_w': dn_norm_w[l], 'w_br_a': w_br_a[l], 'w_br_b': w_br_b[l], 'w_out': w_out[l],
             'w_peer_q': w_peer_q[l], 'w_peer_keys': w_peer_keys[l], 'w_peer_u': w_peer_u[l],
             'w_peer_v': w_peer_v[l]}
        past = (paged(cache_cmp_k[l]), paged(cache_cmp_v[l]), paged(cache_slc_k[l]), paged(cache_slc_v[l]),
                state_win_k[l], state_win_v[l], state_conv[l], state_delta[l])
        yp, *p_new = _layer(yp, c_prompt, None, P)
        ys, *s_new = _layer(ys, c_sample, past, P)
        p_hist.append(p_new)
        s_hist.append(s_new)
    p_cmp_k, p_cmp_v, p_slc_k, p_slc_v, p_win_k, p_win_v, p_conv, p_delta = [jnp.stack(a) for a in zip(*p_hist)]
    s_cmp_k, s_cmp_v, s_slc_k, s_slc_v, s_win_k, s_win_v, s_conv, s_delta = [jnp.stack(a) for a in zip(*s_hist)]
    return (yp, ys, p_cmp_k, p_cmp_v, p_slc_k, p_slc_v, p_win_k, p_win_v, p_conv, p_delta,
            s_cmp_k, s_cmp_v, s_slc_k, s_slc_v, s_win_k, s_win_v, s_conv, s_delta)


_drawn_inputs = setup_inputs


def setup_inputs(seed=0):
    import zlib

    import numpy as np

    out = dict(_drawn_inputs(seed))
    spreads = {}
    factors = {'cache_slc_k': 3.971,
     'cache_slc_v': 4.96,
     'norm2_w': 3.912,
     'q_norm_w': 8.0,
     'k_norm_w': 2.728,
     'b_cmp_k': 8.0,
     'b_cmp_v': 7.584,
     'dn_norm_w': 5.332}
    for name, (base, spread) in spreads.items():
        noise = np.random.default_rng([zlib.crc32(name.encode()), seed]).standard_normal(out[name].shape)
        drawn = base * np.exp(spread * noise) if base else spread * noise
        out[name] = jnp.asarray(drawn.astype(out[name].dtype))
    for name, factor in factors.items():
        out[name] = (out[name] * factor).astype(out[name].dtype)
    return out
```

```python
from contextlib import ExitStack

import concourse.bass as bass
from concourse import mybir

F32 = mybir.dt.float32
I32 = mybir.dt.int32
U32 = mybir.dt.uint32
ALU = mybir.AluOpType
ACT = mybir.ActivationFunctionType
AX = mybir.AxisListType

P = 128
D = 2048
KT = D // P
SEQ = 256
NS = 8
NT = SEQ + NS
NR = 9
H = 8
G = 2
REP = H // G
EPS = 1e-6
SCALE = float(P) ** -0.5
NEG = -1e30
PAST = 1024
PAGES = PAST // P
POOL = 80
WIN = 512
N_CMP = (PAST - 32) // 16 + 1
N_CMP_P = (SEQ - 32) // 16 + 1
NC0 = N_CMP + 2
SLOTS = 4
SLOT = KT * 256
N_ADA0 = 2 * D // 256
T_Q, T_KC, T_VC, T_KS, T_VS, T_KW, T_VW = 0, 8, 10, 12, 14, 16, 18
T_DNQ, T_DNK, T_DNV, T_Z, T_END = 20, 28, 36, 44, 52
N_ADA1 = 34
N_GROUP = 64
TOKEN_TILES = [(0, 128), (128, 128), (256, 8)]
ROUTE_BLOCKS = [(0, 136), (136, 128)]
LOWEST = -3.4e38
N_MERGE_ADA = 14
PAGED = (3, 3, 3, 11)
MERGE_B = [24, 26, 28, 30, 32, 34, 44, 46]
DNT = T_Z - T_DNQ
N_WORK = 6400
NU = 2 * H
N_MERGE = 32
SM_A, SM_B, SM_G, SM = 0, 32, 64, 96

CONSTS, N_CONST = {}, 0
for _name, _n in (("ident", P), ("perm", P), ("sumsel", NR), ("cos", NT), ("sin", NT), ("cosc", N_CMP), ("sinc", N_CMP),
                  ("gsum", P), ("causal", 2 * SEQ), ("cmpbias", 32), ("cmp01", 32), ("upper", P), ("lower", P),
                  ("levels", 3 * P), ("iota", P), ("ident16", 256), ("blockid", 14)):
    CONSTS[_name] = (N_CONST, N_CONST + _n)
    N_CONST += _n
PARAMS, N_PARAM = {}, 0
for _name, _n in (("bada", 96), ("nw", 2 * KT), ("hw", 4), ("wck", 32), ("wcv", 32), ("bck", 1), ("bcv", 1),
                  ("convw", DNT * 4), ("dnw", 1), ("alog", 1), ("dt", 1)):
    PARAMS[_name] = (N_PARAM, N_PARAM + _n)
    N_PARAM += _n


class Chain:

    def __init__(self, eng, sem, base=0):
        self.eng, self.sem, self.n = eng, sem, base

    def __call__(self, ins):
        self.n = self.n + 1
        ins.then_inc(self.sem, 1)
        self.eng.wait_ge(self.sem, self.n)


def build_program(nc, I, O):
    with ExitStack() as ctx:
        def sb(name, shape, dt=F32):
            return ctx.enter_context(nc.sbuf_tensor(name, shape, dt))

        def sem(name):
            return ctx.enter_context(nc.semaphore(name))

        psum = ctx.enter_context(nc.psum_tensor("psum", [P, 8, 512], F32))
        bank = [psum[:, i, :] for i in range(8)]

        ring = sb("ring", [P, SLOTS, SLOT])
        xT = sb("xT", [P, KT, NT])
        hT = sb("hT", [P, KT, NT])
        arena = sb("arena", [P, T_END * NT + N_WORK])
        PR = arena[:, 0:T_END * NT].rearrange("p (t n) -> p t n", n=NT)
        work = arena[:, T_END * NT:]
        adaT = sb("adaT", [P, 6 * KT, NR])
        cstat = sb("cstat", [P, KT, 32])
        consts = sb("consts", [P, N_CONST])
        params = sb("params", [P, N_PARAM])
        hist = sb("hist", [P, DNT, 4, NS])
        CK = sb("CK", [P, 2, NS, G, NC0])
        ones = sb("ones", [P, P])
        adaS = sb("adaS", [P, 2, 256])
        A1 = sb("A1", [P, KT, NR])
        rstd = sb("rstd", [P, NT])
        rowsG = sb("rowsG", [H, NT])
        rowsB = sb("rowsB", [H, NT])
        gates = sb("gates", [3 * H, NT])
        epst = sb("epst", [P, 1])
        ptab = sb("ptab", [1, NS * PAGES], I32)

        gate_scratch = nc.dram_tensor("gate_scratch", (3 * H, NS), F32, kind="Internal").ap()

        def cst(name):
            return consts[:, CONSTS[name][0]:CONSTS[name][1]]

        def par(name):
            return params[:, PARAMS[name][0]:PARAMS[name][1]]

        ident = cst("ident")
        xflat = xT[:].rearrange("p k n -> p (k n)")

        wsmall = work[:, 0:KT * SM].rearrange("p (k n) -> p k n", k=KT)
        sq = [work[:, 1056 * i:1056 * (i + 1)].rearrange("p (t n) -> p t n", t=4) for i in range(2)]
        rs = [work[:, 2112 + 1056 * i:2112 + 1056 * (i + 1)].rearrange("p (t n) -> p t n", t=4) for i in range(2)]
        rtmp = work[:, 4224:5280].rearrange("p (t n) -> p t n", t=4)
        convt = work[:, 5280:6336].rearrange("p (t n) -> p t n", t=4)
        ctmp = xflat[:, 0:G * N_CMP * 32].rearrange("p (g n j) -> p g n j", g=G, j=32)
        ctmpp = xflat[:, 0:G * N_CMP_P * 32].rearrange("p (g n j) -> p g n j", g=G, j=32)
        croll = xflat[:, 0:NS * G * N_CMP].rearrange("p (m n) -> p m n", m=NS * G)
        SB = [work[:, 544 * i:544 * (i + 1)] for i in range(2)]
        PTs = [work[:, 1088 + 640 * i:1088 + 640 * (i + 1)] for i in range(2)]
        V0 = work[0:NC0, 2368:4416].rearrange("p (m d) -> p m d", m=NS * G)
        qpad = work[:, 4416:4928].rearrange("p (m r) -> p m r", m=NS * G)
        VT = work[:, 4928:5952].rearrange("p (a d) -> p a d", a=8)
        CVT = work[0:N_CMP_P, 5952:6208].rearrange("p (g d) -> p g d", g=G)
        SS = xflat[:, 0:1601]
        PTS = xflat[:, 1664:1664 + 13 * P].rearrange("p (a d) -> p a d", a=13)
        convs = rtmp[:, 0:1, 0:DNT * NS].rearrange("p a (t b) -> p (a t) b", b=NS)
        convs2 = rtmp[:, 1:2, 0:DNT * NS].rearrange("p a (t b) -> p (a t) b", b=NS)
        praw = sb("praw", [P, DNT, 3])
        CP = sb("CP", [P, 2, G, N_CMP_P])
        GT = sb("GT", [P, 2, 3 * H])
        gateS = sb("gateS", [P, 4, 3])
        sm1 = sb("sm1", [P, 2, 3, 3])
        smS = sb("smS", [P, 3, 3])
        impb = sb("impb", [P, 5, 16])
        osb = sb("osb", [P, P])

        Mb, Ab = (xflat[:, 2048 * i:2048 * (i + 1)].rearrange("p (u n) -> p u n", u=NU) for i in range(2))
        Tb, Ub = (work[:, 2048 * i:2048 * (i + 1)].rearrange("p (u n) -> p u n", u=NU) for i in range(2))
        Cb, Yb = (work[:, 4096 + 1024 * i:5120 + 1024 * i].rearrange("p (u n) -> p u n", u=H) for i in range(2))
        ckflat = CK[:].rearrange("p v b g n -> p (v b g n)")
        VN, S1 = (ckflat[:, 1024 * i:1024 * (i + 1)].rearrange("p (u n) -> p u n", u=H) for i in range(2))
        Dm, Tm = (work[:, 2048 + 256 * i:2304 + 256 * i].rearrange("p (i j) -> p i j", i=16) for i in range(2))
        dtmp = work[:, 2560:2800]
        dred = work[:, 2816:2832]
        rows2 = sb("rows2", [H, 2, NT])
        alog = sb("alog", [H, 1])
        smp_g = sb("smp_g", [P, P])
        cols = sb("cols", [P, 2, H, 2])
        glast = sb("glast", [P, H, 2])
        kdec = sb("kdec", [P, H, 2])
        bge = sb("bge", [P, H])
        egl = sb("egl", [P, H])
        smp = {n: work[:, 4096 + 64 * i:4160 + 64 * i] for i, n in enumerate(("k0", "k1", "s0", "s1", "eg", "bb", "prod", "qk", "vn", "kc"))}
        kq = work[:, 4096:4224].rearrange("p (m c) -> p m c", c=2)
        sks = work[:, 4224:4352].rearrange("p (m c) -> p m c", c=2)
        ktok, vtok = work[0:64, 4736:4864], work[0:64, 4864:4992]
        vdiag = work[0:64, 5120:6144].rearrange("p (m n) -> p m n", m=8)
        keys = arena[:, 4224:6272].rearrange("p (t n) -> p t n", t=16)
        SC = arena[:, 6272:10368].rearrange("p (a n) -> p a n", a=2)
        SCr = arena[:, 10368:12416]
        kval = arena[:, 12416:12672].rearrange("p (t k) -> p t k", t=16)
        kidxf = arena[:, 12672:12928].rearrange("p (t k) -> p t k", t=16)
        chosen = arena[:, 12928:13312].rearrange("p (v n) -> p v n", v=3)
        cposf = arena[:, 13312:13568].rearrange("p (v h k) -> p v h k", v=2, h=H)
        btop = arena[:, 13568:13576].unsqueeze(2)
        bsum = arena[:, 13576:13584]
        kidx = sb("kidx", [P, 16, 16], U32)
        cpos = sb("cpos", [P, 3, H, 16], U32)
        IT = ckflat[:, 0:3 * NT].rearrange("p (v n) -> p v n", v=3)
        WS = arena[:, 0:ROUTE_BLOCKS[0][1] * P]
        O1, O2 = (arena[:, 17408 + 1024 * i:18432 + 1024 * i].rearrange("p (b t n) -> p b t n", b=2, t=4) for i in range(2))
        acc = arena[:, 0:KT * NT].rearrange("p (t n) -> p t n", n=NT)
        act_x, Wb = (arena[:, 4224 + 1056 * i:5280 + 1056 * i].rearrange("p (b j n) -> p b j n", b=2, j=2) for i in range(2))
        route_w = nc.dram_tensor("route_w", (P, 2 * N_GROUP, NT), F32, kind="Internal").ap()
        x1sq = PR[:, 16:32, :]
        x1tmp = work[:, 0:32].rearrange("p (a t b) -> p a t b", a=2, t=2)
        m_scratch = nc.dram_tensor("m_scratch", (NU, 8, 16, 16), F32, kind="Internal").ap()
        t_scratch = nc.dram_tensor("t_scratch", (NU, 8, 16, 16), F32, kind="Internal").ap()

        slot_full = [sem(f"slot_full{i}") for i in range(SLOTS)]
        slot_used = [sem(f"slot_used{i}") for i in range(SLOTS)]
        cache_full = [sem(f"cache_full{i}") for i in range(SLOTS)]
        names = """consts_in consts_set ada_copied ada_reduced ada_done x_squared x_summed x_std dve_step act_step
            loop_step h_ready wsmall_in small_mm small_evac proj_mm proj_evac out_stored gates_out gates_in
            hn_sq hn_sum hn_std hn_done rope_rot rope_done conv_done conv_silu raw_saved hist_new cmp_ready
            cmp_rot cmp_done vt_mm vt_evac v0_mm qpad_done u_scores u_max u_exp u_norm u_turned u_evac u_mm
            u_out r_scores r_cmpmax r_cmpexp r_imp r_impsum r_max r_exp r_norm r_turned r_evac r_oevac r_oturned
            r_out kv_stored g_parts g_soft g_rows g_cols g_colsc g_bcast kk_mm d_diff d_exp d_half m_out m_in
            t_ready t_out t_zero t_in t_mm t_evac lv_c lv_y lv_ye lv_z lv_u lv_t lv_te vk_tok bv_ready kd_ready
            kdec_diff kdec_exp vn_mm vn_evac o_mm o_evac s1_mm s1_evac zs_mm rhs_ready qe_mm qe_exp qe_ready
            s2_mm s2_ready s2_stored z_silu smp_rows smp_kq smp_mm smp_evac smp_prod smp_vn smp_diag smp_outer
            smp_new smp_stored dn_out x_again br_done x1_done keys_in pq_evac key_mm scores_in best_sub best_exp
            chosen chosen_turned chosen_evac onehot route_mm route_free route_evac route_stored
            route_in0 route_in1 expert_gelu expert_act acc_mm acc_added y_ready""".split()
        S = {n: sem(n) for n in names}

        def slot_kt(s):
            return ring[:, s, :].rearrange("p (k n) -> p k n", k=KT)

        slc_slot = [ring[:, s, :].rearrange("p (a v n) -> p a v n", a=PAGES, v=2) for s in range(SLOTS)]

        block = ctx.enter_context(nc.Block())

        @block.sync
        def _(sp):
            for dst, name in ((cstat, "c"), (xT, "x"), (consts, "consts"), (params, "params"), (ptab, "pages")):
                sp.dma_start(dst[:], I[name]).then_inc(S["consts_in"], 16)
            sp.dma_start(hist[:, :, 0:3, :], I["conv_hist"]).then_inc(S["consts_in"], 16)
            sp.dma_start(wsmall, I["w_small"]).then_inc(S["wsmall_in"], 16)

            def load(s, use, src):
                sp.wait_ge(slot_used[s], use + 1)
                sp.dma_start(ring[:, s, :], src).then_inc(slot_full[s], 16)

            def tile_of(name, n):
                return I[name][bass.ds(n, 1)].rearrange("a p n -> p (a n)")

            def load_pages(s, use, seq, name, dst):
                sp.wait_ge(slot_used[s], use + 1)
                for p in range(PAGES):
                    page = sp.value_load(ptab[0:1, bass.ds(seq * PAGES + p, 1)], min_val=0, max_val=POOL - 1)
                    sp.dma_start(dst(p), I[name][bass.ds(page, 1)].rearrange("a p (v n) -> p (a v) n", v=4)
                                 if name == "cache_cmp" else I[name][bass.ds(page, 1)].rearrange("a p n -> p (a n)")
                                 ).then_inc(cache_full[s], 16)

            sp.wait_ge(S["consts_in"], 16 * 6)
            with sp.Fori(0, N_ADA0 // 4) as i:
                for s in range(4):
                    load(s, i, tile_of("w_ada", 4 * i + s))
            cmp_dst = ring[:, 3, :].rearrange("p (v r) -> p v r", v=4)
            with sp.Fori(0, 8) as i:
                load(0, i + 4, tile_of("w_in", 2 * i))
                load(1, i + 4, tile_of("w_ada", i + 16))
                load(2, i + 4, tile_of("w_in", 2 * i + 1))
                load_pages(3, i + 4, i, "cache_cmp", lambda p: cmp_dst[:, :, p * P:(p + 1) * P])
            with sp.Fori(0, 5) as i:
                load(0, i + 12, tile_of("w_in", 2 * i + 16))
                load(1, i + 12, tile_of("w_ada", 2 * i + 24))
                load(2, i + 12, tile_of("w_in", 2 * i + 17))
                load(3, i + 12, tile_of("w_ada", 2 * i + 25))
            sp.wait_ge(S["raw_saved"], 1)
            sp.wait_ge(S["hist_new"], 1)
            sp.dma_start(O["s_conv"], hist[:, :, 1:4, :]).then_inc(S["kv_stored"], 16)
            sp.dma_start(O["p_conv"], praw[:]).then_inc(S["kv_stored"], 16)
            sp.dma_start(O["s_win_k"], I["win_k_rows"]).then_inc(S["kv_stored"], 16)
            sp.dma_start(O["s_win_v"], I["win_v_rows"]).then_inc(S["kv_stored"], 16)
            sp.wait_ge(S["small_evac"], 3)
            sp.dma_start(gate_scratch, gates[:, SEQ:NT]).then_inc(S["gates_out"], 16)
            sp.wait_ge(S["gates_out"], 16)
            sp.wait_ge(S["consts_set"], 3)
            for j in range(4):
                for a in range(3):
                    src = gate_scratch.rearrange("(g r a) (q s) -> g s r q a", g=G, a=3, s=2)
                    sp.dma_start(gateS[32 * j:32 * j + REP, :, a], src[j % G, j // G, :, :, a],
                                 allow_slow_non_contiguous=True).then_inc(S["gates_in"], 16)
            for q in range(4):
                for m in range(2):
                    s, use = (3 * q + m) % 4, 17 + (3 * q + m) // 4
                    load_pages(s, use, 2 * q + m, "cache_slc", lambda p: ring[:, s, 512 * p:512 * (p + 1)])
                s, use = (3 * q + 2) % 4, 17 + (3 * q + 2) // 4
                sp.wait_ge(slot_used[s], use + 1)
                sp.dma_start(ring[:, s, :].rearrange("p (b n) -> p b n", b=2),
                             I["win"][2 * q:2 * q + 2].rearrange("b p n -> p b n")).then_inc(cache_full[s], 16)
            sp.wait_ge(S["rope_done"], 4)
            sp.dma_start(O["kv"], PR[:, T_KC:T_DNQ, :]).then_inc(S["kv_stored"], 16)
            for m in range(2):
                load(m, 20, I["s_delta0"][m])
            sp.wait_ge(S["d_half"], 2)
            for b in range(8):
                r = slice(16 * b, 16 * b + 16)
                sp.dma_start(m_scratch.rearrange("u b i j -> b i u j")[b], Mb[r, :, r]).then_inc(S["m_out"], 16)
            sp.wait_ge(S["m_out"], 16 * 8)
            sp.dma_start(Dm.rearrange("p i j -> p (i j)"), m_scratch.rearrange("u b i j -> (u b) (i j)")).then_inc(S["m_in"], 16)
            sp.wait_ge(S["t_ready"], 1)
            sp.dma_start(t_scratch.rearrange("u b i j -> (u b) (i j)"), Tm.rearrange("p i j -> p (i j)")).then_inc(S["t_out"], 16)
            sp.wait_ge(S["t_out"], 16)
            sp.wait_ge(S["t_zero"], 1)
            for b in range(8):
                r = slice(16 * b, 16 * b + 16)
                sp.dma_start(Tb[r, :, r], t_scratch.rearrange("u b i j -> b i u j")[b]).then_inc(S["t_in"], 16)
            sp.wait_ge(S["s2_ready"], 1)
            sp.dma_start(O["p_delta"], Yb).then_inc(S["s2_stored"], 16)
            for m in range(2):
                sp.wait_ge(S["smp_new"], m + 1)
                sp.dma_start(O["s_delta"][m], ring[:, m, :]).then_inc(S["smp_stored"], 16)
            sp.wait_ge(S["s2_stored"], 16)
            sp.wait_ge(S["smp_stored"], 32)
            for m in range(2):
                sp.sem_inc(slot_used[m], 1)
            sp.wait_ge(S["kv_stored"], 16 * 5)
            with sp.Fori(0, N_MERGE_ADA // 2) as i:
                load(2, i + 20, tile_of("w_in", 2 * i + T_END // 2))
                load(3, i + 20, tile_of("w_ada", 2 * i + N_ADA1))
                load(0, i + 21, tile_of("w_in", 2 * i + T_END // 2 + 1))
                load(1, i + 21, tile_of("w_ada", 2 * i + N_ADA1 + 1))
            for s in (2, 3):
                load(s, 27, I["w_in"][T_END // 2 + 14 + s - 2])
            sp.wait_ge(S["dn_out"], 1)
            sp.dma_start(xT[:], I["x"]).then_inc(S["x_again"], 16)
            for name, use in (("w_br", 28), ("w_out", 30), ("w_peer_q", 32)):
                with sp.Fori(0, 2) as i:
                    for s in range(SLOTS):
                        load(s, i + use, tile_of(name, 4 * i + s))
            sp.wait_ge(S["x_summed"], 2)
            sp.dma_start(keys, I["w_keys"]).then_inc(S["keys_in"], 16)
            for n in range(2):
                load(2 * n, 34, I["w_peer_u"][n])
                load(2 * n + 1, 34, I["w_peer_v"][n])
            for b, (t0, n) in enumerate(ROUTE_BLOCKS):
                sp.wait_ge(S["route_evac"], (t0 + n) // 4)
                sp.dma_start(route_w[:, :, t0:t0 + n], WS[:, 0:n * P].rearrange("p (i t) -> p i t", t=n)).then_inc(S["route_stored"], 16)
            sp.wait_ge(S["route_stored"], 16 * len(ROUTE_BLOCKS))

            def load_weights(g, b):
                sp.dma_start(Wb[:, b], route_w[:, bass.ds(2 * g, 2), :]).then_inc(S[f"route_in{b}"], 16)

            for b in range(2):
                load_weights(b, b)
            with sp.Fori(0, N_GROUP // 2 - 1) as i:
                for b in range(2):
                    load(2 * b, i + 35, tile_of("w_peer_u", 2 * i + b + 2))
                    load(2 * b + 1, i + 35, tile_of("w_peer_v", 2 * i + b + 2))
                    sp.wait_ge(S["expert_act"], 2 * i + b + 1)
                    load_weights(2 * i + b + 2, b)
            sp.wait_ge(S["y_ready"], 1)
            sp.dma_start(O["y"], acc).then_inc(S["out_stored"], 16)
            sp.wait_ge(S["out_stored"], 16)

        @block.gpsimd
        def _(pool):
            pool.memset(gateS[:], 0.0).then_inc(S["consts_set"], 1)

        @block.tensor
        def _(pe):
            def ada_main(s, use, paged=0):
                pe.wait_ge(slot_full[s], 16 * (use + 1 - paged))
                w = slot_kt(s)
                for k in range(KT):
                    g = 32 * (k % 4)
                    mm = pe.matmul(bank[4 + s % 2][g:g + 32, 0:256], cstat[:, k, :], w[:, k, :],
                                   start=(k < 4), stop=(k >= KT - 4), tile_position=(0, g))
                mm.then_inc(slot_used[s], 1)

            def ada_reduce(s, m):
                pe.wait_ge(S["ada_copied"], m + 1)
                pe.wait_ge(S["ada_done"], m + 1)
                for j in range(2):
                    mm = pe.matmul(bank[6][:, NR * j:NR * j + NR], adaS[:, s % 2, j * P:(j + 1) * P], cst("sumsel"),
                                   start=True, stop=True)
                mm.then_inc(S["ada_reduced"], 1)

            def project(s, use, t, b, paged=0):
                pe.wait_ge(slot_full[s], 16 * (use + 1 - paged))
                w = slot_kt(s)
                for j in range(2):
                    pe.wait_ge(S["proj_evac"], t + j + 1)
                    for k in range(KT):
                        mm = pe.matmul(bank[b + j][:, 0:NT], w[:, k, j * P:(j + 1) * P], hT[:, k, :],
                                       start=(k == 0), stop=(k == KT - 1))
                    mm.then_inc(slot_used[s] if j else S["proj_mm"], 1)

            pe.wait_ge(S["consts_in"], 16 * 6)
            pe.wait_ge(S["consts_set"], 3)
            with pe.Fori(0, N_ADA0 // 4) as i:
                for s in range(4):
                    ada_main(s, i)
                    ada_reduce(s, 4 * i + s)
            for k in range(KT):
                pe.wait_ge(S["x_squared"], k // 4 + 1)
                mm = pe.matmul(bank[7][:, 0:NT], ones[:], hT[:, k, :], start=(k == 0), stop=(k == KT - 1))
            mm.then_inc(S["x_summed"], 1)
            pe.wait_ge(S["h_ready"], 1)
            pe.wait_ge(S["wsmall_in"], 16)
            for k in range(KT):
                mm = pe.matmul(bank[7][0:SM, 0:NT], wsmall[:, k, :], hT[:, k, :], start=(k == 0), stop=(k == KT - 1))
            mm.then_inc(S["small_mm"], 1)
            with pe.Fori(0, 8) as i:
                project(0, i + 4, 4 * i, 0)
                ada_main(1, i + 4)
                project(2, i + 4, 4 * i + 2, 2)
                ada_reduce(1, i + 16)
            with pe.Fori(0, 5) as i:
                project(0, i + 12, 4 * i + 32, 0)
                ada_main(1, i + 12)
                project(2, i + 12, 4 * i + 34, 2)
                ada_reduce(1, 2 * i + 24)
                ada_main(3, i + 12, 8)
                ada_reduce(3, 2 * i + 25)

            def head_sum(n, count):
                pe.wait_ge(S["hn_sq"], n + 1)
                if n >= 2:
                    pe.wait_ge(S["hn_std"], n - 1)
                for t in range(count):
                    mm = pe.matmul(bank[n % 2 * 4 + t][:, 0:NT], ones[:], sq[n % 2][:, t, :], start=True, stop=True)
                mm.then_inc(S["hn_sum"], 1)

            pe.wait_ge(S["ada_done"], 35)
            for n, (t0, count, _) in enumerate(NORM_GROUPS):
                head_sum(n, count)
            pe.wait_ge(S["hn_std"], len(NORM_GROUPS))
            for n, (t0, count) in enumerate(ROPE_GROUPS):
                pe.wait_ge(S["hn_done"], len(NORM_GROUPS))
                if n >= 2:
                    pe.wait_ge(S["rope_done"], n - 1)
                for t in range(count):
                    mm = pe.matmul(bank[n % 2 * 4 + t][:, 0:NT], cst("perm"), PR[:, t0 + t, :], start=True, stop=True)
                mm.then_inc(S["rope_rot"], 1)
            pe.wait_ge(S["rope_done"], 4)
            pe.wait_ge(S["cmp_ready"], 1)
            ck = CK[:, 0, :, :, 1:1 + N_CMP].rearrange("p b g n -> p (b g) n")
            for m in range(2):
                pe.matmul(bank[m][:, 0:8 * N_CMP], cst("perm"), ck[:, 8 * m:8 * m + 8, :], start=True, stop=True)
            pe.matmul(bank[2][:, 0:G * N_CMP_P], cst("perm"), CP[:, 0, :, :].rearrange("p g n -> p (g n)"),
                      start=True, stop=True).then_inc(S["cmp_rot"], 1)
            for m, t in enumerate((T_VS, T_VS + 1, T_VW, T_VW + 1)):
                for a in range(2):
                    j = 2 * m + a
                    pe.transpose(bank[4 + j // 4][:, j % 4 * P:(j % 4 + 1) * P], PR[:, t, a * P:(a + 1) * P], ident)
            for g in range(G):
                pe.transpose(bank[6][0:N_CMP_P, g * P:(g + 1) * P], CP[:, 1, g, :], ident)
            pe.wait_ge(S["small_evac"], 3)
            for a in range(2):
                mm = pe.transpose(bank[7][:, 32 * a:32 * a + 3 * H], gates[:, a * P:(a + 1) * P], ident[0:3 * H, 0:3 * H])
            mm.then_inc(S["vt_mm"], 1)
            pe.wait_ge(S["cmp_done"], 1)
            for m in range(NS * G):
                mm = pe.transpose(bank[m // 4][0:NC0, m % 4 * P:(m % 4 + 1) * P], CK[:, 1, m // G, m % G, :], ident)
            mm.then_inc(S["v0_mm"], 1)

            def unit_scores(u):
                h, a = u // 2, u % 2
                nk, q, b = P * (a + 1), PR[:, h, a * P:(a + 1) * P], u % 2 * 2
                if u == 0:
                    pe.wait_ge(S["vt_evac"], 2)
                else:
                    if u >= 2:
                        pe.wait_ge(S["u_max"], u - 1)
                pe.matmul(bank[b][:, 0:nk], q, PR[:, T_KS + h // REP, 0:nk], start=True, stop=True)
                pe.matmul(bank[b][:, 256:256 + N_CMP_P], q, CP[:, 0, h // REP, :], start=True, stop=True)
                pe.matmul(bank[b + 1][:, 0:nk], q, PR[:, T_KW + h // REP, 0:nk], start=True,
                          stop=True).then_inc(S["u_scores"], 1)

            unit_scores(0)
            for u in range(2 * H):
                if u + 1 < 2 * H:
                    unit_scores(u + 1)
                h, a = u // 2, u % 2
                pe.wait_ge(S["u_norm"], u + 1)
                if u:
                    pe.wait_ge(S["u_evac"], u)
                for m in range(2):
                    for k in range(a + 1):
                        pe.transpose(bank[4][:, (2 * m + k) * P:(2 * m + k + 1) * P],
                                     SB[u % 2][:, 256 * m + k * P:256 * m + (k + 1) * P], ident)
                pe.transpose(bank[5][0:N_CMP_P, 0:P], SB[u % 2][:, 512:512 + N_CMP_P], ident).then_inc(S["u_turned"], 1)
                pe.wait_ge(S["u_evac"], u + 1)
                if u >= 2:
                    pe.wait_ge(S["u_out"], u - 1)
                o = bank[6 + u % 2][:, 0:P]
                pe.matmul(o, CVT[:, h // REP, :], PTs[u % 2][0:N_CMP_P, 512:640], start=True, stop=False)
                for m in range(2):
                    for k in range(a + 1):
                        mm = pe.matmul(o, VT[:, (2 * m + h // REP) * 2 + k, :],
                                       PTs[u % 2][:, (2 * m + k) * P:(2 * m + k + 1) * P],
                                       start=False, stop=(m == 1 and k == a))
                mm.then_inc(S["u_mm"], 1)

            pe.wait_ge(S["qpad_done"], 1)
            for q in range(4):
                items = [3 * q, 3 * q + 1, 3 * q + 2]
                slots = [n % 4 for n in items]
                if q == 0:
                    pe.wait_ge(S["u_out"], 2 * H)
                else:
                    pe.wait_ge(S["r_out"], q)
                for n in items:
                    before = [m for m in range(n + 1) if m % 4 == n % 4]
                    done = 16 * sum(1 if m % 3 == 2 else PAGES for m in before)
                    pe.wait_ge(cache_full[n % 4], done + (16 * PAGES * 8 if n % 4 == 3 else 0))
                wslot = ring[:, slots[2], :].rearrange("p (b n) -> p b n", b=2)
                for j in range(4):
                    b, g, r = j // G, j % G, slice(32 * j, 32 * j + 32)
                    pair, kw = 4 * q + j, dict(start=True, stop=True, tile_position=(0, 32 * j))
                    qs = qpad[:, pair, :]
                    pe.matmul(bank[0][r, 0:NC0], qs, CK[:, 0, 2 * q + b, g, :], **kw)
                    for m in range(2):
                        pe.matmul(bank[1 + m][r, :], qs, slc_slot[slots[b]][:, 4 * m:4 * m + 4, 0, g * P:(g + 1) * P], **kw)
                    mm = pe.matmul(bank[3][r, :], qs, wslot[:, b, g * WIN:(g + 1) * WIN], **kw)
                mm.then_inc(S["r_scores"], 1)
                pe.wait_ge(S["r_imp"], q + 1)
                pe.matmul(bank[4][:, 0:14], cst("gsum"), impb[:, 0, 0:14], start=True, stop=True).then_inc(S["r_impsum"], 1)
                pe.wait_ge(S["r_norm"], q + 1)
                for a in range(13):
                    lo = (a * P if a < 4 else 512 if a == 4 else NC0 + 512 + (a - 5) * P)
                    n = NC0 if a == 4 else P
                    mm = pe.transpose(bank[4 + a // 4][0:n, a % 4 * P:(a % 4 + 1) * P], SS[:, lo:lo + n], ident)
                mm.then_inc(S["r_turned"], 1)
                pe.wait_ge(S["r_evac"], q + 1)
                for j in range(4):
                    b, g, r = j // G, j % G, slice(32 * j, 32 * j + 32)
                    for a in range(13):
                        n = NC0 if a == 4 else P
                        if a < 4:
                            v = wslot[:, b, G * WIN + a * 256 + g * P:G * WIN + a * 256 + (g + 1) * P]
                        elif a == 4:
                            v = V0[:, 4 * q + j, :]
                        else:
                            v = slc_slot[slots[b]][:, a - 5, 1, g * P:(g + 1) * P]
                        mm = pe.matmul(bank[0][r, 0:P], PTS[0:n, a, 32 * j:32 * j + 32], v, start=(a == 0),
                                       stop=(a == 12), tile_position=(0, 32 * j))
                    if j == 1:
                        mm.then_inc(slot_used[slots[0]], 1)
                    if j == 3:
                        mm.then_inc(slot_used[slots[1]], 1)
                pe.wait_ge(slot_used[slots[1]], 18 + items[1] // 4 + 1)
                pe.nop().then_inc(slot_used[slots[2]], 1)
                pe.wait_ge(S["r_oevac"], q + 1)
                pe.transpose(bank[1][:, 0:P], osb[:], ident).then_inc(S["r_oturned"], 1)

            for n in range(5, 9):
                if n == 5:
                    pe.wait_ge(S["r_out"], 4)
                head_sum(n, 4)
            pe.wait_ge(S["hn_std"], 9)
            pe.wait_ge(S["g_rows"], 1)
            for v, rows in enumerate((rowsG, rowsB)):
                for c in range(2):
                    pe.transpose(bank[0][:, 16 * v + 8 * c:16 * v + 8 * c + 8], rows[:, c * P:(c + 1) * P], ident[0:H, 0:H])
                for h in range(H):
                    mm = pe.matmul(bank[1][:, 64 * v + NS * h:64 * v + NS * (h + 1)], ident[0:H, h:h + 1].broadcast_to((H, P)),
                                   rows[:, SEQ:NT], start=True, stop=True)
            mm.then_inc(S["g_cols"], 1)
            pe.wait_ge(S["g_colsc"], 2)
            pe.wait_ge(S["hn_done"], 9)
            for hb in range(2):
                if hb:
                    pe.wait_ge(S["d_half"], 1)
                for a in range(4):
                    mm = pe.matmul(bank[4 + a][:, 0:SEQ], ident[0:H, 4 * hb + a:4 * hb + a + 1].broadcast_to((H, P)),
                                   rowsG[:, 0:SEQ], start=True, stop=True)
                mm.then_inc(S["g_bcast"], 1)
                for v, tile in ((0, T_DNK), (2, T_DNQ)):
                    for a in range(8):
                        h, r = 4 * hb + a // 2, slice(a % 2 * P, (a % 2 + 1) * P)
                        mm = pe.matmul(bank[v + a // 4][:, a % 4 * P:(a % 4 + 1) * P], PR[:, T_DNK + h, r], PR[:, tile + h, r],
                                       start=True, stop=True)
                mm.then_inc(S["kk_mm"], 1)
            pe.wait_ge(S["t_in"], 16 * 8)
            pe.wait_ge(S["d_half"], 2)
            for u in range(NU):
                mm = pe.transpose(bank[u // 4][:, u % 4 * P:(u % 4 + 1) * P], Tb[:, u, :], ident)
            mm.then_inc(S["t_mm"], 1)
            pe.wait_ge(S["t_evac"], 1)
            for n in range(6):
                level, half = n // 2, n % 2
                pe.wait_ge(S["lv_c"], n + 1)
                if n:
                    pe.wait_ge(S["lv_ye"], n)
                for a in range(8):
                    mm = pe.matmul(bank[a // 4][:, a % 4 * P:(a % 4 + 1) * P], Cb[:, a, :], Ub[:, 8 * half + a, :],
                                   start=True, stop=True)
                mm.then_inc(S["lv_y"], 1)
                pe.wait_ge(S["lv_ye"], n + 1)
                if n >= 2:
                    pe.wait_ge(S["lv_te"], n - 1)
                for a in range(8):
                    mm = pe.matmul(bank[2 + a // 4][:, a % 4 * P:(a % 4 + 1) * P], Tb[:, 8 * half + a, :], Yb[:, a, :],
                                   start=True, stop=True)
                mm.then_inc(S["lv_z"], 1)
                pe.wait_ge(S["lv_u"], n + 1)
                if level < 2:
                    for a in range(8):
                        mm = pe.transpose(bank[4 + a // 4][:, a % 4 * P:(a % 4 + 1) * P], Ub[:, 8 * half + a, :], ident)
                    mm.then_inc(S["lv_t"], 1)
            for v, (tile, ready, free) in enumerate(((T_DNV, "vk_tok", 4), (T_DNK, "vk_tok", 4))):
                if v:
                    pe.wait_ge(S["bv_ready"], 1)
                else:
                    pe.wait_ge(S["lv_te"], 4)
                for u in range(NU):
                    mm = pe.transpose(bank[u // 4][:, u % 4 * P:(u % 4 + 1) * P], PR[:, tile + u // 2, u % 2 * P:(u % 2 + 1) * P], ident)
                mm.then_inc(S[ready], 1)
            pe.wait_ge(S["kd_ready"], 1)
            quarter = lambda base, h: bank[base + h // 4][:, h % 4 * P:(h % 4 + 1) * P]
            for h in range(H):
                mm = pe.matmul(quarter(0, h), Ub[:, 2 * h, :], Tb[:, 2 * h, :], start=True, stop=True)
            mm.then_inc(S["vn_mm"], 1)
            pe.wait_ge(S["vn_evac"], 1)
            for h in range(H):
                mm = pe.matmul(quarter(4, h), Mb[:, 2 * h, :], VN[:, h, :], start=True, stop=True)
            mm.then_inc(S["s1_mm"], 1)
            for h in range(H):
                mm = pe.matmul(quarter(2, h), VN[:, h, :], Ab[:, 2 * h, :], start=True, stop=True)
            mm.then_inc(S["o_mm"], 1)
            pe.wait_ge(S["s1_evac"], 1)
            for h in range(H):
                mm = pe.matmul(quarter(6, h), PR[:, T_DNK + h, P:SEQ], S1[:, h, :], start=True, stop=True)
            mm.then_inc(S["zs_mm"], 1)
            for h in range(H):
                mm = pe.matmul(quarter(4, h), ident[0:H, h:h + 1].broadcast_to((H, P)), rowsG[:, P:SEQ], start=True, stop=True)
            mm.then_inc(S["qe_mm"], 1)
            pe.wait_ge(S["rhs_ready"], 1)
            for h in range(H):
                mm = pe.matmul(quarter(0, h), Ub[:, 2 * h + 1, :], Yb[:, h, :], start=True, stop=True)
            mm.then_inc(S["vn_mm"], 1)
            pe.wait_ge(S["vn_evac"], 2)
            pe.wait_ge(S["qe_ready"], 1)
            pe.wait_ge(S["o_evac"], 1)
            for h in range(H):
                pe.matmul(quarter(2, h), S1[:, h, :], Cb[:, h, :], start=True, stop=False)
                mm = pe.matmul(quarter(2, h), VN[:, h, :], Ab[:, 2 * h + 1, :], start=False, stop=True)
            mm.then_inc(S["o_mm"], 1)
            for h in range(H):
                mm = pe.matmul(quarter(6, h), Mb[:, 2 * h + 1, :], VN[:, h, :], start=True, stop=True)
            mm.then_inc(S["s2_mm"], 1)
            pe.wait_ge(S["smp_kq"], 1)
            for m in range(64):
                if m % 32 == 0:
                    pe.wait_ge(slot_full[m // 32], 16 * 18)
                mm = pe.matmul(bank[0][:, 2 * m:2 * m + 2], ring[:, m // 32, m % 32 * P:(m % 32 + 1) * P], kq[:, m, :],
                               start=True, stop=True)
            mm.then_inc(S["smp_mm"], 1)
            pe.wait_ge(S["smp_prod"], 1)
            pe.matmul(bank[1][:, 0:64], ones[:], smp["prod"], start=True, stop=True).then_inc(S["smp_mm"], 1)
            pe.wait_ge(S["smp_vn"], 1)
            pe.wait_ge(S["o_evac"], 2)
            pe.transpose(bank[2][0:64, 0:P], smp["kc"], ident)
            pe.transpose(bank[2][0:64, P:2 * P], smp["vn"], ident).then_inc(S["smp_mm"], 1)
            pe.wait_ge(S["s2_ready"], 1)
            for n in range(8):
                pe.wait_ge(S["smp_diag"], n + 1)
                b = 4 + n % 2 * 2
                for m in range(2):
                    mm = pe.matmul(bank[b + m], ktok, vdiag[:, 4 * m:4 * m + 4, :].rearrange("p m n -> p (m n)"), start=True, stop=True)
                mm.then_inc(S["smp_outer"], 1)
            for n in (9, 10):
                if n == 9:
                    pe.wait_ge(S["smp_new"], 2)
                head_sum(n, 4)

            pe.wait_ge(S["hn_std"], 11)
            with pe.Fori(0, N_MERGE_ADA // 2) as i:
                project(2, i + 20, 4 * i + T_END, 0, PAGED[2])
                ada_main(3, i + 20, PAGED[3])
                project(0, i + 21, 4 * i + T_END + 2, 2, PAGED[0])
                ada_reduce(3, 2 * i + N_ADA1)
                ada_main(1, i + 21, PAGED[1])
                ada_reduce(1, 2 * i + N_ADA1 + 1)
            project(2, 27, T_END + 28, 0, PAGED[2])
            project(3, 27, T_END + 30, 2, PAGED[3])
            pe.wait_ge(S["proj_evac"], T_END + N_MERGE + 4)
            pe.wait_ge(S["ada_done"], 49)
            pe.wait_ge(S["dn_out"], 1)
            for n in range(8):
                s, b = n % 4, n % 2 * 4
                pe.wait_ge(slot_full[s], 16 * (29 + n // 4 - PAGED[s]))
                if n >= 2:
                    pe.wait_ge(S["br_done"], n - 1)
                for j in range(2):
                    for k in range(H):
                        pe.matmul(bank[b + j][:, 0:NT], slot_kt(s)[:, k, j * P:(j + 1) * P], PR[:, k, :], start=(k == 0), stop=(k == H - 1))
                    for k in range(H):
                        mm = pe.matmul(bank[b + 2 + j][:, 0:NT], slot_kt(s)[:, H + k, j * P:(j + 1) * P], PR[:, T_DNV + k, :],
                                       start=(k == 0), stop=(k == H - 1))
                mm.then_inc(slot_used[s], 1)
            pe.wait_ge(S["br_done"], 8)

            def dense(n, use, free, src):
                s = n % 4
                pe.wait_ge(slot_full[s], 16 * (use + n // 4 + 1 - PAGED[s]))
                if n >= 4 and free:
                    pe.wait_ge(S[free], n - 3)
                for j in range(2):
                    for k in range(KT):
                        mm = pe.matmul(bank[2 * s + j][:, 0:NT], slot_kt(s)[:, k, j * P:(j + 1) * P], src[:, k, :],
                                       start=(k == 0), stop=(k == KT - 1))
                mm.then_inc(slot_used[s], 1)

            for n in range(8):
                dense(n, 30, "x1_done", hT)
            pe.wait_ge(S["x1_done"], 8)
            for k in range(KT):
                pe.wait_ge(S["x_squared"], 4 + k // 4 + 1)
                mm = pe.matmul(bank[7][:, 0:NT], ones[:], x1sq[:, k, :], start=(k == 0), stop=(k == KT - 1))
            mm.then_inc(S["x_summed"], 1)

            pe.wait_ge(S["h_ready"], 2)
            for n in range(8):
                dense(n, 32, "pq_evac", hT)

            def scores(a):
                t0, n = TOKEN_TILES[a]
                for t in range(16):
                    mm = pe.matmul(bank[a % 2 * 4 + t // 4][0:n, t % 4 * P:(t % 4 + 1) * P], PR[:, t, t0:t0 + n], keys[:, t, :],
                                   start=True, stop=True)
                mm.then_inc(S["key_mm"], 1)

            def turn(a):
                n = TOKEN_TILES[a][1]
                pe.wait_ge(S["chosen"], a + 1)
                for v in range(3):
                    mm = pe.transpose(bank[a % 2 * 4][:, v * P:v * P + n], chosen[0:n, v, :], ident[0:n, 0:n])
                mm.then_inc(S["chosen_turned"], 1)

            pe.wait_ge(S["pq_evac"], 8)
            pe.wait_ge(S["keys_in"], 16)
            scores(0)
            scores(1)
            turn(0)
            pe.wait_ge(S["chosen_evac"], 1)
            scores(2)
            turn(1)
            turn(2)
            pe.wait_ge(S["chosen_evac"], 3)
            with pe.Fori(0, NT // 8) as i:
                for b in range(2):
                    q = 2 * i + b
                    pe.wait_ge(S["onehot"], q + 1)
                    pe.wait_ge(S["route_free"], q + 1)
                    for t in range(4):
                        mm = pe.matmul(bank[b][:, t * P:(t + 1) * P], O2[:, b, t, :], O1[:, b, t, :], start=True, stop=True)
                    mm.then_inc(S["route_mm"], 1)

            def expert_scores(b, use, free):
                pe.wait_ge(slot_full[2 * b], 16 * (use + 1 - PAGED[2 * b]))
                pe.wait_ge(S["expert_gelu"], free)
                for j in range(2):
                    for k in range(KT):
                        mm = pe.matmul(bank[2 * b + j][:, 0:NT], slot_kt(2 * b)[:, k, j * P:(j + 1) * P], hT[:, k, :],
                                       start=(k == 0), stop=(k == KT - 1))
                mm.then_inc(slot_used[2 * b], 1)

            def expert_values(b, use, g):
                s = 2 * b + 1
                pe.wait_ge(slot_full[s], 16 * (use + 1 - PAGED[s]))
                pe.wait_ge(S["expert_act"], g + 1)
                for d in range(KT):
                    if d % 2 == 0:
                        pe.wait_ge(S["acc_added"], 8 * g + d // 2 + 1)
                    for j in range(2):
                        mm = pe.matmul(bank[4 + d % 4][:, 0:NT], ring[:, s, j * D + d * P:j * D + (d + 1) * P], act_x[:, b, j, :],
                                       start=(j == 0), stop=(j == 1))
                    if d % 2 == 1:
                        mm.then_inc(slot_used[s] if d == KT - 1 else S["acc_mm"], 1)

            pe.wait_ge(S["route_free"], NT // 4 + 2)
            expert_scores(0, 34, 1)
            with pe.Fori(0, N_GROUP // 2 - 1) as i:
                expert_scores(1, i + 34, 2 * i + 2)
                expert_values(0, i + 34, 2 * i)
                expert_scores(0, i + 35, 2 * i + 3)
                expert_values(1, i + 34, 2 * i + 1)
            expert_scores(1, 33 + N_GROUP // 2, N_GROUP)
            expert_values(0, 33 + N_GROUP // 2, N_GROUP - 2)
            expert_values(1, 33 + N_GROUP // 2, N_GROUP - 1)

        @block.scalar
        def _(act):
            act.sem_inc(S["proj_evac"], 4)
            act.sem_inc(S["conv_silu"], 4)
            for s in range(SLOTS):
                act.sem_inc(slot_used[s], 1)
            act.wait_ge(S["consts_in"], 16 * 6)
            for k in range(0, KT, 4):
                act.activation(hT[:, k:k + 4, :], xT[:, k:k + 4, :], ACT.Square).then_inc(S["x_squared"], 1)

            def ada_copy(s, use):
                act.wait_ge(slot_used[s], use + 2)
                act.activation(adaS[:, s % 2, :], bank[4 + s % 2][:, 0:256], ACT.Copy).then_inc(S["ada_copied"], 1)

            def evacuate(s, use, t, n, b, func=ACT.Copy):
                act.wait_ge(S["proj_mm"], n + 1)
                act.activation(PR[:, bass.ds(t, 1), :], bank[b][:, 0:NT], func).then_inc(S["proj_evac"], 1)
                act.wait_ge(slot_used[s], use + 2)
                act.activation(PR[:, bass.ds(t + 1, 1), :], bank[b + 1][:, 0:NT], func).then_inc(S["proj_evac"], 1)

            with act.Fori(0, N_ADA0 // 4) as i:
                for s in range(4):
                    ada_copy(s, i)
            act.wait_ge(S["x_summed"], 1)
            act.wait_ge(S["consts_set"], 3)
            act.activation(rstd[:], bank[7][:, 0:NT], ACT.Sqrt, bias=epst[:], scale=1.0 / D).then_inc(S["x_std"], 1)
            act.wait_ge(S["small_mm"], 1)
            act.activation(rowsG[:], bank[7][SM_A:SM_A + H, 0:NT], ACT.Copy).then_inc(S["small_evac"], 1)
            act.activation(rowsB[:], bank[7][SM_B:SM_B + H, 0:NT], ACT.Sigmoid).then_inc(S["small_evac"], 1)
            act.activation(gates[:], bank[7][SM_G:SM_G + 3 * H, 0:NT], ACT.Sigmoid).then_inc(S["small_evac"], 1)
            with act.Fori(0, 8) as i:
                evacuate(0, i + 4, 4 * i, 2 * i, 0)
                ada_copy(1, i + 4)
                evacuate(2, i + 4, 4 * i + 2, 2 * i + 1, 2)
            with act.Fori(0, 5) as i:
                evacuate(0, i + 12, 4 * i + 32, 2 * i + 16, 0)
                ada_copy(1, i + 12)
                evacuate(2, i + 12, 4 * i + 34, 2 * i + 17, 2)
                ada_copy(3, i + 12)

            def head_square(n, t0, count):
                if n >= 2:
                    act.wait_ge(S["hn_sum"], n - 1)
                act.activation(sq[n % 2][:, 0:count, :], PR[:, t0:t0 + count, :], ACT.Square).then_inc(S["hn_sq"], 1)

            def head_std(n, count, scale):
                act.wait_ge(S["hn_sum"], n + 1)
                if n >= 2:
                    act.wait_ge(S["hn_done"], n - 1)
                act.activation(rs[n % 2][:, 0:count, :], psum[:, n % 2 * 4:n % 2 * 4 + count, 0:NT], ACT.Sqrt,
                               bias=epst[:], scale=scale).then_inc(S["hn_std"], 1)

            act.wait_ge(S["proj_evac"], T_END + 4)
            act.wait_ge(S["small_mm"], 1)
            for n, (t0, count, _) in enumerate(NORM_GROUPS):
                head_square(n, t0, count)
                if n:
                    head_std(n - 1, NORM_GROUPS[n - 1][1], 1.0 / P)
            head_std(len(NORM_GROUPS) - 1, NORM_GROUPS[-1][1], 1.0 / P)
            act.activation(hist[:, :, 3, :], PR[:, T_DNQ:T_Z, SEQ:NT], ACT.Copy).then_inc(S["hist_new"], 1)
            act.activation(praw[:], PR[:, T_DNQ:T_Z, SEQ - 3:SEQ], ACT.Copy).then_inc(S["raw_saved"], 1)
            act.wait_ge(S["hist_new"], 1)
            act.wait_ge(S["raw_saved"], 1)
            with act.Fori(0, DNT // 4) as i:
                for b in range(4):
                    act.wait_ge(S["conv_done"], 4 * i + b + 1)
                    act.activation(PR[:, bass.ds(T_DNQ + 4 * i + b, 1), 0:SEQ], convt[:, b:b + 1, 0:SEQ],
                                   ACT.Silu).then_inc(S["conv_silu"], 1)
            act.wait_ge(S["conv_done"], DNT + 1)
            act.activation(PR[:, T_DNQ:T_Z, SEQ:NT], convs, ACT.Silu).then_inc(S["conv_silu"], 1)
            act.wait_ge(S["conv_silu"], DNT + 5)
            act.wait_ge(S["vt_mm"], 1)
            act.activation(VT.rearrange("p (a c) d -> p a (c d)", a=2), psum[:, 4:6, :], ACT.Copy)
            act.activation(CVT.rearrange("p g d -> p (g d)"), bank[6][0:N_CMP_P, 0:G * P], ACT.Copy)
            act.activation(GT[:], bank[7][:, 0:64].rearrange("p (a c) -> p a c", a=2)[:, :, 0:3 * H],
                           ACT.Copy).then_inc(S["vt_evac"], 1)
            act.wait_ge(S["v0_mm"], 1)
            act.activation(V0.rearrange("p (a c) d -> p a (c d)", a=4), psum[0:NC0, 0:4, :], ACT.Copy).then_inc(S["vt_evac"], 1)

            def unit_exp(u):
                n = P * (u % 2 + 1)
                act.wait_ge(S["u_max"], u + 1)
                for m, (lo, w) in enumerate(((512, N_CMP_P), (0, n), (256, n))):
                    e = act.activation(SB[u % 2][:, lo:lo + w], SB[u % 2][:, lo:lo + w], ACT.Exp,
                                       bias=sm1[:, u % 2, 0, m:m + 1], scale=SCALE, accum_out=sm1[:, u % 2, 1, m:m + 1])
                e.then_inc(S["u_exp"], 1)

            unit_exp(0)
            for u in range(2 * H):
                if u + 1 < 2 * H:
                    unit_exp(u + 1)
                h, a = u // 2, u % 2
                act.wait_ge(S["u_turned"], u + 1)
                if u >= 2:
                    act.wait_ge(S["u_mm"], u - 1)
                n = P * (a + 1)
                act.activation(PTs[u % 2][:, 0:512].rearrange("p (m n) -> p m n", m=2)[:, :, 0:n],
                               bank[4].rearrange("p (m n) -> p m n", m=2)[:, :, 0:n], ACT.Copy)
                act.activation(PTs[u % 2][0:N_CMP_P, 512:640], bank[5][0:N_CMP_P, 0:P], ACT.Copy).then_inc(S["u_evac"], 1)
                act.wait_ge(S["u_mm"], u + 1)
                act.activation(PR[:, h, a * P:(a + 1) * P], bank[6 + u % 2][:, 0:P], ACT.Copy).then_inc(S["u_out"], 1)

            for q in range(4):
                act.wait_ge(S["r_cmpmax"], q + 1)
                act.activation(SS[:, 513:576], SS[:, 513:576], ACT.Exp, bias=smS[:, 0, 0:1], scale=SCALE,
                               accum_out=smS[:, 1, 0:1]).then_inc(S["r_cmpexp"], 1)
                act.wait_ge(S["r_max"], q + 1)
                for m, (lo, hi) in ((1, (576, 1601)), (2, (0, 513))):
                    e = act.activation(SS[:, lo:hi], SS[:, lo:hi], ACT.Exp, bias=smS[:, 0, m:m + 1], scale=SCALE,
                                       accum_out=smS[:, 1, m:m + 1])
                e.then_inc(S["r_exp"], 1)
                act.wait_ge(S["r_turned"], q + 1)
                act.activation(PTS[:, 0:4, :].rearrange("p a d -> p (a d)"), bank[4], ACT.Copy)
                act.activation(PTS[0:NC0, 4, :], bank[5][0:NC0, 0:P], ACT.Copy)
                act.activation(PTS[:, 5:8, :].rearrange("p a d -> p (a d)"), bank[5][:, P:512], ACT.Copy)
                act.activation(PTS[:, 8:12, :].rearrange("p a d -> p (a d)"), bank[6], ACT.Copy)
                act.activation(PTS[:, 12, :], bank[7][:, 0:P], ACT.Copy).then_inc(S["r_evac"], 1)
                act.wait_ge(slot_used[(3 * q + 1) % 4], 18 + (3 * q + 1) // 4 + 1)
                act.activation(osb[:], bank[0][:, 0:P], ACT.Copy).then_inc(S["r_oevac"], 1)
                act.wait_ge(S["r_oturned"], q + 1)
                for b in range(2):
                    o = bank[1][:, 0:P].rearrange("p (b g r) -> p b g r", b=2, g=G)[:, b, :, 0:REP]
                    e = act.activation(PR[:, 0:H, SEQ + 2 * q + b].rearrange("p (g r) -> p g r", g=G), o, ACT.Copy)
                e.then_inc(S["r_out"], 1)

            act.wait_ge(S["g_parts"], 1)
            act.activation(rows2[:, 1, :], rows2[:, 1, :], ACT.Exp).then_inc(S["act_step"], 1)
            act.activation(alog[:], par("alog")[0:H, :], ACT.Exp)
            act.wait_ge(S["act_step"], 1)
            act.activation(rows2[:, 1, :], rows2[:, 1, :], ACT.Ln, bias=ones[0:H, 0:1]).then_inc(S["g_soft"], 1)
            for n in range(5, 9):
                head_square(n, T_DNQ + 4 * (n - 5), 4)
                if n > 5:
                    head_std(n - 1, 4, 1.0)
            head_std(8, 4, 1.0)
            act.activation(PR[:, T_Z:T_END, :], PR[:, T_Z:T_END, :], ACT.Silu).then_inc(S["z_silu"], 1)
            act.wait_ge(S["g_cols"], 1)
            act.activation(cols[:].rearrange("p v h c -> p v c h"), bank[0][:, 0:32].rearrange("p (v c h) -> p v c h", v=2, c=2),
                           ACT.Copy).then_inc(S["g_colsc"], 1)
            act.activation(smp_g[:], bank[1][:, 0:P], ACT.Copy).then_inc(S["g_colsc"], 1)
            for hb in range(2):
                act.wait_ge(S["d_diff"], hb + 1)
                act.activation(Cb, Cb, ACT.Exp)
                act.activation(Yb, Yb, ACT.Exp, scale=-1.0).then_inc(S["d_exp"], 1)
            act.wait_ge(S["kdec_diff"], 1)
            act.activation(kdec[:], kdec[:], ACT.Exp)
            act.activation(bge[:], cols[:, 0, :, 1], ACT.Exp)
            act.activation(egl[:], glast[:, :, 1], ACT.Exp).then_inc(S["kdec_exp"], 1)
            act.wait_ge(S["t_mm"], 1)
            flat = lambda ap: ap.rearrange("p (a u) n -> p a (u n)", u=4)
            act.activation(flat(Ub), psum[:, 0:4, :], ACT.Copy).then_inc(S["t_evac"], 1)
            for n in range(6):
                act.wait_ge(S["lv_y"], n + 1)
                if n:
                    act.wait_ge(S["lv_z"], n)
                act.activation(flat(Yb), psum[:, 0:2, :], ACT.Copy).then_inc(S["lv_ye"], 1)
                if n < 4:
                    act.wait_ge(S["lv_t"], n + 1)
                    act.activation(flat(Tb[:, n % 2 * 8:n % 2 * 8 + 8, :]), psum[:, 4:6, :], ACT.Copy).then_inc(S["lv_te"], 1)
            act.wait_ge(S["vn_mm"], 1)
            act.activation(flat(VN), psum[:, 0:2, :], ACT.Copy).then_inc(S["vn_evac"], 1)
            act.wait_ge(S["s1_mm"], 1)
            act.activation(flat(S1), psum[:, 4:6, :], ACT.Copy).then_inc(S["s1_evac"], 1)
            act.wait_ge(S["o_mm"], 1)
            act.activation(PR[:, T_DNV:T_Z, 0:P], psum[:, 2:4, :].rearrange("p a (u n) -> p (a u) n", u=4), ACT.Copy).then_inc(S["o_evac"], 1)
            act.wait_ge(S["qe_mm"], 1)
            act.activation(flat(Cb), psum[:, 4:6, :], ACT.Exp).then_inc(S["qe_exp"], 1)
            act.wait_ge(S["vn_mm"], 2)
            act.activation(flat(VN), psum[:, 0:2, :], ACT.Copy).then_inc(S["vn_evac"], 1)
            act.wait_ge(S["o_mm"], 2)
            act.activation(PR[:, T_DNV:T_Z, P:SEQ], psum[:, 2:4, :].rearrange("p a (u n) -> p (a u) n", u=4), ACT.Copy).then_inc(S["o_evac"], 1)
            act.activation(smp["eg"], smp_g[:, 0:64], ACT.Exp).then_inc(S["smp_rows"], 1)
            act.wait_ge(S["smp_mm"], 1)
            act.activation(sks.rearrange("p m c -> p (m c)"), bank[0][:, 0:P], ACT.Copy).then_inc(S["smp_evac"], 1)
            act.wait_ge(S["smp_mm"], 2)
            act.activation(smp["qk"], bank[1][:, 0:64], ACT.Copy).then_inc(S["smp_evac"], 1)
            act.wait_ge(S["smp_mm"], 3)
            act.activation(ktok, bank[2][0:64, 0:P], ACT.Copy)
            act.activation(vtok, bank[2][0:64, P:2 * P], ACT.Copy).then_inc(S["smp_evac"], 1)
            act.wait_ge(S["smp_new"], 2)
            for n in (9, 10):
                head_square(n, T_DNV + 4 * (n - 9), 4)
            for n in (9, 10):
                head_std(n, 4, 1.0 / P)
            act.wait_ge(S["kv_stored"], 16 * 5)
            act.wait_ge(S["dn_out"], 1)
            with act.Fori(0, N_MERGE_ADA // 2) as i:
                evacuate(2, i + 20, 4 * i + H, 2 * i + T_END // 2, 0, ACT.Sigmoid)
                ada_copy(3, i + 20)
                evacuate(0, i + 21, 4 * i + H + 2, 2 * i + T_END // 2 + 1, 2, ACT.Sigmoid)
                ada_copy(1, i + 21)
            evacuate(2, 27, T_Z, T_END // 2 + 14, 0, ACT.Sigmoid)
            evacuate(3, 27, T_Z + 2, T_END // 2 + 15, 2, ACT.Sigmoid)
            for k in range(0, KT, 4):
                act.wait_ge(S["x1_done"], k // 2 + 2)
                act.activation(x1sq[:, k:k + 4, :], xT[:, k:k + 4, :], ACT.Square).then_inc(S["x_squared"], 1)
            act.wait_ge(S["x_summed"], 2)
            act.activation(rstd[:], bank[7][:, 0:NT], ACT.Sqrt, bias=epst[:], scale=1.0 / D).then_inc(S["x_std"], 1)
            act.sem_inc(S["expert_gelu"], 2)
            act.sem_inc(S["route_free"], 2)
            for n in range(8):
                s = n % 4
                act.wait_ge(slot_used[s], 32 + n // 4 + 2)
                act.activation(PR[:, 2 * n:2 * n + 2, :], psum[:, 2 * s:2 * s + 2, 0:NT], ACT.Copy).then_inc(S["pq_evac"], 1)

            def take_scores(a):
                n = TOKEN_TILES[a][1]
                act.wait_ge(S["key_mm"], a + 1)
                if a == 2:
                    act.wait_ge(S["chosen"], 1)
                act.activation(SC[0:n, a % 2].rearrange("p (c n) -> p c n", c=4), psum[0:n, a % 2 * 4:a % 2 * 4 + 4, :],
                               ACT.Copy).then_inc(S["scores_in"], 1)

            def softmax_exp(a):
                n = TOKEN_TILES[a][1]
                act.wait_ge(S["best_sub"], a + 1)
                act.activation(chosen[0:n, 2, :], chosen[0:n, 2, :], ACT.Exp).then_inc(S["best_exp"], 1)

            def take_chosen(a):
                t0, n = TOKEN_TILES[a]
                act.wait_ge(S["chosen_turned"], a + 1)
                act.activation(IT[:, :, t0:t0 + n], bank[a % 2 * 4][:, 0:3 * P].rearrange("p (v n) -> p v n", v=3)[:, :, 0:n],
                               ACT.Copy).then_inc(S["chosen_evac"], 1)

            take_scores(0)
            take_scores(1)
            softmax_exp(0)
            take_chosen(0)
            take_scores(2)
            softmax_exp(1)
            take_chosen(1)
            softmax_exp(2)
            take_chosen(2)
            for b, (t0, n) in enumerate(ROUTE_BLOCKS):
                out = WS[:, 0:n * P].rearrange("p (i t) -> p t i", t=n)
                if b:
                    act.wait_ge(S["route_stored"], 16 * b)
                with act.Fori(0, n // 8) as i:
                    for c in range(2):
                        act.wait_ge(S["route_mm"], 2 * i + c + t0 // 4 + 3)
                        act.activation(out[:, bass.ds(8 * i + 4 * c, 4), :], bank[c].rearrange("p (t i) -> p t i", t=4),
                                       ACT.Copy).then_inc(S["route_free"], 1)
                act.wait_ge(S["route_free"], (t0 + n) // 4 + 2)
                act.sem_inc(S["route_evac"], n // 4)

            def expert_gelu(b, use, g):
                act.wait_ge(slot_used[2 * b], use + 2)
                act.wait_ge(slot_used[2 * b + 1], use + 1)
                act.activation(act_x[:, b], psum[:, 2 * b:2 * b + 2, 0:NT], ACT.Gelu_apprx_tanh).then_inc(S["expert_gelu"], 1)

            act.wait_ge(S["route_stored"], 16 * len(ROUTE_BLOCKS))
            with act.Fori(0, N_GROUP // 2) as i:
                for b in range(2):
                    expert_gelu(b, i + 34, 2 * i + b)

        @block.vector
        def _(dve):
            dve.sem_inc(S["ada_done"], 1)
            dve.memset(ones[:], 1.0).then_inc(S["consts_set"], 1)
            dve.memset(epst[:], EPS).then_inc(S["consts_set"], 1)
            step = Chain(dve, S["dve_step"])
            dve.wait_ge(S["consts_in"], 16 * 6)

            def ada_bias(m, t):
                dve.wait_ge(S["ada_reduced"], m + 1)
                dve.tensor_tensor(adaT[:, bass.ds(t, 2), :], bank[6][:, 0:2 * NR].rearrange("p (j r) -> p j r", j=2),
                                  par("bada")[:, bass.ds(t, 2)].unsqueeze(2).broadcast_to((P, 2, NR)),
                                  ALU.add).then_inc(S["ada_done"], 1)

            with dve.Fori(0, N_ADA0) as m:
                ada_bias(m, 2 * m)

            def modulate(which, src, dst, ready):
                sh, sc = 3 * KT * which, 3 * KT * which + KT
                w = par("nw")[:, KT * which:KT * which + KT].unsqueeze(2).broadcast_to((P, KT, NR))
                step(dve.scalar_tensor_tensor(A1[:], adaT[:, sc:sc + KT, :], 1.0, w, ALU.add, ALU.mult))
                step(dve.tensor_tensor(dst, src, rstd[:].unsqueeze(1).broadcast_to((P, KT, NT)), ALU.mult))
                step(dve.tensor_tensor(dst[:, :, SEQ:NT], dst[:, :, SEQ:NT], A1[:, :, 1:NR], ALU.mult))
                dve.tensor_tensor(dst[:, :, SEQ:NT], dst[:, :, SEQ:NT], adaT[:, sh:sh + KT, 1:NR], ALU.add)
                for k in range(KT):
                    ins = dve.tensor_scalar(dst[:, k, 0:SEQ], dst[:, k, 0:SEQ], A1[:, k, 0:1], adaT[:, sh + k, 0:1],
                                            ALU.mult, ALU.add)
                ins.then_inc(ready, 1)

            dve.wait_ge(S["x_std"], 1)
            dve.wait_ge(S["ada_done"], N_ADA0 + 1)
            step(dve.reciprocal(rstd[:], rstd[:]))
            modulate(0, xT[:], hT[:], S["h_ready"])
            dve.wait_ge(S["h_ready"], 1)

            def windows(src, n):
                return bass.AP(src.tensor, src.offset, [list(src.ap[0]), list(src.ap[1]), [16, n], [1, 32]])

            def compress(src, n, w, tmp, dst, link):
                link(dve.tensor_tensor(tmp, windows(src, n), w.unsqueeze(1).unsqueeze(1).broadcast_to((P, G, n, 32)), ALU.mult))
                return dve.tensor_reduce(dst, tmp, AX.X, ALU.add)

            with dve.Fori(0, 8) as i:
                ada_bias(i + 16, 2 * i + 32)
                dve.wait_ge(cache_full[3], 16 * PAGES * (i + 1))
                link = Chain(dve, S["loop_step"], 3 * i)
                for v, w in enumerate(("wck", "wcv")):
                    src = ring[:, 3, v * 2048:(v + 1) * 2048].rearrange("p (g n) -> p g n", g=G)
                    ins = compress(src, N_CMP, par(w), ctmp, CK[:, v, bass.ds(i, 1), :, 1:1 + N_CMP].rearrange("p b g n -> p (b g) n"), link)
                    if v == 0:
                        link(ins)
                    else:
                        ins.then_inc(slot_used[3], 1)
                        dve.wait_ge(slot_used[3], i + 6)
            with dve.Fori(0, 10) as i:
                ada_bias(i + 24, 2 * i + 48)

            def head_norm(n, t0, count, w):
                dve.wait_ge(S["hn_std"], n + 1)
                r = rs[n % 2][:, 0:count, :]
                step(dve.reciprocal(r, r))
                dve.scalar_tensor_tensor(PR[:, t0:t0 + count, :], PR[:, t0:t0 + count, :], w, r, ALU.mult,
                                         ALU.mult).then_inc(S["hn_done"], 1)

            for n, (t0, count, w) in enumerate(NORM_GROUPS):
                head_norm(n, t0, count, par("hw")[:, w:w + 1])
            dve.wait_ge(S["hn_done"], len(NORM_GROUPS))
            for n, (t0, count) in enumerate(ROPE_GROUPS):
                x, t = PR[:, t0:t0 + count, :], rtmp[:, 0:count, :]
                bc = lambda name: cst(name).unsqueeze(1).broadcast_to((P, count, NT))
                dve.wait_ge(S["rope_rot"], n + 1)
                if n:
                    dve.wait_ge(S["rope_done"], n)
                dve.tensor_tensor(t, psum[:, n % 2 * 4:n % 2 * 4 + count, 0:NT], bc("sin"), ALU.mult)
                step(dve.tensor_tensor(x, x, bc("cos"), ALU.mult))
                dve.tensor_tensor(x, x, t, ALU.add).then_inc(S["rope_done"], 1)
            for v, w in enumerate(("wck", "wcv")):
                src = PR[:, T_KC + 2 * v:T_KC + 2 * v + 2, :]
                step(compress(src, N_CMP_P, par(w), ctmpp, CP[:, v, :, :], step))
                b = par("bck" if v == 0 else "bcv")
                step(dve.tensor_scalar(CP[:, v, :, :], CP[:, v, :, :], b, None, ALU.add))
                c = CK[:, v, :, :, 1:1 + N_CMP].rearrange("p b g n -> p (b g) n")
                ins = dve.tensor_scalar(c, c, b, None, ALU.add)
                if v == 0:
                    step(ins)
            ins.then_inc(S["cmp_ready"], 1)
            dve.wait_ge(S["rope_done"], 4)
            for v, tw, ts in ((0, T_KW, T_KS), (1, T_VW, T_VS)):
                dve.tensor_copy(CK[:, v, :, :, 0].rearrange("p b g -> p g b"), PR[:, tw:tw + G, SEQ:NT])
                dve.tensor_copy(CK[:, v, :, :, NC0 - 1].rearrange("p b g -> p g b"), PR[:, ts:ts + G, SEQ:NT])
            dve.wait_ge(S["cmp_rot"], 1)
            c = CK[:, 0, :, :, 1:1 + N_CMP].rearrange("p b g n -> p (b g) n")
            for m in range(2):
                dve.tensor_tensor(croll[:, 8 * m:8 * m + 8, :], bank[m][:, 0:8 * N_CMP].rearrange("p (m n) -> p m n", m=8),
                                  cst("sinc").unsqueeze(1).broadcast_to((P, 8, N_CMP)), ALU.mult)
            step(dve.tensor_tensor(c, c, cst("cosc").unsqueeze(1).broadcast_to((P, NS * G, N_CMP)), ALU.mult))
            step(dve.tensor_tensor(c, c, croll, ALU.add))
            bc = lambda name: cst(name)[:, 0:N_CMP_P].unsqueeze(1).broadcast_to((P, G, N_CMP_P))
            dve.tensor_tensor(croll[:, 0:G, 0:N_CMP_P], bank[2][:, 0:G * N_CMP_P].rearrange("p (g n) -> p g n", g=G),
                              bc("sinc"), ALU.mult)
            step(dve.tensor_tensor(CP[:, 0, :, :], CP[:, 0, :, :], bc("cosc"), ALU.mult))
            dve.tensor_tensor(CP[:, 0, :, :], CP[:, 0, :, :], croll[:, 0:G, 0:N_CMP_P], ALU.add).then_inc(S["cmp_done"], 1)
            with dve.Fori(0, DNT // 4) as i:
                for b in range(4):
                    t = 4 * i + b
                    dve.wait_ge(S["conv_silu"], t + 1)
                    link = Chain(dve, S["loop_step"], 3 * (t + NS))
                    x, y = PR[:, bass.ds(T_DNQ + t, 1), 0:SEQ], convt[:, b:b + 1, 0:SEQ]
                    w = [par("convw")[:, bass.ds(4 * t + j, 1)] for j in range(4)]
                    link(dve.tensor_scalar(y, x, w[3], None, ALU.mult))
                    for j in (1, 2, 3):
                        ins = dve.scalar_tensor_tensor(y[:, :, j:SEQ], x[:, :, 0:SEQ - j], w[3 - j], y[:, :, j:SEQ], ALU.mult, ALU.add)
                        if j < 3:
                            link(ins)
                    ins.then_inc(S["conv_done"], 1)
            cw = par("convw").rearrange("p (t j) -> p t j", j=4)
            dve.wait_ge(S["hist_new"], 1)
            for j in range(4):
                w = cw[:, :, j].unsqueeze(2).broadcast_to((P, DNT, NS))
                step(dve.tensor_tensor(convs if j == 0 else convs2, hist[:, :, j, :], w, ALU.mult))
                if j:
                    ins = dve.tensor_tensor(convs, convs, convs2, ALU.add)
                    if j < 3:
                        step(ins)
            ins.then_inc(S["conv_done"], 1)

            dve.wait_ge(S["conv_done"], DNT + 1)
            step(dve.memset(qpad, 0.0))
            for g in range(G):
                ins = dve.tensor_copy(qpad.rearrange("p (b g) r -> p b g r", g=G)[:, :, g, 0:REP],
                                      PR[:, g * REP:(g + 1) * REP, SEQ:NT].rearrange("p r b -> p b r"))
            ins.then_inc(S["qpad_done"], 1)
            causal = cst("causal").rearrange("p (a n) -> p a n", a=2)
            cmpbias = cst("cmpbias").rearrange("p (a n) -> p a n", a=2)
            cmp01 = cst("cmp01").rearrange("p (a n) -> p a n", a=2)

            def unit_max(u):
                a, b, n = u % 2, u % 2 * 2, P * (u % 2 + 1)
                dve.wait_ge(S["u_scores"], u + 1)
                if u >= 2:
                    dve.wait_ge(S["u_turned"], u - 1)
                s = SB[u % 2]
                dve.tensor_tensor(s[:, 512:512 + N_CMP_P], bank[b][:, 256:256 + N_CMP_P], cmpbias[:, a, 0:N_CMP_P], ALU.add)
                dve.tensor_tensor(s[:, 0:n], bank[b][:, 0:n], causal[:, a, 0:n], ALU.add)
                step(dve.tensor_tensor(s[:, 256:256 + n], bank[b + 1][:, 0:n], causal[:, a, 0:n], ALU.add))
                mx = sm1[:, u % 2, 2, :]
                for m, (lo, w) in enumerate(((512, N_CMP_P), (0, n), (256, n))):
                    ins = dve.tensor_reduce(mx[:, m:m + 1], s[:, lo:lo + w], AX.X, ALU.max)
                step(ins)
                dve.tensor_scalar(sm1[:, u % 2, 0, :], mx, -SCALE, None, ALU.mult).then_inc(S["u_max"], 1)

            dve.wait_ge(S["vt_evac"], 1)
            unit_max(0)
            for u in range(2 * H):
                if u + 1 < 2 * H:
                    unit_max(u + 1)
                h, a, n = u // 2, u % 2, P * (u % 2 + 1)
                f, s = sm1[:, u % 2, 1, :], SB[u % 2]
                dve.wait_ge(S["u_exp"], u + 1)
                step(dve.reciprocal(f, f))
                step(dve.tensor_tensor(f, f, GT[:, a, 3 * h:3 * h + 3], ALU.mult))
                dve.scalar_tensor_tensor(s[:, 512:512 + N_CMP_P], s[:, 512:512 + N_CMP_P], f[:, 0:1],
                                         cmp01[:, a, 0:N_CMP_P], ALU.mult, ALU.mult)
                dve.tensor_scalar(s[:, 0:n], s[:, 0:n], f[:, 1:2], None, ALU.mult)
                dve.tensor_scalar(s[:, 256:256 + n], s[:, 256:256 + n], f[:, 2:3], None, ALU.mult).then_inc(S["u_norm"], 1)

            dve.wait_ge(S["gates_in"], 16 * 12)
            dve.wait_ge(S["qpad_done"], 1)
            for q in range(4):
                dve.wait_ge(S["r_scores"], q + 1)
                if q:
                    dve.wait_ge(S["r_out"], q)
                dve.tensor_copy(SS[:, 0:512], bank[3])
                step(dve.tensor_copy(SS[:, 512:512 + NC0], bank[0][:, 0:NC0]))
                dve.tensor_copy(SS[:, 577:1601].rearrange("p (a n) -> p a n", a=2), psum[:, 1:3, :])
                step(dve.tensor_reduce(smS[:, 2, 0:1], SS[:, 513:576], AX.X, ALU.max))
                dve.tensor_scalar(smS[:, 0, 0:1], smS[:, 2, 0:1], -SCALE, None, ALU.mult).then_inc(S["r_cmpmax"], 1)
                dve.wait_ge(S["r_cmpexp"], q + 1)
                step(dve.reciprocal(smS[:, 1, 0:1], smS[:, 1, 0:1]))
                step(dve.tensor_scalar(SS[:, 513:576], SS[:, 513:576], smS[:, 1, 0:1], None, ALU.mult))
                win = bass.AP(SS.tensor, SS.offset + 513 + 3, [list(SS.ap[0]), [4, 14], [1, 5]])
                dve.tensor_reduce(impb[:, 0, 0:14], win, AX.X, ALU.add).then_inc(S["r_imp"], 1)
                dve.wait_ge(S["r_impsum"], q + 1)
                imp = bank[4][:, 0:14]
                step(dve.tensor_reduce(impb[:, 4, 0:1], imp, AX.X, ALU.min))
                step(dve.tensor_scalar(impb[:, 1, 0:14], imp, impb[:, 4, 0:1], None, ALU.is_equal))
                step(dve.tensor_tensor(impb[:, 1, 0:14], impb[:, 1, 0:14], cst("blockid"), ALU.mult))
                step(dve.tensor_reduce(impb[:, 4, 1:2], impb[:, 1, 0:14], AX.X, ALU.max))
                step(dve.tensor_scalar(impb[:, 2, 0:14], cst("blockid"), impb[:, 4, 1:2], NEG, ALU.is_equal, ALU.mult))
                blocks = SS[:, 577 + 64:577 + 64 * 15].rearrange("p (s n) -> p s n", s=14)
                step(dve.tensor_tensor(blocks, blocks, impb[:, 2, 0:14].unsqueeze(2).broadcast_to((P, 14, 64)), ALU.add))
                dve.tensor_reduce(smS[:, 2, 1:2], SS[:, 576:1601], AX.X, ALU.max)
                step(dve.tensor_reduce(smS[:, 2, 2:3], SS[:, 0:513], AX.X, ALU.max))
                dve.tensor_scalar(smS[:, 0, 1:3], smS[:, 2, 1:3], -SCALE, None, ALU.mult).then_inc(S["r_max"], 1)
                dve.wait_ge(S["r_exp"], q + 1)
                step(dve.reciprocal(smS[:, 1, 1:3], smS[:, 1, 1:3]))
                step(dve.tensor_tensor(smS[:, 1, 1:3], smS[:, 1, 1:3], gateS[:, q, 1:3], ALU.mult))
                dve.tensor_scalar(SS[:, 513:576], SS[:, 513:576], gateS[:, q, 0:1], None, ALU.mult)
                dve.tensor_scalar(SS[:, 576:1601], SS[:, 576:1601], smS[:, 1, 1:2], None, ALU.mult)
                dve.tensor_scalar(SS[:, 0:513], SS[:, 0:513], smS[:, 1, 2:3], None, ALU.mult).then_inc(S["r_norm"], 1)

            dve.wait_ge(S["small_evac"], 3)
            step(dve.tensor_scalar(rowsG[:], rowsG[:], par("dt")[0:H, :], None, ALU.add))
            step(dve.tensor_scalar(rows2[:, 0, :], rowsG[:], -1.0, None, ALU.mult))
            dve.tensor_tensor(rows2[:, 1, :], rows2[:, 0, :], rowsG[:], ALU.min).then_inc(S["g_parts"], 1)
            dve.wait_ge(S["g_soft"], 1)
            step(dve.scalar_tensor_tensor(rows2[:, 0, :], rowsG[:], 0.0, rows2[:, 1, :], ALU.max, ALU.add))
            step(dve.tensor_scalar(rows2[:, 0, :], rows2[:, 0, :], alog[:], -1.0, ALU.mult, ALU.mult))
            dve.tensor_copy(rowsG[:, SEQ:NT], rows2[:, 0, SEQ:NT])
            for c in range(2):
                r = slice(c * P, (c + 1) * P)
                ins = dve.tensor_tensor_scan(rowsG[:, r], ones[0:H, :], rows2[:, 0, r], 0.0, ALU.mult, ALU.add)
            ins.then_inc(S["g_rows"], 1)
            for n in range(5, 9):
                t0 = T_DNQ + 4 * (n - 5)
                dve.wait_ge(S["hn_std"], n + 1)
                r = rs[n % 2]
                step(dve.reciprocal(r, r))
                dve.tensor_tensor(PR[:, t0:t0 + 4, :], PR[:, t0:t0 + 4, :], r, ALU.mult).then_inc(S["hn_done"], 1)
            dve.wait_ge(S["g_colsc"], 2)
            dve.wait_ge(S["hn_done"], 9)
            gcol = cols[:, 0, :, :].rearrange("p h c -> p (h c)")
            bcol = cols[:, 1, :, :].rearrange("p h c -> p (h c)")
            for hb in range(2):
                dve.wait_ge(S["g_bcast"], hb + 1)
                if hb:
                    dve.wait_ge(S["d_half"], 1)
                for c in range(2):
                    dve.tensor_copy(glast[:, 4 * hb:4 * hb + 4, c], psum[:, 4:8, c * P + P - 1])
                for a in range(8):
                    u = 8 * hb + a
                    g = bank[4 + a // 2][:, a % 2 * P:(a % 2 + 1) * P]
                    dve.tensor_scalar(Cb[:, a, :], g, gcol[:, u:u + 1], 0.0, ALU.subtract, ALU.min)
                    ins = dve.tensor_scalar(Yb[:, a, :], g, gcol[:, u:u + 1], 0.0, ALU.subtract, ALU.max)
                ins.then_inc(S["d_diff"], 1)
                dve.wait_ge(S["d_exp"], hb + 1)
                dve.tensor_tensor(Cb, Cb, cst("upper").unsqueeze(1).broadcast_to((P, H, P)), ALU.mult)
                step(dve.tensor_tensor(Yb, Yb, cst("lower").unsqueeze(1).broadcast_to((P, H, P)), ALU.mult))
                dve.wait_ge(S["kk_mm"], hb + 1)
                flat = lambda ap: ap.rearrange("p (a u) n -> p a (u n)", u=4)
                dve.scalar_tensor_tensor(flat(Ab[:, 8 * hb:8 * hb + 8, :]), psum[:, 2:4, :], SCALE, flat(Cb), ALU.mult, ALU.mult)
                for a in range(8):
                    u = 8 * hb + a
                    ins = dve.scalar_tensor_tensor(Mb[:, u, :], bank[a // 4][:, a % 4 * P:(a % 4 + 1) * P], bcol[:, u:u + 1],
                                                   Yb[:, a, :], ALU.mult, ALU.mult)
                ins.then_inc(S["d_half"], 1)
            step(dve.tensor_tensor(kdec[:], glast[:], cols[:, 0, :, :], ALU.subtract))
            dve.nop().then_inc(S["kdec_diff"], 1)
            dve.memset(Tb, 0.0).then_inc(S["t_zero"], 1)
            step(dve.tensor_copy(Tm.rearrange("p i j -> p (i j)"), cst("ident16")))
            dve.wait_ge(S["m_in"], 16)
            for i in range(1, 16):
                t = dtmp[:, 0:16 * i].rearrange("p (j c) -> p j c", c=16)
                step(dve.tensor_tensor(t, Dm[:, i, 0:i].unsqueeze(2).broadcast_to((P, i, 16)), Tm[:, 0:i, :], ALU.mult))
                step(dve.tensor_reduce(dred, t.rearrange("p j c -> p c j"), AX.X, ALU.add))
                ins = dve.tensor_tensor(Tm[:, i, :], Tm[:, i, :], dred, ALU.subtract)
                if i < 15:
                    step(ins)
            ins.then_inc(S["t_ready"], 1)
            dve.wait_ge(S["t_evac"], 1)
            for n in range(6):
                level, half = n // 2, n % 2
                if n:
                    dve.wait_ge(S["lv_y"], n)
                mask = cst("levels")[:, level * P:(level + 1) * P].unsqueeze(1).broadcast_to((P, H, P))
                dve.tensor_tensor(Cb, Mb[:, 8 * half:8 * half + 8, :], mask, ALU.mult).then_inc(S["lv_c"], 1)
                dve.wait_ge(S["lv_z"], n + 1)
                u = flat(Ub[:, 8 * half:8 * half + 8, :])
                dve.tensor_tensor(u, u, psum[:, 2:4, :], ALU.subtract).then_inc(S["lv_u"], 1)
            banks4 = psum[:, 0:4, :].rearrange("p a (u n) -> p (a u) n", u=4)
            dve.wait_ge(S["vk_tok"], 1)
            dve.tensor_tensor(Tb, banks4, bcol.unsqueeze(2).broadcast_to((P, NU, P)), ALU.mult).then_inc(S["bv_ready"], 1)
            dve.wait_ge(S["kdec_exp"], 1)
            step(dve.tensor_tensor(bge[:], bge[:], cols[:, 1, :, 1], ALU.mult))
            dve.wait_ge(S["vk_tok"], 2)
            dve.tensor_tensor(Mb, banks4, kdec[:].rearrange("p h c -> p (h c)").unsqueeze(2).broadcast_to((P, NU, P)),
                              ALU.mult).then_inc(S["kd_ready"], 1)
            dve.wait_ge(S["zs_mm"], 1)
            odd = lambda ap: ap.rearrange("p (h c) n -> p h c n", c=2)[:, :, 1, :]
            units2 = lambda b: psum[:, b:b + 2, :].rearrange("p a (u n) -> p (a u) n", u=4)
            step(dve.tensor_tensor(Yb, units2(6), bge[:].unsqueeze(2).broadcast_to((P, H, P)), ALU.mult))
            dve.tensor_tensor(Yb, odd(Tb), Yb, ALU.subtract).then_inc(S["rhs_ready"], 1)
            dve.wait_ge(S["qe_exp"], 1)
            dve.scalar_tensor_tensor(Cb, Cb, SCALE, PR[:, T_DNQ:T_DNK, P:SEQ], ALU.mult, ALU.mult).then_inc(S["qe_ready"], 1)
            dve.wait_ge(S["s2_mm"], 1)
            step(dve.tensor_tensor(Yb, S1, egl[:].unsqueeze(2).broadcast_to((P, H, P)), ALU.mult))
            dve.tensor_tensor(Yb, Yb, units2(6), ALU.add).then_inc(S["s2_ready"], 1)
            dve.wait_ge(S["o_evac"], 2)
            hb_view = lambda t: PR[:, t:t + H, SEQ:NT]
            mat = lambda ap: ap.rearrange("p (h b) -> p h b", h=H)
            dve.tensor_copy(kq.rearrange("p (h b) c -> p h b c", h=H)[:, :, :, 0], hb_view(T_DNK))
            dve.tensor_copy(kq.rearrange("p (h b) c -> p h b c", h=H)[:, :, :, 1], hb_view(T_DNQ)).then_inc(S["smp_kq"], 1)
            dve.tensor_copy(mat(smp["kc"]), hb_view(T_DNK))
            dve.tensor_tensor(mat(smp["prod"]), hb_view(T_DNQ), hb_view(T_DNK), ALU.mult).then_inc(S["smp_prod"], 1)
            dve.wait_ge(S["smp_evac"], 2)
            dve.wait_ge(S["smp_rows"], 1)
            sk, sq_ = sks[:, :, 0], sks[:, :, 1]
            step(dve.tensor_tensor(smp["vn"], sk, smp["eg"], ALU.mult))
            step(dve.tensor_tensor(mat(smp["vn"]), hb_view(T_DNV), mat(smp["vn"]), ALU.subtract))
            dve.tensor_tensor(smp["vn"], smp["vn"], smp_g[:, 64:P], ALU.mult).then_inc(S["smp_vn"], 1)
            dve.wait_ge(S["smp_vn"], 1)
            step(dve.tensor_tensor(smp["prod"], sq_, smp["eg"], ALU.mult))
            step(dve.tensor_tensor(smp["qk"], smp["qk"], smp["vn"], ALU.mult))
            step(dve.tensor_tensor(smp["prod"], smp["prod"], smp["qk"], ALU.add))
            step(dve.tensor_scalar(hb_view(T_DNV), mat(smp["prod"]), SCALE, None, ALU.mult))
            dve.wait_ge(S["smp_evac"], 3)
            dve.wait_ge(S["s2_stored"], 16)
            dve.wait_ge(S["smp_mm"], 1)
            for m in range(2):
                s0 = ring[:, m, :].rearrange("p (m n) -> p m n", n=P)
                step(dve.tensor_tensor(s0, s0, smp["eg"][:, 32 * m:32 * m + 32].unsqueeze(2).broadcast_to((P, 32, P)), ALU.mult))
            for n in range(9):
                if n < 8:
                    if n:
                        dve.wait_ge(S["smp_outer"], n)
                    dve.tensor_tensor(vdiag, vtok.unsqueeze(1).broadcast_to((64, 8, P)),
                                      ident[0:64, 8 * n:8 * n + 8].unsqueeze(2).broadcast_to((64, 8, P)),
                                      ALU.mult).then_inc(S["smp_diag"], 1)
                if n:
                    m = n - 1
                    s0 = ring[:, m // 4, m % 4 * 1024:(m % 4 + 1) * 1024].rearrange("p (a n) -> p a n", a=2)
                    dve.wait_ge(S["smp_outer"], n)
                    b = 4 + m % 2 * 2
                    ins = dve.tensor_tensor(s0, s0, psum[:, b:b + 2, :], ALU.add)
                    if m % 4 == 3:
                        ins.then_inc(S["smp_new"], 1)
            dve.wait_ge(S["z_silu"], 1)
            for n in (9, 10):
                t0 = T_DNV + 4 * (n - 9)
                head_norm(n, t0, 4, par("dnw"))
                dve.wait_ge(S["hn_done"], n + 1)
                ins = dve.tensor_tensor(PR[:, t0:t0 + 4, :], PR[:, t0:t0 + 4, :], PR[:, t0 + 8:t0 + 12, :], ALU.mult)
            ins.then_inc(S["dn_out"], 1)
            with dve.Fori(0, N_MERGE_ADA) as i:
                ada_bias(i + N_ADA1, 2 * i + 2 * N_ADA1)
            pairs = lambda b: psum[:, b:b + 2, 0:NT]
            dve.wait_ge(S["proj_evac"], T_END + N_MERGE + 4)
            for n in range(8):
                b, t = n % 2 * 4, 2 * n
                ga, gb = PR[:, H + t:H + t + 2, :], PR[:, MERGE_B[n]:MERGE_B[n] + 2, :]
                dve.wait_ge(slot_used[n % 4], 28 + n // 4 + 2)
                dve.tensor_tensor(ga, ga, pairs(b), ALU.mult)
                step(dve.tensor_tensor(gb, gb, pairs(b + 2), ALU.mult))
                dve.tensor_tensor(hT[:, t:t + 2, :], ga, gb, ALU.add).then_inc(S["br_done"], 1)
            dve.wait_ge(S["x_again"], 16)
            dve.wait_ge(S["ada_done"], 49)
            for n in range(8):
                b, t = n % 4 * 2, 2 * n
                dve.wait_ge(slot_used[n % 4], 30 + n // 4 + 2)
                x1s = x1tmp[:, n % 2]
                step(dve.tensor_tensor(x1s, psum[:, b:b + 2, SEQ:NT], adaT[:, 2 * KT + t:2 * KT + t + 2, 1:NR], ALU.mult))
                for j in range(2):
                    dve.scalar_tensor_tensor(xT[:, t + j, 0:SEQ], bank[b + j][:, 0:SEQ], adaT[:, 2 * KT + t + j, 0:1],
                                             xT[:, t + j, 0:SEQ], ALU.mult, ALU.add)
                dve.tensor_tensor(xT[:, t:t + 2, SEQ:NT], xT[:, t:t + 2, SEQ:NT], x1s, ALU.add).then_inc(S["x1_done"], 1)
            dve.wait_ge(S["x_std"], 2)
            step(dve.reciprocal(rstd[:], rstd[:]))
            dve.wait_ge(S["x1_done"], 8)
            modulate(1, xT[:], hT[:], S["h_ready"])

            dve.sem_inc(S["acc_added"], 2)
            for a, (t0, n) in enumerate(TOKEN_TILES):
                sc, alt = SC[0:n, a % 2].rearrange("p (t n) -> p t n", n=P), SCr[0:n].rearrange("p (t n) -> p t n", n=P)
                val, idx = kval[0:n], kidx[0:n]
                dve.wait_ge(S["scores_in"], a + 1)

                def top16(src, alt, val, idx, count):
                    for t in range(count):
                        ins = dve.max(val[:, t, 0:8], src[:, t, :])
                    step(ins)
                    for t in range(count):
                        dve.max_index(idx[:, t, 0:8], val[:, t, 0:8], src[:, t, :])
                        ins = dve.match_replace(alt[:, t, :], val[:, t, 0:8], src[:, t, :], LOWEST)
                    step(ins)
                    for t in range(count):
                        ins = dve.max(val[:, t, 8:16], alt[:, t, :])
                    step(ins)
                    for t in range(count):
                        ins = dve.max_index(idx[:, t, 8:16], val[:, t, 8:16], alt[:, t, :])
                    step(ins)

                top16(sc, alt, val, idx, 16)
                step(dve.tensor_copy(kidxf[0:n], idx))
                half = lambda ap, m: ap.rearrange("p (h m) k -> p h m k", m=2)[:, :, m, :]
                step(dve.tensor_tensor(sc.rearrange("p (h a) (b k) -> p h (a b) k", a=2, k=16),
                                       half(val, 0).unsqueeze(3).broadcast_to((n, H, 16, 16)),
                                       half(val, 1).unsqueeze(2).broadcast_to((n, H, 16, 16)), ALU.add))
                wide = lambda ap: ap.rearrange("p (h a) n -> p h (a n)", a=2)
                best = chosen[0:n, 2, :].rearrange("p (h k) -> p h k", h=H)
                if a:
                    dve.wait_ge(S["chosen_turned"], a)
                top16(wide(sc), wide(alt), best, cpos[0:n, 0], H)
                step(dve.tensor_scalar(cpos[0:n, 1], cpos[0:n, 0], 4, None, ALU.logical_shift_right))
                step(dve.tensor_scalar(cpos[0:n, 2], cpos[0:n, 0], 15, None, ALU.bitwise_and))
                step(dve.tensor_copy(cposf[0:n], cpos[0:n, 1:3]))
                step(dve.tensor_copy(btop[0:n], best[:, :, 0:1]))
                dve.tensor_tensor(best, best, btop[0:n].broadcast_to((n, H, 16)), ALU.subtract).then_inc(S["best_sub"], 1)
                for m in range(2):
                    eq = alt.rearrange("p t (a j) -> p (t a) j", j=16)
                    step(dve.tensor_tensor(eq, cst("iota")[0:n, 0:16].unsqueeze(1).broadcast_to((n, P, 16)),
                                           cposf[0:n, m].rearrange("p h k -> p (h k)").unsqueeze(2).broadcast_to((n, P, 16)), ALU.is_equal))
                    eq4 = eq.rearrange("p (h k) j -> p h k j", h=H)
                    step(dve.tensor_tensor(eq4, eq4, half(kidxf[0:n], m).unsqueeze(2).broadcast_to((n, H, 16, 16)), ALU.mult))
                    step(dve.tensor_reduce(chosen[0:n, m, :], eq, AX.X, ALU.add))
                dve.wait_ge(S["best_exp"], a + 1)
                step(dve.tensor_reduce(bsum[0:n], best, AX.X, ALU.add))
                step(dve.reciprocal(bsum[0:n], bsum[0:n]))
                dve.tensor_tensor(best, best, bsum[0:n].unsqueeze(2).broadcast_to((n, H, 16)), ALU.mult).then_inc(S["chosen"], 1)
            dve.sem_inc(S["route_mm"], 2)
            dve.wait_ge(S["chosen_evac"], 3)
            with dve.Fori(0, NT // 8) as i:
                for b in range(2):
                    dve.wait_ge(S["route_mm"], 2 * i + b + 1)
                    for t in range(4):
                        col = 8 * i + 4 * b + t
                        dve.tensor_scalar(O2[:, b, t, :], cst("iota"), IT[:, 1, bass.ds(col, 1)], IT[:, 2, bass.ds(col, 1)],
                                                ALU.is_equal, ALU.mult)
                        ins = dve.tensor_scalar(O1[:, b, t, :], cst("iota"), IT[:, 0, bass.ds(col, 1)], None, ALU.is_equal)
                    ins.then_inc(S["onehot"], 1)
            dve.wait_ge(S["route_stored"], 16 * len(ROUTE_BLOCKS))
            step(dve.memset(acc, 0.0))

            def expert_act(b, i, g):
                dve.wait_ge(S["expert_gelu"], g + 3)
                dve.wait_ge(S[f"route_in{b}"], 16 * (i + 1))
                dve.tensor_tensor(act_x[:, b], act_x[:, b], Wb[:, b], ALU.mult).then_inc(S["expert_act"], 1)

            def expert_sum(b, use, g):
                for m in range(8):
                    if m < 7:
                        dve.wait_ge(S["acc_mm"], 7 * g + m + 1)
                    else:
                        dve.wait_ge(slot_used[2 * b + 1], use + 2)
                    if m == 0:
                        dve.wait_ge(S["acc_added"], 8 * g + 2)
                    dst = acc[:, 2 * m:2 * m + 2, :]
                    v = 4 + m % 2 * 2
                    dve.tensor_tensor(dst, dst, psum[:, v:v + 2, 0:NT], ALU.add).then_inc(S["acc_added"], 1)

            expert_act(0, 0, 0)
            with dve.Fori(0, N_GROUP // 2 - 1) as i:
                expert_act(1, i, 2 * i + 1)
                expert_sum(0, i + 34, 2 * i)
                expert_act(0, i + 1, 2 * i + 2)
                expert_sum(1, i + 34, 2 * i + 1)
            expert_act(1, N_GROUP // 2 - 1, N_GROUP - 1)
            expert_sum(0, 33 + N_GROUP // 2, N_GROUP - 2)
            expert_sum(1, 33 + N_GROUP // 2, N_GROUP - 1)
            dve.wait_ge(S["acc_added"], 8 * N_GROUP + 2)
            gate2 = adaT[:, 5 * KT:6 * KT, :]
            for t in range(KT):
                dve.scalar_tensor_tensor(acc[:, t, 0:SEQ], acc[:, t, 0:SEQ], gate2[:, t, 0:1], xT[:, t, 0:SEQ], ALU.mult, ALU.add)
            step(dve.tensor_tensor(acc[:, :, SEQ:NT], acc[:, :, SEQ:NT], gate2[:, :, 1:NR], ALU.mult))
            dve.tensor_tensor(acc[:, :, SEQ:NT], acc[:, :, SEQ:NT], xT[:, :, SEQ:NT], ALU.add).then_inc(S["y_ready"], 1)


NORM_GROUPS = [(0, 4, 0), (4, 4, 0), (T_KC, 2, 1), (T_KS, 2, 2), (T_KW, 2, 3)]
ROPE_GROUPS = [(0, 4), (4, 4), (T_KS, 2), (T_KW, 2)]


def column_tiles(w, n):
    import numpy as np
    return np.ascontiguousarray(w.reshape(KT, P, n, 256).transpose(2, 1, 0, 3).reshape(n, P, SLOT))


def feature_major(a):
    import numpy as np
    return np.ascontiguousarray(a.T.reshape(KT, P, -1).transpose(1, 0, 2))


def packed(places, width, values):
    import numpy as np
    out = np.zeros((P, width), np.float32)
    for name, v in values.items():
        v = np.asarray(v, np.float32)
        lo, hi = places[name]
        out[:v.shape[0], lo:hi] = v.reshape(v.shape[0], hi - lo)
    return out


def shape_constants():
    import numpy as np
    p = np.arange(P)
    half = P // 2
    perm = np.zeros((P, P))
    perm[np.arange(half) + half, np.arange(half)] = -1
    perm[np.arange(half), np.arange(half) + half] = 1
    sumsel = np.zeros((P, NR))
    for g in range(4):
        sumsel[32 * g + np.arange(NR), np.arange(NR)] = 1
    inv = (10000.0 ** (-np.arange(half, dtype=np.float64) / half)).astype(np.float32)

    def rope(pos):
        ang = (pos[None, :].astype(np.float32) * inv[:, None]).astype(np.float64)
        ang = np.concatenate([ang, ang])
        return np.cos(ang), np.sin(ang)

    cos, sin = rope(np.concatenate([np.arange(SEQ), np.full(NS, PAST)]))
    cosc, sinc = rope(np.arange(N_CMP) * 16 + 31)
    t = np.arange(SEQ).reshape(2, P).T
    end = np.arange(16) * 16 + 31
    seen = end[None, None] <= t[:, :, None]
    return packed(CONSTS, N_CONST, dict(
        ident=np.eye(P), perm=perm, sumsel=sumsel, cos=cos, sin=sin, cosc=cosc, sinc=sinc,
        gsum=(p[:, None] // 32 == p[None] // 32) & (p[:, None] % 32 < REP),
        causal=np.where(np.arange(SEQ)[None, None] <= t[:, :, None], 0, NEG),
        cmpbias=np.where(seen | (t[:, :, None] < 31), 0, NEG), cmp01=seen,
        upper=p[:, None] <= p[None], lower=p[:, None] > p[None],
        levels=np.stack([((p[:, None] // b) % 2 == 1) & (p[None] // b == p[:, None] // b - 1) for b in (16, 32, 64)], 1),
        iota=np.tile(p, (P, 1)), ident16=np.tile(np.eye(16).reshape(1, -1), (P, 1)),
        blockid=np.tile(np.arange(1, 15), (P, 1))))


def lay_out(X):
    import numpy as np
    tile = lambda v: v.reshape(-1, P).T
    c = np.zeros((32, D), np.float32)
    c[0], c[1:NR] = X["c_prompt"][0], X["c_sample"]
    w = X["w_in"][0]
    o = np.cumsum([0, 1024, 1536, 24, 3072, 8, 8, 1024, 4096])
    small = np.zeros((D, SM), np.float32)
    small[:, SM_A:SM_A + H] = w[:, o[4]:o[5]]
    small[:, SM_B:SM_B + H] = w[:, o[5]:o[6]]
    small[:, SM_G:SM_G + 3 * H] = w[:, o[2]:o[3]]
    rows = lambda a: a.transpose(0, 3, 2, 1)
    ck, cv, sk, sv = (X["cache_" + n][0] for n in ("cmp_k", "cmp_v", "slc_k", "slc_v"))
    wk, wv = X["state_win_k"][0], X["state_win_v"][0]
    d = dict(
        c=feature_major(c), x=feature_major(np.concatenate([X["x_prompt"][0], X["x_sample"][:, 0]])),
        consts=shape_constants(),
        params=packed(PARAMS, N_PARAM, dict(
            bada=tile(X["b_ada"][0]), nw=np.stack([tile(X["norm1_w"][0]), tile(X["norm2_w"][0])], 1),
            hw=np.stack([X["q_norm_w"][0], *X["k_norm_w"][0]], 1), wck=X["w_cmp_k"][0].T, wcv=X["w_cmp_v"][0].T,
            bck=X["b_cmp_k"][0][:, None], bcv=X["b_cmp_v"][0][:, None],
            convw=X["dn_conv_w"][0].reshape(4, DNT, P).transpose(2, 1, 0), dnw=X["dn_norm_w"][0][:, None],
            alog=X["dn_A_log"][0][:, None], dt=X["dn_dt_bias"][0][:, None])),
        w_small=small.reshape(KT, P, SM).transpose(1, 0, 2),
        w_ada=column_tiles(X["w_ada"][0], 48),
        w_in=column_tiles(np.concatenate([w[:, o[0]:o[2]], w[:, o[3]:o[4]], w[:, o[6]:o[8]]], 1), 42),
        w_br=column_tiles(np.concatenate([X["w_br_a"][0], X["w_br_b"][0]]), 8), w_out=column_tiles(X["w_out"][0], 8),
        w_peer_q=X["w_peer_q"][0].reshape(H, KT, P, 256).transpose(0, 2, 1, 3).reshape(H, P, SLOT),
        w_keys=X["w_peer_keys"][0].reshape(2 * H, P, P).transpose(2, 0, 1),
        w_peer_u=X["w_peer_u"][0].reshape(N_GROUP, 256, KT, P).transpose(0, 3, 2, 1).reshape(N_GROUP, P, SLOT),
        w_peer_v=X["w_peer_v"][0].reshape(N_GROUP, 2, P, D).transpose(0, 2, 1, 3).reshape(N_GROUP, P, SLOT),
        pages=X["page_table"].reshape(1, NS * PAGES),
        conv_hist=X["state_conv"][0].reshape(NS, 3, DNT, P).transpose(3, 2, 1, 0),
        cache_cmp=np.stack([rows(ck), rows(cv)], 2).reshape(POOL, P, 4 * P),
        cache_slc=np.concatenate([rows(sk).reshape(POOL, P, 2 * P), sv.reshape(POOL, P, 2 * P)], 2),
        win=np.concatenate([wk.transpose(0, 3, 2, 1).reshape(NS, P, G * WIN),
                            wv.reshape(NS, 4, P, G * P).transpose(0, 2, 1, 3).reshape(NS, P, G * WIN)], 2),
        win_k_rows=wk.reshape(NS, -1)[:, G * P:], win_v_rows=wv.reshape(NS, -1)[:, G * P:],
        s_delta0=X["state_delta"][0].transpose(2, 1, 0, 3).reshape(P, 2, SLOT).transpose(1, 0, 2))
    return {k: np.ascontiguousarray(v) for k, v in d.items()}


OUTS = dict(y=(P, KT, NT), kv=(P, 12, NT), p_conv=(P, DNT, 3), p_delta=(P, H, P), s_win_k=(NS, (WIN - 1) * G * P),
            s_win_v=(NS, (WIN - 1) * G * P), s_conv=(P, DNT, 3, NS), s_delta=(2, P, SLOT))


def gather_outputs(r):
    import numpy as np
    y = r["y"].transpose(2, 1, 0).reshape(NT, D)
    kv = r["kv"].reshape(P, 6, G, NT).transpose(1, 3, 2, 0)
    win = [np.concatenate([r[n].reshape(NS, WIN - 1, G, P), kv[i, SEQ:, None]], 1)[None]
           for n, i in (("s_win_k", 4), ("s_win_v", 5))]
    out = (y[None, :SEQ], y[SEQ:, None],
           *(kv[i, :SEQ][None, None] for i in range(6)),
           r["p_conv"].transpose(2, 1, 0).reshape(1, 1, 3, DNT * P),
           r["p_delta"].transpose(1, 0, 2)[None, None],
           *(kv[i, SEQ:][None, :, None] for i in range(4)), *win,
           r["s_conv"].transpose(3, 2, 1, 0).reshape(1, NS, 3, DNT * P),
           r["s_delta"].transpose(1, 0, 2).reshape(P, H, NS, P).transpose(2, 1, 0, 3)[None])
    return tuple(np.ascontiguousarray(a) for a in out)


def kernel(**inputs):
    import numpy as _np
    import concourse.bacc as _bacc
    from concourse import mybir as _mybir
    from concourse.bass_utils import run_bass_kernel_spmd as _run

    nc = _bacc.Bacc("TRN2", target_bir_lowering=False, num_devices=1, dynamic_dma_scratch_size=1024)
    data = lay_out({k: _np.asarray(v) for k, v in inputs.items()})
    I = {k: nc.dram_tensor("in_" + k, a.shape, _mybir.dt.from_np(a.dtype), kind="ExternalInput").ap() for k, a in data.items()}
    O = {k: nc.dram_tensor("out_" + k, s, _mybir.dt.float32, kind="ExternalOutput").ap() for k, s in OUTS.items()}
    build_program(nc, I, O)
    r = _run(nc, [{"in_" + k: a for k, a in data.items()}], core_ids=[0])
    return gather_outputs({k: r.results[0]["out_" + k] for k in OUTS})
```

```python
from contextlib import ExitStack

import concourse.bass as bass
from concourse import mybir

F32 = mybir.dt.float32
F32R = mybir.dt.float32r
I32 = mybir.dt.int32
U32 = mybir.dt.uint32
ALU = mybir.AluOpType
ACT = mybir.ActivationFunctionType
AX = mybir.AxisListType

P = 128
D = 2048
KT = D // P
SEQ = 256
NS = 8
NT = SEQ + NS
NR = 1 + NS
H, G = 8, 2
REP = H // G
EPS = 1e-6
SCALE = float(P) ** -0.5
NEG = -1e30
LOWEST = -3.4e38
PAST = 1024
PAGES = PAST // P
POOL = 80
WIN = 512
N_CMP = (PAST - 32) // 16 + 1
N_CMP_P = (SEQ - 32) // 16 + 1
NC0 = N_CMP + 2
N_WORK = 6400
NU = 2 * H
SM_A, SM_B, SM_G, SM = 0, 32, 64, 96

T_KC, T_VC, T_KS, T_VS, T_KW, T_VW = 8, 10, 12, 14, 16, 18
T_DNQ, T_DNK, T_DNV, T_Z, T_END = 20, 28, 36, 44, 52
DNT = T_Z - T_DNQ

SLOTS = 4
SLOT = KT * 256
PAGED = (3, 3, 3, 11)

N_ADA0 = 2 * D // 256
N_ADA1 = 30
LAST_ADA = [(2, 26), (3, 26), (0, 27), (1, 27), (2, 27), (3, 27)]
N_MERGE = 32
N_MERGE_EARLY = 4
MERGE_B = [24, 26, 28, 30, 32, 34, 44, 46]
N_DENSE = 24
T_DENSE = 48 * NT

N_GROUP = 64
N_EARLY = 20
N_LATE = N_GROUP - N_EARLY
V_USE = 39 + N_LATE // 2
TOKEN_TILES = [(0, 128), (128, 128), (256, 8)]
ROUTE_BLOCKS = [(0, 136), (136, 128)]

CONSTS, N_CONST = {}, 0
for _name, _n in (("ident", P), ("perm", P), ("sumsel", NR), ("cos", NT), ("sin", NT), ("cosc", N_CMP), ("sinc", N_CMP),
                  ("gsum", P), ("causal", 2 * SEQ), ("cmpbias", 32), ("cmp01", 32), ("upper", P), ("lower", P),
                  ("levels", 3 * P), ("iota", P), ("ident16", 256), ("blockid", 14)):
    CONSTS[_name] = (N_CONST, N_CONST + _n)
    N_CONST += _n
PARAMS, N_PARAM = {}, 0
for _name, _n in (("bada", 96), ("nw", 2 * KT), ("hw", 4), ("wck", 32), ("wcv", 32), ("bck", 1), ("bcv", 1),
                  ("convw", DNT * 4), ("dnw", 1), ("alog", 1), ("dt", 1)):
    PARAMS[_name] = (N_PARAM, N_PARAM + _n)
    N_PARAM += _n


class Chain:

    def __init__(self, eng, sem, base=0):
        self.eng, self.sem, self.n = eng, sem, base

    def __call__(self, ins):
        self.n = self.n + 1
        ins.then_inc(self.sem, 1)
        self.eng.wait_ge(self.sem, self.n)


def build_program(nc, I, O):
    with ExitStack() as ctx:
        def sb(name, shape, dt=F32):
            return ctx.enter_context(nc.sbuf_tensor(name, shape, dt))

        def sem(name):
            return ctx.enter_context(nc.semaphore(name))

        psum = ctx.enter_context(nc.psum_tensor("psum", [P, 8, 512], F32))
        bank = [psum[:, i, :] for i in range(8)]

        ring = sb("ring", [P, SLOTS, SLOT])
        xT = sb("xT", [P, KT, NT])
        hT = sb("hT", [P, KT, NT])
        arena = sb("arena", [P, T_END * NT + N_WORK])
        PR = arena[:, 0:T_END * NT].rearrange("p (t n) -> p t n", n=NT)
        work = arena[:, T_END * NT:]
        adaT = sb("adaT", [P, 6 * KT, NR])
        cstat = sb("cstat", [P, KT, 32])
        consts = sb("consts", [P, N_CONST])
        params = sb("params", [P, N_PARAM])
        hist = sb("hist", [P, DNT, 4, NS])
        CK = sb("CK", [P, 2, NS, G, NC0])
        ones = sb("ones", [P, P])
        adaS = sb("adaS", [P, 2, 256])
        A1 = sb("A1", [P, KT, NR])
        rstd = sb("rstd", [P, NT])
        rowsG = sb("rowsG", [H, NT])
        rowsB = sb("rowsB", [H, NT])
        gates = sb("gates", [3 * H, NT])
        epst = sb("epst", [P, 1])
        ptab = sb("ptab", [1, NS * PAGES], I32)

        gate_scratch = nc.dram_tensor("gate_scratch", (3 * H, NS), F32, kind="Internal").ap()

        def cst(name):
            return consts[:, CONSTS[name][0]:CONSTS[name][1]]

        def par(name):
            return params[:, PARAMS[name][0]:PARAMS[name][1]]

        ident = cst("ident")
        xflat = xT[:].rearrange("p k n -> p (k n)")

        wsmall = work[:, 0:KT * SM].rearrange("p (k n) -> p k n", k=KT)
        sq = [work[:, 1056 * i:1056 * (i + 1)].rearrange("p (t n) -> p t n", t=4) for i in range(2)]
        rs = [work[:, 2112 + 1056 * i:2112 + 1056 * (i + 1)].rearrange("p (t n) -> p t n", t=4) for i in range(2)]
        rtmp = work[:, 4224:5280].rearrange("p (t n) -> p t n", t=4)
        convt = work[:, 5280:6336].rearrange("p (t n) -> p t n", t=4)
        ctmp = xflat[:, 0:G * N_CMP * 32].rearrange("p (g n j) -> p g n j", g=G, j=32)
        ctmpp = xflat[:, 0:G * N_CMP_P * 32].rearrange("p (g n j) -> p g n j", g=G, j=32)
        croll = xflat[:, 0:NS * G * N_CMP].rearrange("p (m n) -> p m n", m=NS * G)
        SB = [work[:, 0:544], work[:, 544:1088], xflat[:, 3400:3944]]
        PTs = [work[:, 1088 + 640 * i:1088 + 640 * (i + 1)] for i in range(2)]
        V0 = work[0:NC0, 2368:4416].rearrange("p (m d) -> p m d", m=NS * G)
        qpad = work[:, 4416:4928].rearrange("p (m r) -> p m r", m=NS * G)
        VT = work[:, 4928:5952].rearrange("p (a d) -> p a d", a=8)
        CVT = work[0:N_CMP_P, 5952:6208].rearrange("p (g d) -> p g d", g=G)
        SS = xflat[:, 0:1601]
        PTS = xflat[:, 1664:1664 + 13 * P].rearrange("p (a d) -> p a d", a=13)
        convs = rtmp[:, 0:1, 0:DNT * NS].rearrange("p a (t b) -> p (a t) b", b=NS)
        convs2 = rtmp[:, 1:2, 0:DNT * NS].rearrange("p a (t b) -> p (a t) b", b=NS)
        praw = sb("praw", [P, DNT, 3])
        CP = sb("CP", [P, 2, G, N_CMP_P])
        GT = sb("GT", [P, 2, 3 * H])
        gateS = sb("gateS", [P, 4, 3])
        sm1 = sb("sm1", [P, 2, 3, 3])
        smS = sb("smS", [P, 3, 3])
        impb = sb("impb", [P, 5, 16])
        osb = sb("osb", [P, P])

        Mb, Ab = (xflat[:, 2048 * i:2048 * (i + 1)].rearrange("p (u n) -> p u n", u=NU) for i in range(2))
        Tb, Ub = (work[:, 2048 * i:2048 * (i + 1)].rearrange("p (u n) -> p u n", u=NU) for i in range(2))
        Cb, Yb = (work[:, 4096 + 1024 * i:5120 + 1024 * i].rearrange("p (u n) -> p u n", u=H) for i in range(2))
        ckflat = CK[:].rearrange("p v b g n -> p (v b g n)")
        VN, S1 = (ckflat[:, 1024 * i:1024 * (i + 1)].rearrange("p (u n) -> p u n", u=H) for i in range(2))
        Dm, Tm = (work[:, 2048 + 256 * i:2304 + 256 * i].rearrange("p (i j) -> p i j", i=16) for i in range(2))
        dtmp = work[:, 2560:2800]
        dred = work[:, 2816:2832]
        rows2 = sb("rows2", [H, 2, NT])
        alog = sb("alog", [H, 1])
        smp_g = sb("smp_g", [P, P])
        cols = sb("cols", [P, 2, H, 2])
        glast = sb("glast", [P, H, 2])
        kdec = sb("kdec", [P, H, 2])
        bge = sb("bge", [P, H])
        egl = sb("egl", [P, H])
        smp = {n: work[:, 4096 + 64 * i:4160 + 64 * i] for i, n in enumerate(("k0", "k1", "s0", "s1", "eg", "bb", "prod", "qk", "vn", "kc"))}
        kq = work[:, 4096:4224].rearrange("p (m c) -> p m c", c=2)
        sks = work[:, 4224:4352].rearrange("p (m c) -> p m c", c=2)
        ktok, vtok = work[0:64, 4736:4864], work[0:64, 4864:4992]
        vdiag = work[0:64, 5120:6144].rearrange("p (m n) -> p m n", m=8)
        keys = arena[:, 4224:6272].rearrange("p (t n) -> p t n", t=16)
        SC = arena[:, 13824:19968].rearrange("p (a n) -> p a n", a=3)
        SCr = arena[:, 10368:12416]
        kval = arena[:, 12416:12672].rearrange("p (t k) -> p t k", t=16)
        kidxf = arena[:, 12672:12928].rearrange("p (t k) -> p t k", t=16)
        chosen = arena[:, 12928:13312].rearrange("p (v n) -> p v n", v=3)
        cposf = arena[:, 13312:13568].rearrange("p (v h k) -> p v h k", v=2, h=H)
        btop = arena[:, 13568:13576].unsqueeze(2)
        bsum = arena[:, 13576:13584]
        kidx = sb("kidx", [P, 16, 16], U32)
        cpos = sb("cpos", [P, 3, H, 16], U32)
        IT = ckflat[:, 0:3 * NT].rearrange("p (v n) -> p v n", v=3)
        WS = arena[:, 0:ROUTE_BLOCKS[0][1] * P]
        O1, O2 = (arena[:, 17408 + 1024 * i:18432 + 1024 * i].rearrange("p (b t n) -> p b t n", b=2, t=4) for i in range(2))
        acc = arena[:, 0:KT * NT].rearrange("p (t n) -> p t n", n=NT)
        act_x, Wb = (arena[:, 4224 + 1056 * i:5280 + 1056 * i].rearrange("p (b j n) -> p b j n", b=2, j=2) for i in range(2))

        def overlay(name, tensor, column, shape):
            return nc.alloc_sbuf_tensor_at(name, shape, F32R, offset=nc.lookup_mloc(tensor).addr + 4 * column)

        act_lo = overlay("act_lo", arena, 4224, [P, 2, 2, NT])
        act_hi = overlay("act_hi", arena, 6336, [P, 2, 2, NT])
        w_hi = overlay("w_hi", arena, 7392, [P, 2, SLOT])
        h2_hi = overlay("h2_hi", arena, 7392 + 2 * SLOT, [P, KT, NT])
        w_lo = overlay("w_lo", ring, 0, [P, SLOTS, SLOT])
        h2_lo = overlay("h2_lo", hT, 0, [P, KT, NT])
        o_hi = overlay("o_hi", xT, 0, [P, 2 * H, NT])
        pr_lo = overlay("pr_lo", arena, 0, [P, T_END, NT])
        mixed_hi = overlay("mixed_hi", arena, H * NT, [P, KT, NT])
        hq_hi, hq_lo = (overlay(n, arena, t * NT, [P, KT, NT]) for n, t in (("hq_hi", 16), ("hq_lo", 32)))
        quarter_hi = [overlay("wd_hi0", arena, T_DENSE, [P, 4, SLOT // 4]), overlay("wd_hi1", arena, T_DENSE + SLOT, [P, 2, SLOT // 4]),
                      overlay("wd_hi2", CK, 0, [P, 2, SLOT // 4])]

        def dense_hi(part, c):
            return quarter_hi[0][:, c, :] if part == 0 else quarter_hi[1 + c // 2][:, c % 2, :]
        early_x = ckflat[:, 3 * NT:7 * NT].rearrange("p (b j n) -> p b j n", b=2, j=2)
        gelu_scratch = nc.dram_tensor("gelu_scratch", (N_EARLY, P, 2, NT), F32, kind="Internal").ap()
        route_w = nc.dram_tensor("route_w", (P, 2 * N_GROUP, NT), F32, kind="Internal").ap()
        x1sq = PR[:, 28:44, :]
        x1tmp = work[:, 5120:5152].rearrange("p (a t b) -> p a t b", a=2, t=2)
        m_scratch = nc.dram_tensor("m_scratch", (NU, 8, 16, 16), F32, kind="Internal").ap()
        t_scratch = nc.dram_tensor("t_scratch", (NU, 8, 16, 16), F32, kind="Internal").ap()

        slot_full = [sem(f"slot_full{i}") for i in range(SLOTS)]
        slot_used = [sem(f"slot_used{i}") for i in range(SLOTS)]
        cache_full = [sem(f"cache_full{i}") for i in range(SLOTS)]
        names = """consts_in consts_set ada_copied ada_reduced ada_done x_squared x_summed x_std dve_step act_step
            loop_step h_ready wsmall_in small_mm small_evac proj_mm proj_evac gates_out gates_in
            hn_sq hn_sum hn_std hn_done rope_rot rope_done conv_done conv_silu raw_saved hist_new cmp_ready
            cmp_rot cmp_done vt_mm vt_evac qpad_done u_scores u_max u_exp u_norm u_turned u_evac u_mm
            u_out r_scores r_cmpmax r_cmpexp r_imp r_impsum r_max r_exp r_norm r_turned r_evac r_oevac r_oturned
            r_out stored g_parts g_soft g_rows g_cols g_colsc g_bcast kk_mm d_diff d_exp d_half m_out m_in
            t_ready t_out t_zero t_in t_mm t_evac lv_c lv_y lv_ye lv_z lv_u lv_t lv_te vk_tok bv_ready kd_ready
            kdec_diff kdec_exp vn_mm vn_evac o_mm o_evac s1_mm s1_evac zs_mm rhs_ready qe_mm qe_exp qe_ready
            s2_mm s2_ready s2_stored z_silu smp_rows smp_kq smp_mm smp_evac smp_vn smp_diag smp_outer
            smp_new smp_stored dn_out o_top o_split x_again br_done x1_done keys_in pq_evac key_mm scores_in best_sub best_exp
            chosen chosen_turned chosen_evac onehot route_mm route_free route_evac route_stored
            route_in0 route_in1 split_hi split_lo split_lo2 act_chain gelu_early gelu_stored0 gelu_stored1 expert_gelu expert_act acc_mm acc_added y_ready""".split()
        S = {n: sem(n) for n in names}

        def slot_kt(s):
            return ring[:, s, :].rearrange("p (k n) -> p k n", k=KT)

        slc_slot = [ring[:, s, :].rearrange("p (a v n) -> p a v n", a=PAGES, v=2) for s in range(SLOTS)]

        block = ctx.enter_context(nc.Block())

        @block.sync
        def _(sp):
            for dst, name in ((cstat, "c"), (xT, "x"), (consts, "consts"), (params, "params"), (ptab, "pages")):
                sp.dma_start(dst[:], I[name]).then_inc(S["consts_in"], 16)
            sp.dma_start(hist[:, :, 0:3, :], I["conv_hist"]).then_inc(S["consts_in"], 16)
            sp.dma_start(wsmall, I["w_small"]).then_inc(S["wsmall_in"], 16)

            def load(s, use, src):
                sp.wait_ge(slot_used[s], use + 1)
                sp.dma_start(ring[:, s, :], src).then_inc(slot_full[s], 16)

            def tile_of(name, n):
                return I[name][bass.ds(n, 1)].rearrange("a p n -> p (a n)")

            def load_pages(s, use, seq, name, dst):
                sp.wait_ge(slot_used[s], use + 1)
                for p in range(PAGES):
                    page = sp.value_load(ptab[0:1, bass.ds(seq * PAGES + p, 1)], min_val=0, max_val=POOL - 1)
                    sp.dma_start(dst(p), I[name][bass.ds(page, 1)].rearrange("a p (v n) -> p (a v) n", v=4)
                                 if name == "cache_cmp" else I[name][bass.ds(page, 1)].rearrange("a p n -> p (a n)")
                                 ).then_inc(cache_full[s], 16)

            sp.wait_ge(S["consts_in"], 16 * 6)
            with sp.Fori(0, N_ADA0 // 4) as i:
                for s in range(4):
                    load(s, i, tile_of("w_ada", 4 * i + s))
            cmp_dst = ring[:, 3, :].rearrange("p (v r) -> p v r", v=4)
            with sp.Fori(0, 8) as i:
                load(0, i + 4, tile_of("w_in", 2 * i))
                load(1, i + 4, tile_of("w_ada", i + 16))
                load(2, i + 4, tile_of("w_in", 2 * i + 1))
                load_pages(3, i + 4, i, "cache_cmp", lambda p: cmp_dst[:, :, p * P:(p + 1) * P])
            with sp.Fori(0, 3) as i:
                load(0, i + 12, tile_of("w_in", 2 * i + 16))
                load(1, i + 12, tile_of("w_ada", 2 * i + 24))
                load(2, i + 12, tile_of("w_in", 2 * i + 17))
                load(3, i + 12, tile_of("w_ada", 2 * i + 25))
            for s in range(SLOTS):
                load(s, 15, I["w_in"][T_Z // 2 + s])
            sp.wait_ge(S["raw_saved"], 1)
            sp.wait_ge(S["hist_new"], 1)
            sp.dma_start(O["s_conv"], hist[:, :, 1:4, :]).then_inc(S["stored"], 16)
            sp.dma_start(O["p_conv"], praw[:]).then_inc(S["stored"], 16)
            sp.dma_start(O["s_win_k"], I["win_k_rows"]).then_inc(S["stored"], 16)
            sp.dma_start(O["s_win_v"], I["win_v_rows"]).then_inc(S["stored"], 16)
            sp.wait_ge(S["small_evac"], 3)
            sp.dma_start(gate_scratch, gates[:, SEQ:NT]).then_inc(S["gates_out"], 16)
            sp.wait_ge(S["gates_out"], 16)
            sp.wait_ge(S["consts_set"], 3)
            for j in range(4):
                for a in range(3):
                    src = gate_scratch.rearrange("(g r a) (q s) -> g s r q a", g=G, a=3, s=2)
                    sp.dma_start(gateS[32 * j:32 * j + REP, :, a], src[j % G, j // G, :, :, a],
                                 allow_slow_non_contiguous=True).then_inc(S["gates_in"], 16)
            for q in range(4):
                for m in range(2):
                    s, use = (3 * q + m) % 4, 16 + (3 * q + m) // 4
                    load_pages(s, use, 2 * q + m, "cache_slc", lambda p: ring[:, s, 512 * p:512 * (p + 1)])
                s, use = (3 * q + 2) % 4, 16 + (3 * q + 2) // 4
                sp.wait_ge(slot_used[s], use + 1)
                sp.dma_start(ring[:, s, :].rearrange("p (b n) -> p b n", b=2),
                             I["win"][2 * q:2 * q + 2].rearrange("b p n -> p b n")).then_inc(cache_full[s], 16)
            sp.wait_ge(S["rope_done"], 4)
            sp.dma_start(O["kv"], PR[:, T_KC:T_DNQ, :]).then_inc(S["stored"], 16)
            for s in range(SLOTS):
                load(s, 19, I["w_in"][T_END // 2 + s])
            sp.wait_ge(S["d_half"], 2)
            for b in range(8):
                r = slice(16 * b, 16 * b + 16)
                sp.dma_start(m_scratch.rearrange("u b i j -> b i u j")[b], Mb[r, :, r]).then_inc(S["m_out"], 16)
            sp.wait_ge(S["m_out"], 16 * 8)
            sp.dma_start(Dm.rearrange("p i j -> p (i j)"), m_scratch.rearrange("u b i j -> (u b) (i j)")).then_inc(S["m_in"], 16)
            sp.wait_ge(S["t_ready"], 1)
            sp.dma_start(t_scratch.rearrange("u b i j -> (u b) (i j)"), Tm.rearrange("p i j -> p (i j)")).then_inc(S["t_out"], 16)
            sp.wait_ge(S["t_out"], 16)
            sp.wait_ge(S["t_zero"], 1)
            for b in range(8):
                r = slice(16 * b, 16 * b + 16)
                sp.dma_start(Tb[r, :, r], t_scratch.rearrange("u b i j -> b i u j")[b]).then_inc(S["t_in"], 16)
            for m in range(2):
                load(m, 20, I["s_delta0"][m])
            load(2, 20, I["w_in"][T_END // 2 + N_MERGE_EARLY])
            load(3, 20, I["w_ada"][N_ADA1])
            sp.wait_ge(S["s2_ready"], 1)
            sp.dma_start(O["p_delta"], Yb).then_inc(S["s2_stored"], 16)
            for m in range(2):
                sp.wait_ge(S["smp_new"], m + 1)
                sp.dma_start(O["s_delta"][m], ring[:, m, :]).then_inc(S["smp_stored"], 16)
            sp.wait_ge(S["s2_stored"], 16)
            sp.wait_ge(S["smp_stored"], 32)
            for m in range(2):
                sp.sem_inc(slot_used[m], 1)
            sp.wait_ge(S["stored"], 16 * 5)
            def load_other_half(i):
                load(0, i + 21, tile_of("w_in", 2 * i + T_END // 2 + N_MERGE_EARLY + 1))
                load(1, i + 21, tile_of("w_ada", 2 * i + N_ADA1 + 1))

            with sp.Fori(0, 5) as i:
                load_other_half(i)
                load(2, i + 21, tile_of("w_in", 2 * i + T_END // 2 + N_MERGE_EARLY + 2))
                load(3, i + 21, tile_of("w_ada", 2 * i + N_ADA1 + 2))
            load_other_half(5)
            for n, (s, use) in enumerate(LAST_ADA):
                load(s, use, I["w_ada"][N_ADA1 + 12 + n])
            with sp.Fori(0, 2) as i:
                for s in range(SLOTS):
                    load(s, i + 28, tile_of("w_br", 4 * i + s))
            for s in range(3):
                load(s, 30, I["w_out"][s])
            sp.wait_ge(slot_used[3], 31)
            sp.dma_start(xT[:], I["x"]).then_inc(S["x_again"], 16)
            load(3, 30, I["w_out"][3])
            for s in range(SLOTS):
                load(s, 31, I["w_out"][4 + s])
            with sp.Fori(0, 2) as i:
                for s in range(SLOTS):
                    load(s, i + 32, tile_of("w_peer_q", 4 * i + s))
            for s in range(2):
                load(s, 34, I["w_peer_u"][s])
            sp.wait_ge(S["pq_evac"], 8)
            sp.dma_start(keys, I["w_keys"]).then_inc(S["keys_in"], 16)
            for s in (2, 3):
                load(s, 34, I["w_peer_u"][s])
            with sp.Fori(0, 2) as i:
                for s in range(SLOTS):
                    load(s, i + 35, tile_of("w_peer_u", 4 * i + s + 4))
            for b, (t0, n) in enumerate(ROUTE_BLOCKS):
                if b == 0:
                    for s in range(SLOTS):
                        load(s, 37, I["w_peer_u"][12 + s])
                    for s in range(2):
                        load(s, 38, I["w_peer_u"][16 + s])
                else:
                    for s in (2, 3):
                        load(s, 38, I["w_peer_u"][16 + s])
                    load(0, 39, I["w_peer_u"][N_EARLY])
                    load(1, 39, I["w_peer_v"][N_EARLY])
                sp.wait_ge(S["route_evac"], (t0 + n) // 4)
                sp.dma_start(route_w[:, :, t0:t0 + n], WS[:, 0:n * P].rearrange("p (i t) -> p i t", t=n)).then_inc(S["route_stored"], 16)
            load(2, 39, I["w_peer_u"][N_EARLY + 1])
            load(3, 39, I["w_peer_v"][N_EARLY + 1])
            sp.wait_ge(S["route_stored"], 16 * len(ROUTE_BLOCKS))

            def load_routing(g, b):
                sp.dma_start(Wb[:, b], route_w[:, bass.ds(2 * g, 2), :]).then_inc(S[f"route_in{b}"], 16)

            for b in range(2):
                load_routing(N_EARLY + b, b)

            def late_values(g, b, use):
                load(2 * b + 1, use, tile_of("w_peer_v", g + N_EARLY))
                sp.wait_ge(S["expert_act"], g - 1)
                load_routing(g + N_EARLY, b)

            load(0, 40, I["w_peer_u"][N_EARLY + 2])
            with sp.Fori(0, N_LATE // 2 - 2) as i:
                for b in range(2):
                    load(2 - 2 * b, i + 40 + b, tile_of("w_peer_u", 2 * i + b + 3 + N_EARLY))
                    late_values(2 * i + b + 2, b, i + 40)
            load(2, V_USE - 1, I["w_peer_u"][N_GROUP - 1])
            late_values(N_LATE - 2, 0, V_USE - 1)
            late_values(N_LATE - 1, 1, V_USE - 1)
            for b in range(2):
                sp.wait_ge(S[f"gelu_stored{b}"], 16 * (N_EARLY // 2 + 1))

            def early_group(s, e, use, free, free_use):
                load(s, use, tile_of("w_peer_v", e))
                sp.wait_ge(slot_used[free], free_use + 2)
                load_routing(e, s % 2)
                sp.dma_start(act_x[:, s % 2], gelu_scratch[bass.ds(e, 1)].rearrange("a p j n -> p (a j) n")).then_inc(S[f"route_in{s % 2}"], 16)

            early_group(0, 0, V_USE, 1, V_USE - 1)
            early_group(1, 1, V_USE, 3, V_USE - 1)
            early_group(2, 2, V_USE, 0, V_USE)
            early_group(3, 3, V_USE, 1, V_USE)
            with sp.Fori(0, N_EARLY // 4 - 1) as i:
                for s in range(SLOTS):
                    early_group(s, 4 * i + s + 4, i + V_USE + 1, (s + 2) % 4, i + V_USE + s // 2)
            sp.wait_ge(S["y_ready"], 1)
            sp.dma_start(O["y"], acc).then_inc(S["stored"], 16)
            sp.wait_ge(S["stored"], 96)

        @block.gpsimd
        def _(pool):
            pool.memset(gateS[:], 0.0).then_inc(S["consts_set"], 1)

            def lo_half(s, part, split):
                for c in (2, 3):
                    r = slice(c * SLOT // 4, (c + 1) * SLOT // 4)
                    pool.wait_ge(S["split_hi"], 4 * (split + 1 + N_DENSE) + c + 1)
                    pool.tensor_tensor(w_lo[:, s, r], ring[:, s, r], w_hi[:, part, r], ALU.subtract).then_inc(S["split_lo2"], 1)

            for q in range(N_DENSE):
                s = q % 4
                for c in (2, 3):
                    r = slice(c * SLOT // 4, (c + 1) * SLOT // 4)
                    pool.wait_ge(S["split_hi"], 4 * q + c + 1)
                    pool.tensor_tensor(w_lo[:, s, r], ring[:, s, r], dense_hi(q % 2, c), ALU.subtract).then_inc(S["split_lo2"], 1)
            lo_half(0, 0, 0)
            lo_half(2, 1, 1)
            with pool.Fori(0, N_LATE // 2 - 1) as i:
                for n, (s, part) in enumerate(((1, 0), (0, 1), (3, 0), (2, 1))):
                    lo_half(s, part, 4 * i + n + 2)
            lo_half(1, 0, 2 * N_LATE - 2)
            lo_half(3, 1, 2 * N_LATE - 1)
            with pool.Fori(0, N_EARLY // 4) as i:
                for s in range(SLOTS):
                    lo_half(s, s % 2, 4 * i + s + 2 * N_LATE)

        @block.tensor
        def _(pe):
            def ada_main(s, use, paged=0):
                pe.wait_ge(slot_full[s], 16 * (use + 1 - paged))
                w = slot_kt(s)
                for k in range(KT):
                    g = 32 * (k % 4)
                    mm = pe.matmul(bank[4 + s % 2][g:g + 32, 0:256], cstat[:, k, :], w[:, k, :],
                                   start=(k < 4), stop=(k >= KT - 4), tile_position=(0, g))
                mm.then_inc(slot_used[s], 1)

            def ada_reduce(s, m):
                pe.wait_ge(S["ada_copied"], m + 1)
                pe.wait_ge(S["ada_done"], m + 1)
                for j in range(2):
                    mm = pe.matmul(bank[6][:, NR * j:NR * j + NR], adaS[:, s % 2, j * P:(j + 1) * P], cst("sumsel"),
                                   start=True, stop=True)
                mm.then_inc(S["ada_reduced"], 1)

            def project(s, use, t, b, paged=0):
                pe.wait_ge(slot_full[s], 16 * (use + 1 - paged))
                w = slot_kt(s)
                for j in range(2):
                    pe.wait_ge(S["proj_evac"], t + j + 1)
                    for k in range(KT):
                        mm = pe.matmul(bank[b + j][:, 0:NT], w[:, k, j * P:(j + 1) * P], hT[:, k, :],
                                       start=(k == 0), stop=(k == KT - 1))
                    mm.then_inc(slot_used[s] if j else S["proj_mm"], 1)

            pe.wait_ge(S["consts_in"], 16 * 6)
            pe.wait_ge(S["consts_set"], 3)
            with pe.Fori(0, N_ADA0 // 4) as i:
                for s in range(4):
                    ada_main(s, i)
                    ada_reduce(s, 4 * i + s)
            for k in range(KT):
                pe.wait_ge(S["x_squared"], k // 4 + 1)
                mm = pe.matmul(bank[7][:, 0:NT], ones[:], hT[:, k, :], start=(k == 0), stop=(k == KT - 1))
            mm.then_inc(S["x_summed"], 1)
            pe.wait_ge(S["h_ready"], 1)
            pe.wait_ge(S["wsmall_in"], 16)
            for k in range(KT):
                mm = pe.matmul(bank[7][0:SM, 0:NT], wsmall[:, k, :], hT[:, k, :], start=(k == 0), stop=(k == KT - 1))
            mm.then_inc(S["small_mm"], 1)
            with pe.Fori(0, 8) as i:
                project(0, i + 4, 4 * i, 0)
                ada_main(1, i + 4)
                project(2, i + 4, 4 * i + 2, 2)
                ada_reduce(1, i + 16)
            with pe.Fori(0, 3) as i:
                project(0, i + 12, 4 * i + 32, 0)
                ada_main(1, i + 12)
                project(2, i + 12, 4 * i + 34, 2)
                ada_reduce(1, 2 * i + 24)
                ada_main(3, i + 12, 8)
                ada_reduce(3, 2 * i + 25)

            def head_sum(n, count):
                pe.wait_ge(S["hn_sq"], n + 1)
                if n >= 2:
                    pe.wait_ge(S["hn_std"], n - 1)
                for t in range(count):
                    mm = pe.matmul(bank[n % 2 * 4 + t][:, 0:NT], ones[:], sq[n % 2][:, t, :], start=True, stop=True)
                mm.then_inc(S["hn_sum"], 1)

            pe.wait_ge(S["ada_done"], N_ADA1 + 1)
            for n, (t0, count, _) in enumerate(NORM_GROUPS):
                head_sum(n, count)
            pe.wait_ge(S["hn_std"], len(NORM_GROUPS))
            for n, (t0, count) in enumerate(ROPE_GROUPS):
                pe.wait_ge(S["hn_done"], len(NORM_GROUPS))
                if n >= 2:
                    pe.wait_ge(S["rope_done"], n - 1)
                for t in range(count):
                    mm = pe.matmul(bank[n % 2 * 4 + t][:, 0:NT], cst("perm"), PR[:, t0 + t, :], start=True, stop=True)
                mm.then_inc(S["rope_rot"], 1)
            pe.wait_ge(S["rope_done"], 4)
            pe.wait_ge(S["cmp_ready"], 1)
            ck = CK[:, 0, :, :, 1:1 + N_CMP].rearrange("p b g n -> p (b g) n")
            for m in range(2):
                pe.matmul(bank[m][:, 0:8 * N_CMP], cst("perm"), ck[:, 8 * m:8 * m + 8, :], start=True, stop=True)
            pe.matmul(bank[2][:, 0:G * N_CMP_P], cst("perm"), CP[:, 0, :, :].rearrange("p g n -> p (g n)"),
                      start=True, stop=True).then_inc(S["cmp_rot"], 1)
            pe.wait_ge(S["cmp_done"], 1)
            for s in range(SLOTS):
                project(s, 15, T_Z + 2 * s, 2 * s, 8 if s == 3 else 0)
            pe.wait_ge(S["proj_evac"], T_END + 4)
            for m, t in enumerate((T_VS, T_VS + 1, T_VW, T_VW + 1)):
                for a in range(2):
                    j = 2 * m + a
                    pe.transpose(bank[4 + j // 4][:, j % 4 * P:(j % 4 + 1) * P], PR[:, t, a * P:(a + 1) * P], ident)
            for g in range(G):
                pe.transpose(bank[6][0:N_CMP_P, g * P:(g + 1) * P], CP[:, 1, g, :], ident)
            pe.wait_ge(S["small_evac"], 3)
            for a in range(2):
                mm = pe.transpose(bank[7][:, 32 * a:32 * a + 3 * H], gates[:, a * P:(a + 1) * P], ident[0:3 * H, 0:3 * H])
            mm.then_inc(S["vt_mm"], 1)
            for m in range(NS * G):
                mm = pe.transpose(bank[m // 4][0:NC0, m % 4 * P:(m % 4 + 1) * P], CK[:, 1, m // G, m % G, :], ident)
            mm.then_inc(S["vt_mm"], 1)

            def unit_scores(u):
                h, a = u // 2, u % 2
                nk, q, b = P * (a + 1), PR[:, h, a * P:(a + 1) * P], u % 2 * 2
                if u == 0:
                    pe.wait_ge(S["vt_evac"], 2)
                else:
                    if u >= 2:
                        pe.wait_ge(S["u_max"], u - 1)
                pe.matmul(bank[b][:, 0:nk], q, PR[:, T_KS + h // REP, 0:nk], start=True, stop=True)
                pe.matmul(bank[b][:, 256:256 + N_CMP_P], q, CP[:, 0, h // REP, :], start=True, stop=True)
                pe.matmul(bank[b + 1][:, 0:nk], q, PR[:, T_KW + h // REP, 0:nk], start=True,
                          stop=True).then_inc(S["u_scores"], 1)

            def unit_turn(u):
                a = u % 2
                pe.wait_ge(S["u_norm"], u + 1)
                if u:
                    pe.wait_ge(S["u_evac"], u)
                for m in range(2):
                    for k in range(a + 1):
                        pe.transpose(bank[4][:, (2 * m + k) * P:(2 * m + k + 1) * P],
                                     SB[u % 3][:, 256 * m + k * P:256 * m + (k + 1) * P], ident)
                pe.transpose(bank[5][0:N_CMP_P, 0:P], SB[u % 3][:, 512:512 + N_CMP_P], ident).then_inc(S["u_turned"], 1)

            def unit_values(u):
                h, a = u // 2, u % 2
                pe.wait_ge(S["u_evac"], u + 1)
                if u >= 2:
                    pe.wait_ge(S["u_out"], u - 1)
                o = bank[6 + u % 2][:, 0:P]
                pe.matmul(o, CVT[:, h // REP, :], PTs[u % 2][0:N_CMP_P, 512:640], start=True, stop=False)
                for m in range(2):
                    for k in range(a + 1):
                        mm = pe.matmul(o, VT[:, (2 * m + h // REP) * 2 + k, :],
                                       PTs[u % 2][:, (2 * m + k) * P:(2 * m + k + 1) * P],
                                       start=False, stop=(m == 1 and k == a))
                mm.then_inc(S["u_mm"], 1)

            unit_scores(0)
            unit_scores(1)
            for u in range(2 * H):
                if u + 2 < 2 * H:
                    unit_scores(u + 2)
                unit_turn(u)
                if u:
                    unit_values(u - 1)
            unit_values(2 * H - 1)

            pe.wait_ge(S["qpad_done"], 1)
            for q in range(4):
                items = [3 * q, 3 * q + 1, 3 * q + 2]
                slots = [n % 4 for n in items]
                if q == 0:
                    pe.wait_ge(S["u_out"], 2 * H)
                else:
                    pe.wait_ge(S["r_out"], q)
                for n in items:
                    before = [m for m in range(n + 1) if m % 4 == n % 4]
                    done = 16 * sum(1 if m % 3 == 2 else PAGES for m in before)
                    pe.wait_ge(cache_full[n % 4], done + (16 * PAGES * 8 if n % 4 == 3 else 0))
                wslot = ring[:, slots[2], :].rearrange("p (b n) -> p b n", b=2)
                for j in range(4):
                    b, g, r = j // G, j % G, slice(32 * j, 32 * j + 32)
                    pair, kw = 4 * q + j, dict(start=True, stop=True, tile_position=(0, 32 * j))
                    qs = qpad[:, pair, :]
                    pe.matmul(bank[0][r, 0:NC0], qs, CK[:, 0, 2 * q + b, g, :], **kw)
                    for m in range(2):
                        pe.matmul(bank[1 + m][r, :], qs, slc_slot[slots[b]][:, 4 * m:4 * m + 4, 0, g * P:(g + 1) * P], **kw)
                    mm = pe.matmul(bank[3][r, :], qs, wslot[:, b, g * WIN:(g + 1) * WIN], **kw)
                mm.then_inc(S["r_scores"], 1)
                pe.wait_ge(S["r_imp"], q + 1)
                pe.matmul(bank[4][:, 0:14], cst("gsum"), impb[:, 0, 0:14], start=True, stop=True).then_inc(S["r_impsum"], 1)
                pe.wait_ge(S["r_norm"], q + 1)
                for a in range(13):
                    lo = (a * P if a < 4 else 512 if a == 4 else NC0 + 512 + (a - 5) * P)
                    n = NC0 if a == 4 else P
                    mm = pe.transpose(bank[4 + a // 4][0:n, a % 4 * P:(a % 4 + 1) * P], SS[:, lo:lo + n], ident)
                mm.then_inc(S["r_turned"], 1)
                pe.wait_ge(S["r_evac"], q + 1)
                for j in range(4):
                    b, g, r = j // G, j % G, slice(32 * j, 32 * j + 32)
                    for a in range(13):
                        n = NC0 if a == 4 else P
                        if a < 4:
                            v = wslot[:, b, G * WIN + a * 256 + g * P:G * WIN + a * 256 + (g + 1) * P]
                        elif a == 4:
                            v = V0[:, 4 * q + j, :]
                        else:
                            v = slc_slot[slots[b]][:, a - 5, 1, g * P:(g + 1) * P]
                        mm = pe.matmul(bank[0][r, 0:P], PTS[0:n, a, 32 * j:32 * j + 32], v, start=(a == 0),
                                       stop=(a == 12), tile_position=(0, 32 * j))
                    if j == 1:
                        mm.then_inc(slot_used[slots[0]], 1)
                    if j == 3:
                        mm.then_inc(slot_used[slots[1]], 1)
                pe.wait_ge(slot_used[slots[1]], 17 + items[1] // 4 + 1)
                pe.nop().then_inc(slot_used[slots[2]], 1)
                pe.wait_ge(S["r_oevac"], q + 1)
                pe.transpose(bank[1][:, 0:P], osb[:], ident).then_inc(S["r_oturned"], 1)

            for n in range(5, 9):
                if n == 5:
                    pe.wait_ge(S["r_out"], 4)
                head_sum(n, 4)
            pe.wait_ge(S["hn_std"], 9)
            pe.wait_ge(S["g_rows"], 1)
            for v, rows in enumerate((rowsG, rowsB)):
                for c in range(2):
                    pe.transpose(bank[0][:, 16 * v + 8 * c:16 * v + 8 * c + 8], rows[:, c * P:(c + 1) * P], ident[0:H, 0:H])
                for h in range(H):
                    mm = pe.matmul(bank[1][:, 64 * v + NS * h:64 * v + NS * (h + 1)], ident[0:H, h:h + 1].broadcast_to((H, P)),
                                   rows[:, SEQ:NT], start=True, stop=True)
            mm.then_inc(S["g_cols"], 1)
            project(0, 19, T_END, 2, PAGED[0])
            pe.wait_ge(S["g_colsc"], 2)
            pe.wait_ge(S["proj_evac"], T_END + 6)
            pe.wait_ge(S["hn_done"], 9)
            for hb in range(2):
                if hb:
                    pe.wait_ge(S["d_half"], 1)
                for a in range(4):
                    mm = pe.matmul(bank[4 + a][:, 0:SEQ], ident[0:H, 4 * hb + a:4 * hb + a + 1].broadcast_to((H, P)),
                                   rowsG[:, 0:SEQ], start=True, stop=True)
                mm.then_inc(S["g_bcast"], 1)
                for v, tile in ((0, T_DNK), (2, T_DNQ)):
                    for a in range(8):
                        h, r = 4 * hb + a // 2, slice(a % 2 * P, (a % 2 + 1) * P)
                        mm = pe.matmul(bank[v + a // 4][:, a % 4 * P:(a % 4 + 1) * P], PR[:, T_DNK + h, r], PR[:, tile + h, r],
                                       start=True, stop=True)
                mm.then_inc(S["kk_mm"], 1)
            pe.wait_ge(S["d_half"], 2)
            project(1, 19, T_END + 2, 0, PAGED[1])

            def project_part(s, t, part):
                if part == 0:
                    pe.wait_ge(slot_full[s], 16 * (20 - PAGED[s]))
                    pe.wait_ge(S["proj_evac"], t + 4)
                for n in range(part * 2 * KT // 6, (part + 1) * 2 * KT // 6):
                    j, k = n // KT, n % KT
                    mm = pe.matmul(bank[6 + j][:, 0:NT], slot_kt(s)[:, k, j * P:(j + 1) * P], hT[:, k, :], start=(k == 0), stop=(k == KT - 1))
                    if k == KT - 1:
                        mm.then_inc(slot_used[s] if j else S["proj_mm"], 1)

            pe.wait_ge(S["t_in"], 16 * 8)
            pe.wait_ge(S["proj_evac"], T_END + 8)
            for u in range(NU):
                mm = pe.transpose(bank[u // 4][:, u % 4 * P:(u % 4 + 1) * P], Tb[:, u, :], ident)
            mm.then_inc(S["t_mm"], 1)
            pe.wait_ge(S["t_evac"], 1)
            for n in range(6):
                level, half = n // 2, n % 2
                pe.wait_ge(S["lv_c"], n + 1)
                if n:
                    pe.wait_ge(S["lv_ye"], n)
                for a in range(8):
                    mm = pe.matmul(bank[a // 4][:, a % 4 * P:(a % 4 + 1) * P], Cb[:, a, :], Ub[:, 8 * half + a, :],
                                   start=True, stop=True)
                mm.then_inc(S["lv_y"], 1)
                s, part = 2 + n // 3, n % 3 * 2
                project_part(s, T_END + 2 * s, part)
                pe.wait_ge(S["lv_ye"], n + 1)
                if n >= 2:
                    pe.wait_ge(S["lv_te"], n - 1)
                for a in range(8):
                    mm = pe.matmul(bank[2 + a // 4][:, a % 4 * P:(a % 4 + 1) * P], Tb[:, 8 * half + a, :], Yb[:, a, :],
                                   start=True, stop=True)
                mm.then_inc(S["lv_z"], 1)
                project_part(s, T_END + 2 * s, part + 1)
                pe.wait_ge(S["lv_u"], n + 1)
                if level < 2:
                    for a in range(8):
                        mm = pe.transpose(bank[4 + a // 4][:, a % 4 * P:(a % 4 + 1) * P], Ub[:, 8 * half + a, :], ident)
                    mm.then_inc(S["lv_t"], 1)
            for v, tile in enumerate((T_DNV, T_DNK)):
                if v:
                    pe.wait_ge(S["bv_ready"], 1)
                else:
                    pe.wait_ge(S["lv_te"], 4)
                for u in range(NU):
                    mm = pe.transpose(bank[u // 4][:, u % 4 * P:(u % 4 + 1) * P], PR[:, tile + u // 2, u % 2 * P:(u % 2 + 1) * P], ident)
                mm.then_inc(S["vk_tok"], 1)
            pe.wait_ge(S["kd_ready"], 1)
            quarter = lambda base, h: bank[base + h // 4][:, h % 4 * P:(h % 4 + 1) * P]
            for h in range(H):
                mm = pe.matmul(quarter(0, h), Ub[:, 2 * h, :], Tb[:, 2 * h, :], start=True, stop=True)
            mm.then_inc(S["vn_mm"], 1)
            pe.wait_ge(S["vn_evac"], 1)
            for h in range(H):
                mm = pe.matmul(quarter(4, h), Mb[:, 2 * h, :], VN[:, h, :], start=True, stop=True)
            mm.then_inc(S["s1_mm"], 1)
            for h in range(H):
                mm = pe.matmul(quarter(2, h), VN[:, h, :], Ab[:, 2 * h, :], start=True, stop=True)
            mm.then_inc(S["o_mm"], 1)
            pe.wait_ge(S["s1_evac"], 1)
            pe.wait_ge(S["proj_evac"], T_END + 2 * N_MERGE_EARLY + 4)
            for h in range(H):
                mm = pe.matmul(quarter(6, h), PR[:, T_DNK + h, P:SEQ], S1[:, h, :], start=True, stop=True)
            mm.then_inc(S["zs_mm"], 1)
            for h in range(H):
                mm = pe.matmul(quarter(4, h), ident[0:H, h:h + 1].broadcast_to((H, P)), rowsG[:, P:SEQ], start=True, stop=True)
            mm.then_inc(S["qe_mm"], 1)
            pe.wait_ge(S["rhs_ready"], 1)
            for h in range(H):
                mm = pe.matmul(quarter(0, h), Ub[:, 2 * h + 1, :], Yb[:, h, :], start=True, stop=True)
            mm.then_inc(S["vn_mm"], 1)
            pe.wait_ge(S["vn_evac"], 2)
            pe.wait_ge(S["qe_ready"], 1)
            pe.wait_ge(S["o_evac"], 1)
            for h in range(H):
                pe.matmul(quarter(2, h), S1[:, h, :], Cb[:, h, :], start=True, stop=False)
                mm = pe.matmul(quarter(2, h), VN[:, h, :], Ab[:, 2 * h + 1, :], start=False, stop=True)
            mm.then_inc(S["o_mm"], 1)
            for h in range(H):
                mm = pe.matmul(quarter(6, h), Mb[:, 2 * h + 1, :], VN[:, h, :], start=True, stop=True)
            mm.then_inc(S["s2_mm"], 1)
            pe.wait_ge(S["smp_kq"], 1)
            for m in range(64):
                if m % 32 == 0:
                    pe.wait_ge(slot_full[m // 32], 16 * 18)
                mm = pe.matmul(bank[0][:, 2 * m:2 * m + 2], ring[:, m // 32, m % 32 * P:(m % 32 + 1) * P], kq[:, m, :],
                               start=True, stop=True)
            mm.then_inc(S["smp_mm"], 1)
            pe.wait_ge(S["smp_kq"], 2)
            pe.matmul(bank[1][:, 0:64], ones[:], smp["prod"], start=True, stop=True).then_inc(S["smp_mm"], 1)
            pe.wait_ge(S["smp_vn"], 1)
            pe.wait_ge(S["o_evac"], 2)
            pe.wait_ge(S["smp_evac"], 2)
            pe.transpose(bank[1][0:64, 0:P], smp["kc"], ident)
            pe.transpose(bank[1][0:64, P:2 * P], smp["vn"], ident).then_inc(S["smp_mm"], 1)
            project(2, 20, T_END + 8, 2, PAGED[2])
            pe.wait_ge(S["s2_ready"], 1)
            for n in range(8):
                pe.wait_ge(S["smp_diag"], n + 1)
                b = 4 + n % 2 * 2
                for m in range(2):
                    mm = pe.matmul(bank[b + m], ktok, vdiag[:, 4 * m:4 * m + 4, :].rearrange("p m n -> p (m n)"), start=True, stop=True)
                mm.then_inc(S["smp_outer"], 1)
            for n in (9, 10):
                if n == 9:
                    pe.wait_ge(S["smp_new"], 2)
                head_sum(n, 4)

            pe.wait_ge(S["hn_std"], 11)
            def other_half(i):
                ada_main(3, i + 20, PAGED[3])
                project(0, i + 21, 4 * i + T_END + 10, 0, PAGED[0])
                ada_reduce(3, 2 * i + N_ADA1)
                ada_main(1, i + 21, PAGED[1])

            with pe.Fori(0, 5) as i:
                other_half(i)
                project(2, i + 21, 4 * i + T_END + 12, 2, PAGED[2])
                ada_reduce(1, 2 * i + N_ADA1 + 1)
            other_half(5)
            ada_reduce(1, N_ADA1 + 11)
            for n, (s, use) in enumerate(LAST_ADA):
                ada_main(s, use, PAGED[s])
                ada_reduce(s, N_ADA1 + 12 + n)
            pe.wait_ge(S["proj_evac"], T_END + N_MERGE + 4)
            pe.wait_ge(S["ada_done"], 49)
            pe.wait_ge(S["dn_out"], 1)
            def three_pass(out, w, w_top, x, x_top, start, stop):
                pe.matmul(out, w_top, x_top, start=start, stop=False)
                pe.matmul(out, w, x_top, start=False, stop=False)
                return pe.matmul(out, w_top, x, start=False, stop=stop)

            def dense_tile(q, k, j):
                top = dense_hi(q % 2, k // 4)[:, k % 4 * 256 + j * P:k % 4 * 256 + (j + 1) * P]
                return w_lo[:, q % 4, k * 256 + j * P:k * 256 + (j + 1) * P], top

            def split_done(q):
                pe.wait_ge(S["split_lo"], 2 * q + 2)
                pe.wait_ge(S["split_lo2"], 2 * q + 2)

            pe.wait_ge(S["o_split"], 4)
            for n in range(8):
                b = n % 2 * 4
                split_done(n)
                if n >= 2:
                    pe.wait_ge(S["br_done"], n - 1)
                for j in range(2):
                    for k in range(2 * H):
                        o = pr_lo[:, k if k < H else T_DNV + k - H, :]
                        mm = three_pass(bank[b + 2 * (k // H) + j][:, 0:NT], *dense_tile(n, k, j), o, o_hi[:, k, :], k % H == 0, k % H == H - 1)
                mm.then_inc(slot_used[n % 4], 1)
            pe.wait_ge(S["br_done"], 8)

            def dense(q, free, x, x_top):
                s = q % 4
                split_done(q)
                if q % 8 >= 4:
                    pe.wait_ge(S[free], q % 8 - 3)
                for j in range(2):
                    for k in range(KT):
                        mm = three_pass(bank[2 * s + j][:, 0:NT], *dense_tile(q, k, j), x[:, k, :], x_top[:, k, :], k == 0, k == KT - 1)
                mm.then_inc(slot_used[s], 1)

            for n in range(8):
                dense(8 + n, "x1_done", h2_lo, mixed_hi)
            pe.wait_ge(S["x1_done"], 8)
            for k in range(KT):
                pe.wait_ge(S["x_squared"], 4 + k // 4 + 1)
                mm = pe.matmul(bank[7][:, 0:NT], ones[:], x1sq[:, k, :], start=(k == 0), stop=(k == KT - 1))
            mm.then_inc(S["x_summed"], 1)

            pe.wait_ge(S["o_split"], 8)
            for n in range(8):
                dense(16 + n, "pq_evac", hq_lo, hq_hi)

            def scores(a):
                t0, n = TOKEN_TILES[a]
                if a:
                    pe.wait_ge(S["scores_in"], a)
                for t in range(16):
                    mm = pe.matmul(bank[4 + t // 4][0:n, t % 4 * P:(t % 4 + 1) * P], PR[:, t, t0:t0 + n], keys[:, t, :],
                                   start=True, stop=True)
                mm.then_inc(S["key_mm"], 1)

            def turn(a):
                n = TOKEN_TILES[a][1]
                pe.wait_ge(S["chosen"], a + 1)
                if a:
                    pe.wait_ge(S["chosen_evac"], a)
                for v in range(3):
                    mm = pe.transpose(bank[7][:, v * P:v * P + n], chosen[0:n, v, :], ident[0:n, 0:n])
                mm.then_inc(S["chosen_turned"], 1)

            def early_scores(s, use, e, beside=lambda k: None):
                b = s % 2 * 2
                pe.wait_ge(slot_full[s], 16 * (use + 1 - PAGED[s]))
                pe.wait_ge(S["gelu_early"], e + 1)
                for j in range(2):
                    for k in range(KT):
                        if k % 4 == 0:
                            beside(4 * j + k // 4)
                        mm = pe.matmul(bank[b + j][:, 0:NT], slot_kt(s)[:, k, j * P:(j + 1) * P], hT[:, k, :],
                                       start=(k == 0), stop=(k == KT - 1))
                mm.then_inc(slot_used[s], 1)

            pe.wait_ge(S["pq_evac"], 8)
            for n in range(3):
                for s in range(SLOTS):
                    early_scores(s, 34 + n, 4 * n + s)
                    if n == 0 and s == 0:
                        pe.wait_ge(S["keys_in"], 16)
                        for a in range(3):
                            scores(a)
                        pe.wait_ge(S["scores_in"], 3)
                turn(n)
            pe.wait_ge(S["chosen_evac"], 3)

            def route(m):
                for b in range(2):
                    pe.wait_ge(S["onehot"], 2 * m + b + 1)
                    pe.wait_ge(S["route_free"], 2 * m + b + 1)
                    for t in range(4):
                        mm = pe.matmul(bank[4 + b][:, t * P:(t + 1) * P], O2[:, b, t, :], O1[:, b, t, :], start=True, stop=True)
                    mm.then_inc(S["route_mm"], 1)

            route(0)
            with pe.Fori(0, 2) as i:
                for s in range(2):
                    early_scores(s, i + 37, 4 * i + s + 12, lambda k: route(16 * i + 8 * s + k + 1))
                for s in (2, 3):
                    early_scores(s, i + 37, 4 * i + s + 12)

            def expert_scores(b, part, split, g):
                pe.wait_ge(S["split_lo"], 2 * (split + N_DENSE) + 6)
                pe.wait_ge(S["split_lo2"], 2 * (split + N_DENSE) + 2)
                pe.wait_ge(S["expert_gelu"], g + 1)
                top, rest = (ap.rearrange("p (k n) -> p k n", k=KT) for ap in (w_hi[:, part], w_lo[:, 2 * b]))
                for j in range(2):
                    for k in range(KT):
                        c = slice(j * P, (j + 1) * P)
                        mm = three_pass(bank[2 * b + j][:, 0:NT], rest[:, k, c], top[:, k, c], h2_lo[:, k, :], h2_hi[:, k, :],
                                        k == 0, k == KT - 1)
                mm.then_inc(slot_used[2 * b], 1)

            def expert_values(b, s, part, split, g):
                pe.wait_ge(S["split_lo"], 2 * (split + N_DENSE) + 6)
                pe.wait_ge(S["split_lo2"], 2 * (split + N_DENSE) + 2)
                pe.wait_ge(S["expert_act"], g + 1)
                for d in range(KT):
                    if d % 2 == 0:
                        pe.wait_ge(S["acc_added"], 8 * g + d // 2 + 1)
                    for j in range(2):
                        c = slice(j * D + d * P, j * D + (d + 1) * P)
                        mm = three_pass(bank[4 + d % 4][:, 0:NT], w_lo[:, s, c], w_hi[:, part, c], act_lo[:, b, j, :], act_hi[:, b, j, :],
                                        j == 0, j == 1)
                    if d % 2 == 1:
                        mm.then_inc(slot_used[s] if d == KT - 1 else S["acc_mm"], 1)

            pe.wait_ge(S["gelu_early"], N_EARLY + 2)
            expert_scores(0, 0, 0, 0)
            expert_scores(1, 1, 1, 1)
            with pe.Fori(0, N_LATE // 2 - 1) as i:
                for m in range(2):
                    expert_values(m, 2 * m + 1, 0, 4 * i + 2 * m + 2, 2 * i + m)
                    expert_scores(m, 1, 4 * i + 2 * m + 3, 2 * i + m + 2)
            expert_values(0, 1, 0, 2 * N_LATE - 2, N_LATE - 2)
            expert_values(1, 3, 1, 2 * N_LATE - 1, N_LATE - 1)
            with pe.Fori(0, N_EARLY // 4) as i:
                for s in range(SLOTS):
                    expert_values(s % 2, s, s % 2, 4 * i + s + 2 * N_LATE, 4 * i + s + N_LATE)

        @block.scalar
        def _(act):
            act.sem_inc(S["proj_evac"], 4)
            act.sem_inc(S["conv_silu"], 4)
            for s in range(SLOTS):
                act.sem_inc(slot_used[s], 1)
            act.wait_ge(S["consts_in"], 16 * 6)
            for k in range(0, KT, 4):
                act.activation(hT[:, k:k + 4, :], xT[:, k:k + 4, :], ACT.Square).then_inc(S["x_squared"], 1)

            def ada_copy(s, use):
                act.wait_ge(slot_used[s], use + 2)
                act.activation(adaS[:, s % 2, :], bank[4 + s % 2][:, 0:256], ACT.Copy).then_inc(S["ada_copied"], 1)

            def evacuate(s, use, t, n, b, func=ACT.Copy):
                act.wait_ge(S["proj_mm"], n + 1)
                act.activation(PR[:, bass.ds(t, 1), :], bank[b][:, 0:NT], func).then_inc(S["proj_evac"], 1)
                act.wait_ge(slot_used[s], use + 2)
                act.activation(PR[:, bass.ds(t + 1, 1), :], bank[b + 1][:, 0:NT], func).then_inc(S["proj_evac"], 1)

            with act.Fori(0, N_ADA0 // 4) as i:
                for s in range(4):
                    ada_copy(s, i)
            act.wait_ge(S["x_summed"], 1)
            act.wait_ge(S["consts_set"], 3)
            act.activation(rstd[:], bank[7][:, 0:NT], ACT.Sqrt, bias=epst[:], scale=1.0 / D).then_inc(S["x_std"], 1)
            act.wait_ge(S["small_mm"], 1)
            act.activation(rowsG[:], bank[7][SM_A:SM_A + H, 0:NT], ACT.Copy).then_inc(S["small_evac"], 1)
            act.activation(rowsB[:], bank[7][SM_B:SM_B + H, 0:NT], ACT.Sigmoid).then_inc(S["small_evac"], 1)
            act.activation(gates[:], bank[7][SM_G:SM_G + 3 * H, 0:NT], ACT.Sigmoid).then_inc(S["small_evac"], 1)
            with act.Fori(0, 8) as i:
                evacuate(0, i + 4, 4 * i, 2 * i, 0)
                ada_copy(1, i + 4)
                evacuate(2, i + 4, 4 * i + 2, 2 * i + 1, 2)
            with act.Fori(0, 3) as i:
                evacuate(0, i + 12, 4 * i + 32, 2 * i + 16, 0)
                ada_copy(1, i + 12)
                evacuate(2, i + 12, 4 * i + 34, 2 * i + 17, 2)
                ada_copy(3, i + 12)

            def head_square(n, t0, count):
                if n >= 2:
                    act.wait_ge(S["hn_sum"], n - 1)
                act.activation(sq[n % 2][:, 0:count, :], PR[:, t0:t0 + count, :], ACT.Square).then_inc(S["hn_sq"], 1)

            def head_std(n, count, scale):
                act.wait_ge(S["hn_sum"], n + 1)
                if n >= 2:
                    act.wait_ge(S["hn_done"], n - 1)
                act.activation(rs[n % 2][:, 0:count, :], psum[:, n % 2 * 4:n % 2 * 4 + count, 0:NT], ACT.Sqrt,
                               bias=epst[:], scale=scale).then_inc(S["hn_std"], 1)

            act.wait_ge(S["proj_evac"], T_Z + 4)
            act.wait_ge(S["small_mm"], 1)
            for n, (t0, count, _) in enumerate(NORM_GROUPS):
                head_square(n, t0, count)
                if n:
                    head_std(n - 1, NORM_GROUPS[n - 1][1], 1.0 / P)
            head_std(len(NORM_GROUPS) - 1, NORM_GROUPS[-1][1], 1.0 / P)
            act.activation(hist[:, :, 3, :], PR[:, T_DNQ:T_Z, SEQ:NT], ACT.Copy).then_inc(S["hist_new"], 1)
            act.activation(praw[:], PR[:, T_DNQ:T_Z, SEQ - 3:SEQ], ACT.Copy).then_inc(S["raw_saved"], 1)
            act.wait_ge(S["hist_new"], 1)
            act.wait_ge(S["raw_saved"], 1)
            with act.Fori(0, DNT // 4) as i:
                for b in range(4):
                    act.wait_ge(S["conv_done"], 4 * i + b + 1)
                    act.activation(PR[:, bass.ds(T_DNQ + 4 * i + b, 1), 0:SEQ], convt[:, b:b + 1, 0:SEQ],
                                   ACT.Silu).then_inc(S["conv_silu"], 1)
            act.wait_ge(S["conv_done"], DNT + 1)
            act.activation(PR[:, T_DNQ:T_Z, SEQ:NT], convs, ACT.Silu).then_inc(S["conv_silu"], 1)
            for s in range(SLOTS):
                evacuate(s, 15, T_Z + 2 * s, T_Z // 2 + s, 2 * s)
            act.wait_ge(S["conv_silu"], DNT + 5)
            act.wait_ge(S["vt_mm"], 1)
            act.activation(VT.rearrange("p (a c) d -> p a (c d)", a=2), psum[:, 4:6, :], ACT.Copy)
            act.activation(CVT.rearrange("p g d -> p (g d)"), bank[6][0:N_CMP_P, 0:G * P], ACT.Copy)
            act.activation(GT[:], bank[7][:, 0:64].rearrange("p (a c) -> p a c", a=2)[:, :, 0:3 * H],
                           ACT.Copy).then_inc(S["vt_evac"], 1)
            act.wait_ge(S["vt_mm"], 2)
            act.activation(V0.rearrange("p (a c) d -> p a (c d)", a=4), psum[0:NC0, 0:4, :], ACT.Copy).then_inc(S["vt_evac"], 1)

            def unit_exp(u):
                n = P * (u % 2 + 1)
                act.wait_ge(S["u_max"], u + 1)
                for m, (lo, w) in enumerate(((512, N_CMP_P), (0, n), (256, n))):
                    e = act.activation(SB[u % 3][:, lo:lo + w], SB[u % 3][:, lo:lo + w], ACT.Exp,
                                       bias=sm1[:, u % 2, 0, m:m + 1], scale=SCALE, accum_out=sm1[:, u % 2, 1, m:m + 1])
                e.then_inc(S["u_exp"], 1)

            def unit_out(u):
                h, a = u // 2, u % 2
                act.wait_ge(S["u_mm"], u + 1)
                act.activation(PR[:, h, a * P:(a + 1) * P], bank[6 + u % 2][:, 0:P], ACT.Copy).then_inc(S["u_out"], 1)

            unit_exp(0)
            for u in range(2 * H):
                if u + 1 < 2 * H:
                    unit_exp(u + 1)
                act.wait_ge(S["u_turned"], u + 1)
                if u >= 2:
                    act.wait_ge(S["u_mm"], u - 1)
                n = P * (u % 2 + 1)
                act.activation(PTs[u % 2][:, 0:512].rearrange("p (m n) -> p m n", m=2)[:, :, 0:n],
                               bank[4].rearrange("p (m n) -> p m n", m=2)[:, :, 0:n], ACT.Copy)
                act.activation(PTs[u % 2][0:N_CMP_P, 512:640], bank[5][0:N_CMP_P, 0:P], ACT.Copy).then_inc(S["u_evac"], 1)
                if u:
                    unit_out(u - 1)
            unit_out(2 * H - 1)

            for q in range(4):
                act.wait_ge(S["r_cmpmax"], q + 1)
                act.activation(SS[:, 513:576], SS[:, 513:576], ACT.Exp, bias=smS[:, 0, 0:1], scale=SCALE,
                               accum_out=smS[:, 1, 0:1]).then_inc(S["r_cmpexp"], 1)
                act.wait_ge(S["r_max"], q + 1)
                for m, (lo, hi) in ((1, (576, 1601)), (2, (0, 513))):
                    e = act.activation(SS[:, lo:hi], SS[:, lo:hi], ACT.Exp, bias=smS[:, 0, m:m + 1], scale=SCALE,
                                       accum_out=smS[:, 1, m:m + 1])
                e.then_inc(S["r_exp"], 1)
                act.wait_ge(S["r_turned"], q + 1)
                act.activation(PTS[:, 0:4, :].rearrange("p a d -> p (a d)"), bank[4], ACT.Copy)
                act.activation(PTS[0:NC0, 4, :], bank[5][0:NC0, 0:P], ACT.Copy)
                act.activation(PTS[:, 5:8, :].rearrange("p a d -> p (a d)"), bank[5][:, P:512], ACT.Copy)
                act.activation(PTS[:, 8:12, :].rearrange("p a d -> p (a d)"), bank[6], ACT.Copy)
                act.activation(PTS[:, 12, :], bank[7][:, 0:P], ACT.Copy).then_inc(S["r_evac"], 1)
                act.wait_ge(slot_used[(3 * q + 1) % 4], 17 + (3 * q + 1) // 4 + 1)
                act.activation(osb[:], bank[0][:, 0:P], ACT.Copy).then_inc(S["r_oevac"], 1)
                act.wait_ge(S["r_oturned"], q + 1)
                for b in range(2):
                    o = bank[1][:, 0:P].rearrange("p (b g r) -> p b g r", b=2, g=G)[:, b, :, 0:REP]
                    e = act.activation(PR[:, 0:H, SEQ + 2 * q + b].rearrange("p (g r) -> p g r", g=G), o, ACT.Copy)
                e.then_inc(S["r_out"], 1)

            act.wait_ge(S["g_parts"], 1)
            act.activation(rows2[:, 1, :], rows2[:, 1, :], ACT.Exp).then_inc(S["act_step"], 1)
            act.activation(alog[:], par("alog")[0:H, :], ACT.Exp)
            act.wait_ge(S["act_step"], 1)
            act.activation(rows2[:, 1, :], rows2[:, 1, :], ACT.Ln, bias=ones[0:H, 0:1]).then_inc(S["g_soft"], 1)
            for n in range(5, 9):
                head_square(n, T_DNQ + 4 * (n - 5), 4)
                if n > 5:
                    head_std(n - 1, 4, 1.0)
            head_std(8, 4, 1.0)
            act.activation(PR[:, T_Z:T_END, :], PR[:, T_Z:T_END, :], ACT.Silu).then_inc(S["z_silu"], 1)
            act.wait_ge(S["g_cols"], 1)
            act.activation(cols[:].rearrange("p v h c -> p v c h"), bank[0][:, 0:32].rearrange("p (v c h) -> p v c h", v=2, c=2),
                           ACT.Copy).then_inc(S["g_colsc"], 1)
            act.activation(smp_g[:], bank[1][:, 0:P], ACT.Copy).then_inc(S["g_colsc"], 1)
            act.wait_ge(S["stored"], 16 * 5)
            evacuate(0, 19, H, T_END // 2, 2, ACT.Sigmoid)
            for hb in range(2):
                act.wait_ge(S["d_diff"], hb + 1)
                act.activation(Cb, Cb, ACT.Exp)
                act.activation(Yb, Yb, ACT.Exp, scale=-1.0).then_inc(S["d_exp"], 1)
            act.wait_ge(S["kdec_diff"], 1)
            act.activation(kdec[:], kdec[:], ACT.Exp)
            act.activation(bge[:], cols[:, 0, :, 1], ACT.Exp)
            act.activation(egl[:], glast[:, :, 1], ACT.Exp).then_inc(S["kdec_exp"], 1)
            evacuate(1, 19, H + 2, T_END // 2 + 1, 0, ACT.Sigmoid)
            act.wait_ge(S["t_mm"], 1)
            flat = lambda ap: ap.rearrange("p (a u) n -> p a (u n)", u=4)
            act.activation(flat(Ub), psum[:, 0:4, :], ACT.Copy).then_inc(S["t_evac"], 1)
            for n in range(6):
                act.wait_ge(S["lv_y"], n + 1)
                if n:
                    act.wait_ge(S["lv_z"], n)
                act.activation(flat(Yb), psum[:, 0:2, :], ACT.Copy).then_inc(S["lv_ye"], 1)
                if n < 4:
                    act.wait_ge(S["lv_t"], n + 1)
                    act.activation(flat(Tb[:, n % 2 * 8:n % 2 * 8 + 8, :]), psum[:, 4:6, :], ACT.Copy).then_inc(S["lv_te"], 1)
                if n % 3 == 2:
                    s = 2 + n // 3
                    evacuate(s, 19, H + 2 * s, T_END // 2 + s, 6, ACT.Sigmoid)
            act.wait_ge(S["vn_mm"], 1)
            act.activation(flat(VN), psum[:, 0:2, :], ACT.Copy).then_inc(S["vn_evac"], 1)
            act.wait_ge(S["s1_mm"], 1)
            act.activation(flat(S1), psum[:, 4:6, :], ACT.Copy).then_inc(S["s1_evac"], 1)
            act.wait_ge(S["o_mm"], 1)
            act.activation(PR[:, T_DNV:T_Z, 0:P], psum[:, 2:4, :].rearrange("p a (u n) -> p (a u) n", u=4), ACT.Copy).then_inc(S["o_evac"], 1)
            act.wait_ge(S["qe_mm"], 1)
            act.activation(flat(Cb), psum[:, 4:6, :], ACT.Exp).then_inc(S["qe_exp"], 1)
            act.wait_ge(S["vn_mm"], 2)
            act.activation(flat(VN), psum[:, 0:2, :], ACT.Copy).then_inc(S["vn_evac"], 1)
            act.wait_ge(S["o_mm"], 2)
            act.activation(PR[:, T_DNV:T_Z, P:SEQ], psum[:, 2:4, :].rearrange("p a (u n) -> p (a u) n", u=4), ACT.Copy).then_inc(S["o_evac"], 1)
            act.activation(smp["eg"], smp_g[:, 0:64], ACT.Exp).then_inc(S["smp_rows"], 1)
            act.wait_ge(S["smp_mm"], 1)
            act.activation(sks.rearrange("p m c -> p (m c)"), bank[0][:, 0:P], ACT.Copy).then_inc(S["smp_evac"], 1)
            act.wait_ge(S["smp_mm"], 2)
            act.activation(smp["qk"], bank[1][:, 0:64], ACT.Copy).then_inc(S["smp_evac"], 1)
            act.wait_ge(S["smp_mm"], 3)
            act.activation(ktok, bank[1][0:64, 0:P], ACT.Copy)
            act.activation(vtok, bank[1][0:64, P:2 * P], ACT.Copy).then_inc(S["smp_evac"], 1)
            evacuate(2, 20, H + 8, T_END // 2 + 4, 2, ACT.Sigmoid)
            act.wait_ge(S["smp_new"], 2)
            for n in (9, 10):
                head_square(n, T_DNV + 4 * (n - 9), 4)
            for n in (9, 10):
                head_std(n, 4, 1.0 / P)
            act.wait_ge(S["dn_out"], 1)
            for k in range(0, 2 * H, 4):
                t = k if k < H else T_DNV + k - H
                act.activation(o_hi[:, k:k + 4, :], PR[:, t:t + 4, :], ACT.Copy).then_inc(S["o_top"], 1)

            def take_other_half(i, t):
                ada_copy(3, i + 20)
                evacuate(0, i + 21, t, 2 * i + T_END // 2 + 5, 0, ACT.Sigmoid)
                ada_copy(1, i + 21)

            with act.Fori(0, 4) as i:
                take_other_half(i, 4 * i + H + 10)
                evacuate(2, i + 21, 4 * i + H + 12, 2 * i + T_END // 2 + 6, 2, ACT.Sigmoid)
            take_other_half(4, H + 26)
            evacuate(2, 25, T_Z, T_END // 2 + 14, 2, ACT.Sigmoid)
            take_other_half(5, T_Z + 2)
            for s, use in LAST_ADA:
                ada_copy(s, use)

            def dense_top(q):
                s = q % 4
                act.wait_ge(slot_full[s], 16 * (28 + q // 4 + 1 - PAGED[s]))
                if q >= 2:
                    act.wait_ge(slot_used[(s + 2) % 4], 28 + (q - 2) // 4 + 2)
                for c in range(4):
                    act.activation(dense_hi(q % 2, c), ring[:, s, c * SLOT // 4:(c + 1) * SLOT // 4], ACT.Copy).then_inc(S["split_hi"], 1)

            def x1_square(k):
                act.wait_ge(S["x1_done"], k // 2 + 2)
                act.activation(x1sq[:, k:k + 4, :], xT[:, k:k + 4, :], ACT.Square).then_inc(S["x_squared"], 1)

            for q in range(12):
                dense_top(q)
            x1_square(0)
            dense_top(12)
            dense_top(13)
            x1_square(4)
            dense_top(14)
            dense_top(15)
            x1_square(8)
            dense_top(16)
            x1_square(12)
            dense_top(17)
            act.wait_ge(S["x_summed"], 2)
            act.activation(rstd[:], bank[7][:, 0:NT], ACT.Sqrt, bias=epst[:], scale=1.0 / D).then_inc(S["x_std"], 1)
            act.wait_ge(S["h_ready"], 2)
            for k in range(0, KT, 4):
                act.activation(hq_hi[:, k:k + 4, :], hT[:, k:k + 4, :], ACT.Copy).then_inc(S["o_top"], 1)
            act.sem_inc(S["expert_gelu"], 2)
            act.sem_inc(S["gelu_early"], 2)
            act.sem_inc(S["route_free"], 2)
            for n in range(8):
                s = n % 4
                act.wait_ge(slot_used[s], 32 + n // 4 + 2)
                act.activation(PR[:, 2 * n:2 * n + 2, :], psum[:, 2 * s:2 * s + 2, 0:NT], ACT.Copy).then_inc(S["pq_evac"], 1)
                if n < 6:
                    dense_top(18 + n)

            def take_scores(a):
                n = TOKEN_TILES[a][1]
                act.wait_ge(S["key_mm"], a + 1)
                act.activation(SC[0:n, a].rearrange("p (c n) -> p c n", c=4), psum[0:n, 4:8, :],
                               ACT.Copy).then_inc(S["scores_in"], 1)

            def softmax_exp(a):
                n = TOKEN_TILES[a][1]
                act.wait_ge(S["best_sub"], a + 1)
                act.activation(chosen[0:n, 2, :], chosen[0:n, 2, :], ACT.Exp).then_inc(S["best_exp"], 1)

            def take_chosen(a):
                t0, n = TOKEN_TILES[a]
                act.wait_ge(S["chosen_turned"], a + 1)
                act.activation(IT[:, :, t0:t0 + n], bank[7][:, 0:3 * P].rearrange("p (v n) -> p v n", v=3)[:, :, 0:n],
                               ACT.Copy).then_inc(S["chosen_evac"], 1)

            def early_gelu(s, use, e):
                act.wait_ge(slot_used[s], use + 2)
                act.wait_ge(S[f"gelu_stored{s % 2}"], 16 * (e // 2 + 1))
                act.activation(early_x[:, s % 2], psum[:, s % 2 * 2:s % 2 * 2 + 2, 0:NT], ACT.Gelu_apprx_tanh).then_inc(S["gelu_early"], 1)
                act.wait_ge(S["gelu_early"], e + 3)
                act.dma_start(gelu_scratch[bass.ds(e, 1)].rearrange("a p j n -> p (a j) n"), early_x[:, s % 2]).then_inc(S[f"gelu_stored{s % 2}"], 16)

            for b in range(2):
                act.sem_inc(S[f"gelu_stored{b}"], 16)
            for a in range(3):
                for s in range(SLOTS):
                    early_gelu(s, 34 + a, 4 * a + s)
                    if a == 0 and s == 0:
                        for b in range(3):
                            take_scores(b)
                    if s == 2:
                        softmax_exp(a)
                take_chosen(a)
            for b, (t0, n) in enumerate(ROUTE_BLOCKS):
                out = WS[:, 0:n * P].rearrange("p (i t) -> p t i", t=n)
                m0 = t0 // 8
                if b:
                    act.wait_ge(S["route_stored"], 16 * b)

                def take_route(m):
                    for c in range(2):
                        act.wait_ge(S["route_mm"], 2 * (m + m0) + c + 3)
                        act.activation(out[:, bass.ds(8 * m + 4 * c, 4), :], bank[4 + c].rearrange("p (t i) -> p t i", t=4),
                                       ACT.Copy).then_inc(S["route_free"], 1)

                first = 1 - b
                if first:
                    take_route(0)
                for s in range(2):
                    with act.Fori(0, 8) as i:
                        take_route(i + first + 8 * s)
                    if s == 1:
                        act.wait_ge(S["route_free"], (t0 + n) // 4 + 2)
                        act.sem_inc(S["route_evac"], n // 4)
                    early_gelu(s, 37 + b, 12 + 4 * b + s)
                for s in (2, 3):
                    early_gelu(s, 37 + b, 12 + 4 * b + s)

            def expert_gelu(b, use):
                act.wait_ge(slot_used[2 * b], use + 2)
                act.activation(act_x[:, b], psum[:, 2 * b:2 * b + 2, 0:NT], ACT.Gelu_apprx_tanh).then_inc(S["expert_gelu"], 1)

            def hi_part(s, use, part, before):
                act.wait_ge(slot_full[s], 16 * (use + 1 - PAGED[s]))
                if before:
                    act.wait_ge(slot_used[before[0]], before[1] + 2)
                for c in range(4):
                    r = slice(c * SLOT // 4, (c + 1) * SLOT // 4)
                    act.activation(w_hi[:, part, r], ring[:, s, r], ACT.Copy).then_inc(S["split_hi"], 1)

            act.wait_ge(S["route_stored"], 16 * len(ROUTE_BLOCKS))
            for k in range(0, KT, 4):
                act.activation(h2_hi[:, k:k + 4, :], hT[:, k:k + 4, :], ACT.Copy).then_inc(S["split_hi"], 1)
            hi_part(0, 39, 0, None)
            hi_part(2, 39, 1, None)
            expert_gelu(0, 39)
            with act.Fori(0, N_LATE // 2 - 1) as i:
                hi_part(1, i + 39, 0, (3, i + 38))
                expert_gelu(1, i + 39)
                hi_part(0, i + 40, 1, (2, i + 39))
                hi_part(3, i + 39, 0, (1, i + 39))
                expert_gelu(0, i + 40)
                hi_part(2, i + 40, 1, (0, i + 40))
            hi_part(1, V_USE - 1, 0, (3, V_USE - 2))
            expert_gelu(1, V_USE - 1)
            hi_part(3, V_USE - 1, 1, (2, V_USE - 1))
            for s in range(SLOTS):
                hi_part(s, V_USE, s % 2, ((1, V_USE - 1), (3, V_USE - 1), (0, V_USE), (1, V_USE))[s])
            with act.Fori(0, N_EARLY // 4 - 1) as i:
                for s in range(SLOTS):
                    hi_part(s, i + V_USE + 1, s % 2, ((s + 2) % 4, i + V_USE + s // 2))

        @block.vector
        def _(dve):
            dve.sem_inc(S["ada_done"], 1)
            dve.memset(ones[:], 1.0).then_inc(S["consts_set"], 1)
            dve.memset(epst[:], EPS).then_inc(S["consts_set"], 1)
            step = Chain(dve, S["dve_step"])
            dve.wait_ge(S["consts_in"], 16 * 6)

            def ada_bias(m, t):
                dve.wait_ge(S["ada_reduced"], m + 1)
                dve.tensor_tensor(adaT[:, bass.ds(t, 2), :], bank[6][:, 0:2 * NR].rearrange("p (j r) -> p j r", j=2),
                                  par("bada")[:, bass.ds(t, 2)].unsqueeze(2).broadcast_to((P, 2, NR)),
                                  ALU.add).then_inc(S["ada_done"], 1)

            with dve.Fori(0, N_ADA0) as m:
                ada_bias(m, 2 * m)

            def modulate(which, src, dst, ready):
                sh, sc = 3 * KT * which, 3 * KT * which + KT
                w = par("nw")[:, KT * which:KT * which + KT].unsqueeze(2).broadcast_to((P, KT, NR))
                step(dve.scalar_tensor_tensor(A1[:], adaT[:, sc:sc + KT, :], 1.0, w, ALU.add, ALU.mult))
                step(dve.tensor_tensor(dst, src, rstd[:].unsqueeze(1).broadcast_to((P, KT, NT)), ALU.mult))
                step(dve.tensor_tensor(dst[:, :, SEQ:NT], dst[:, :, SEQ:NT], A1[:, :, 1:NR], ALU.mult))
                dve.tensor_tensor(dst[:, :, SEQ:NT], dst[:, :, SEQ:NT], adaT[:, sh:sh + KT, 1:NR], ALU.add)
                for k in range(KT):
                    ins = dve.tensor_scalar(dst[:, k, 0:SEQ], dst[:, k, 0:SEQ], A1[:, k, 0:1], adaT[:, sh + k, 0:1],
                                            ALU.mult, ALU.add)
                ins.then_inc(ready, 1)

            dve.wait_ge(S["x_std"], 1)
            dve.wait_ge(S["ada_done"], N_ADA0 + 1)
            step(dve.reciprocal(rstd[:], rstd[:]))
            modulate(0, xT[:], hT[:], S["h_ready"])
            dve.wait_ge(S["h_ready"], 1)

            def windows(src, n):
                return bass.AP(src.tensor, src.offset, [list(src.ap[0]), list(src.ap[1]), [16, n], [1, 32]])

            def compress(src, n, w, tmp, dst, link):
                link(dve.tensor_tensor(tmp, windows(src, n), w.unsqueeze(1).unsqueeze(1).broadcast_to((P, G, n, 32)), ALU.mult))
                return dve.tensor_reduce(dst, tmp, AX.X, ALU.add)

            with dve.Fori(0, 8) as i:
                ada_bias(i + 16, 2 * i + 32)
                dve.wait_ge(cache_full[3], 16 * PAGES * (i + 1))
                link = Chain(dve, S["loop_step"], 3 * i)
                for v, w in enumerate(("wck", "wcv")):
                    src = ring[:, 3, v * 2048:(v + 1) * 2048].rearrange("p (g n) -> p g n", g=G)
                    ins = compress(src, N_CMP, par(w), ctmp, CK[:, v, bass.ds(i, 1), :, 1:1 + N_CMP].rearrange("p b g n -> p (b g) n"), link)
                    if v == 0:
                        link(ins)
                    else:
                        ins.then_inc(slot_used[3], 1)
                        dve.wait_ge(slot_used[3], i + 6)
            with dve.Fori(0, 6) as i:
                ada_bias(i + 24, 2 * i + 48)

            def head_norm(n, t0, count, w):
                dve.wait_ge(S["hn_std"], n + 1)
                r = rs[n % 2][:, 0:count, :]
                step(dve.reciprocal(r, r))
                dve.scalar_tensor_tensor(PR[:, t0:t0 + count, :], PR[:, t0:t0 + count, :], w, r, ALU.mult,
                                         ALU.mult).then_inc(S["hn_done"], 1)

            for n, (t0, count, w) in enumerate(NORM_GROUPS):
                head_norm(n, t0, count, par("hw")[:, w:w + 1])
            dve.wait_ge(S["hn_done"], len(NORM_GROUPS))
            for n, (t0, count) in enumerate(ROPE_GROUPS):
                x, t = PR[:, t0:t0 + count, :], rtmp[:, 0:count, :]
                bc = lambda name: cst(name).unsqueeze(1).broadcast_to((P, count, NT))
                dve.wait_ge(S["rope_rot"], n + 1)
                if n:
                    dve.wait_ge(S["rope_done"], n)
                dve.tensor_tensor(t, psum[:, n % 2 * 4:n % 2 * 4 + count, 0:NT], bc("sin"), ALU.mult)
                step(dve.tensor_tensor(x, x, bc("cos"), ALU.mult))
                dve.tensor_tensor(x, x, t, ALU.add).then_inc(S["rope_done"], 1)
            for v, w in enumerate(("wck", "wcv")):
                src = PR[:, T_KC + 2 * v:T_KC + 2 * v + 2, :]
                step(compress(src, N_CMP_P, par(w), ctmpp, CP[:, v, :, :], step))
                b = par("bck" if v == 0 else "bcv")
                step(dve.tensor_scalar(CP[:, v, :, :], CP[:, v, :, :], b, None, ALU.add))
                c = CK[:, v, :, :, 1:1 + N_CMP].rearrange("p b g n -> p (b g) n")
                ins = dve.tensor_scalar(c, c, b, None, ALU.add)
                if v == 0:
                    step(ins)
            ins.then_inc(S["cmp_ready"], 1)
            dve.wait_ge(S["rope_done"], 4)
            for v, tw, ts in ((0, T_KW, T_KS), (1, T_VW, T_VS)):
                dve.tensor_copy(CK[:, v, :, :, 0].rearrange("p b g -> p g b"), PR[:, tw:tw + G, SEQ:NT])
                dve.tensor_copy(CK[:, v, :, :, NC0 - 1].rearrange("p b g -> p g b"), PR[:, ts:ts + G, SEQ:NT])
            dve.wait_ge(S["cmp_rot"], 1)
            c = CK[:, 0, :, :, 1:1 + N_CMP].rearrange("p b g n -> p (b g) n")
            for m in range(2):
                dve.tensor_tensor(croll[:, 8 * m:8 * m + 8, :], bank[m][:, 0:8 * N_CMP].rearrange("p (m n) -> p m n", m=8),
                                  cst("sinc").unsqueeze(1).broadcast_to((P, 8, N_CMP)), ALU.mult)
            step(dve.tensor_tensor(c, c, cst("cosc").unsqueeze(1).broadcast_to((P, NS * G, N_CMP)), ALU.mult))
            step(dve.tensor_tensor(c, c, croll, ALU.add))
            bc = lambda name: cst(name)[:, 0:N_CMP_P].unsqueeze(1).broadcast_to((P, G, N_CMP_P))
            dve.tensor_tensor(croll[:, 0:G, 0:N_CMP_P], bank[2][:, 0:G * N_CMP_P].rearrange("p (g n) -> p g n", g=G),
                              bc("sinc"), ALU.mult)
            step(dve.tensor_tensor(CP[:, 0, :, :], CP[:, 0, :, :], bc("cosc"), ALU.mult))
            dve.tensor_tensor(CP[:, 0, :, :], CP[:, 0, :, :], croll[:, 0:G, 0:N_CMP_P], ALU.add).then_inc(S["cmp_done"], 1)
            with dve.Fori(0, DNT // 4) as i:
                for b in range(4):
                    t = 4 * i + b
                    dve.wait_ge(S["conv_silu"], t + 1)
                    link = Chain(dve, S["loop_step"], 3 * (t + NS))
                    x, y = PR[:, bass.ds(T_DNQ + t, 1), 0:SEQ], convt[:, b:b + 1, 0:SEQ]
                    w = [par("convw")[:, bass.ds(4 * t + j, 1)] for j in range(4)]
                    link(dve.tensor_scalar(y, x, w[3], None, ALU.mult))
                    for j in (1, 2, 3):
                        ins = dve.scalar_tensor_tensor(y[:, :, j:SEQ], x[:, :, 0:SEQ - j], w[3 - j], y[:, :, j:SEQ], ALU.mult, ALU.add)
                        if j < 3:
                            link(ins)
                    ins.then_inc(S["conv_done"], 1)
            cw = par("convw").rearrange("p (t j) -> p t j", j=4)
            dve.wait_ge(S["hist_new"], 1)
            for j in range(4):
                w = cw[:, :, j].unsqueeze(2).broadcast_to((P, DNT, NS))
                step(dve.tensor_tensor(convs if j == 0 else convs2, hist[:, :, j, :], w, ALU.mult))
                if j:
                    ins = dve.tensor_tensor(convs, convs, convs2, ALU.add)
                    if j < 3:
                        step(ins)
            ins.then_inc(S["conv_done"], 1)

            dve.wait_ge(S["conv_done"], DNT + 1)
            step(dve.memset(qpad, 0.0))
            for g in range(G):
                ins = dve.tensor_copy(qpad.rearrange("p (b g) r -> p b g r", g=G)[:, :, g, 0:REP],
                                      PR[:, g * REP:(g + 1) * REP, SEQ:NT].rearrange("p r b -> p b r"))
            ins.then_inc(S["qpad_done"], 1)
            causal = cst("causal").rearrange("p (a n) -> p a n", a=2)
            cmpbias = cst("cmpbias").rearrange("p (a n) -> p a n", a=2)
            cmp01 = cst("cmp01").rearrange("p (a n) -> p a n", a=2)

            def unit_max(u):
                a, b, n = u % 2, u % 2 * 2, P * (u % 2 + 1)
                dve.wait_ge(S["u_scores"], u + 1)
                if u >= 3:
                    dve.wait_ge(S["u_turned"], u - 2)
                s = SB[u % 3]
                dve.tensor_tensor(s[:, 512:512 + N_CMP_P], bank[b][:, 256:256 + N_CMP_P], cmpbias[:, a, 0:N_CMP_P], ALU.add)
                dve.tensor_tensor(s[:, 0:n], bank[b][:, 0:n], causal[:, a, 0:n], ALU.add)
                step(dve.tensor_tensor(s[:, 256:256 + n], bank[b + 1][:, 0:n], causal[:, a, 0:n], ALU.add))
                mx = sm1[:, u % 2, 2, :]
                for m, (lo, w) in enumerate(((512, N_CMP_P), (0, n), (256, n))):
                    ins = dve.tensor_reduce(mx[:, m:m + 1], s[:, lo:lo + w], AX.X, ALU.max)
                step(ins)
                dve.tensor_scalar(sm1[:, u % 2, 0, :], mx, -SCALE, None, ALU.mult).then_inc(S["u_max"], 1)

            dve.wait_ge(S["vt_evac"], 1)
            unit_max(0)
            for u in range(2 * H):
                if u + 1 < 2 * H:
                    unit_max(u + 1)
                h, a, n = u // 2, u % 2, P * (u % 2 + 1)
                f, s = sm1[:, u % 2, 1, :], SB[u % 3]
                dve.wait_ge(S["u_exp"], u + 1)
                step(dve.reciprocal(f, f))
                step(dve.tensor_tensor(f, f, GT[:, a, 3 * h:3 * h + 3], ALU.mult))
                dve.scalar_tensor_tensor(s[:, 512:512 + N_CMP_P], s[:, 512:512 + N_CMP_P], f[:, 0:1],
                                         cmp01[:, a, 0:N_CMP_P], ALU.mult, ALU.mult)
                dve.tensor_scalar(s[:, 0:n], s[:, 0:n], f[:, 1:2], None, ALU.mult)
                dve.tensor_scalar(s[:, 256:256 + n], s[:, 256:256 + n], f[:, 2:3], None, ALU.mult).then_inc(S["u_norm"], 1)

            dve.wait_ge(S["gates_in"], 16 * 12)
            dve.wait_ge(S["qpad_done"], 1)
            for q in range(4):
                dve.wait_ge(S["r_scores"], q + 1)
                if q:
                    dve.wait_ge(S["r_out"], q)
                dve.tensor_copy(SS[:, 0:512], bank[3])
                step(dve.tensor_copy(SS[:, 512:512 + NC0], bank[0][:, 0:NC0]))
                dve.tensor_copy(SS[:, 577:1601].rearrange("p (a n) -> p a n", a=2), psum[:, 1:3, :])
                step(dve.tensor_reduce(smS[:, 2, 0:1], SS[:, 513:576], AX.X, ALU.max))
                dve.tensor_scalar(smS[:, 0, 0:1], smS[:, 2, 0:1], -SCALE, None, ALU.mult).then_inc(S["r_cmpmax"], 1)
                dve.wait_ge(S["r_cmpexp"], q + 1)
                step(dve.reciprocal(smS[:, 1, 0:1], smS[:, 1, 0:1]))
                step(dve.tensor_scalar(SS[:, 513:576], SS[:, 513:576], smS[:, 1, 0:1], None, ALU.mult))
                win = bass.AP(SS.tensor, SS.offset + 513 + 3, [list(SS.ap[0]), [4, 14], [1, 5]])
                dve.tensor_reduce(impb[:, 0, 0:14], win, AX.X, ALU.add).then_inc(S["r_imp"], 1)
                dve.wait_ge(S["r_impsum"], q + 1)
                imp = bank[4][:, 0:14]
                step(dve.tensor_reduce(impb[:, 4, 0:1], imp, AX.X, ALU.min))
                step(dve.tensor_scalar(impb[:, 1, 0:14], imp, impb[:, 4, 0:1], None, ALU.is_equal))
                step(dve.tensor_tensor(impb[:, 1, 0:14], impb[:, 1, 0:14], cst("blockid"), ALU.mult))
                step(dve.tensor_reduce(impb[:, 4, 1:2], impb[:, 1, 0:14], AX.X, ALU.max))
                step(dve.tensor_scalar(impb[:, 2, 0:14], cst("blockid"), impb[:, 4, 1:2], NEG, ALU.is_equal, ALU.mult))
                blocks = SS[:, 577 + 64:577 + 64 * 15].rearrange("p (s n) -> p s n", s=14)
                step(dve.tensor_tensor(blocks, blocks, impb[:, 2, 0:14].unsqueeze(2).broadcast_to((P, 14, 64)), ALU.add))
                dve.tensor_reduce(smS[:, 2, 1:2], SS[:, 576:1601], AX.X, ALU.max)
                step(dve.tensor_reduce(smS[:, 2, 2:3], SS[:, 0:513], AX.X, ALU.max))
                dve.tensor_scalar(smS[:, 0, 1:3], smS[:, 2, 1:3], -SCALE, None, ALU.mult).then_inc(S["r_max"], 1)
                dve.wait_ge(S["r_exp"], q + 1)
                step(dve.reciprocal(smS[:, 1, 1:3], smS[:, 1, 1:3]))
                step(dve.tensor_tensor(smS[:, 1, 1:3], smS[:, 1, 1:3], gateS[:, q, 1:3], ALU.mult))
                dve.tensor_scalar(SS[:, 513:576], SS[:, 513:576], gateS[:, q, 0:1], None, ALU.mult)
                dve.tensor_scalar(SS[:, 576:1601], SS[:, 576:1601], smS[:, 1, 1:2], None, ALU.mult)
                dve.tensor_scalar(SS[:, 0:513], SS[:, 0:513], smS[:, 1, 2:3], None, ALU.mult).then_inc(S["r_norm"], 1)

            dve.wait_ge(S["small_evac"], 3)
            step(dve.tensor_scalar(rowsG[:], rowsG[:], par("dt")[0:H, :], None, ALU.add))
            step(dve.tensor_scalar(rows2[:, 0, :], rowsG[:], -1.0, None, ALU.mult))
            dve.tensor_tensor(rows2[:, 1, :], rows2[:, 0, :], rowsG[:], ALU.min).then_inc(S["g_parts"], 1)
            dve.wait_ge(S["g_soft"], 1)
            step(dve.scalar_tensor_tensor(rows2[:, 0, :], rowsG[:], 0.0, rows2[:, 1, :], ALU.max, ALU.add))
            step(dve.tensor_scalar(rows2[:, 0, :], rows2[:, 0, :], alog[:], -1.0, ALU.mult, ALU.mult))
            dve.tensor_copy(rowsG[:, SEQ:NT], rows2[:, 0, SEQ:NT])
            for c in range(2):
                r = slice(c * P, (c + 1) * P)
                ins = dve.tensor_tensor_scan(rowsG[:, r], ones[0:H, :], rows2[:, 0, r], 0.0, ALU.mult, ALU.add)
            ins.then_inc(S["g_rows"], 1)
            for n in range(5, 9):
                t0 = T_DNQ + 4 * (n - 5)
                dve.wait_ge(S["hn_std"], n + 1)
                r = rs[n % 2]
                step(dve.reciprocal(r, r))
                dve.tensor_tensor(PR[:, t0:t0 + 4, :], PR[:, t0:t0 + 4, :], r, ALU.mult).then_inc(S["hn_done"], 1)
            dve.wait_ge(S["g_colsc"], 2)
            dve.wait_ge(S["hn_done"], 9)
            gcol = cols[:, 0, :, :].rearrange("p h c -> p (h c)")
            bcol = cols[:, 1, :, :].rearrange("p h c -> p (h c)")
            for hb in range(2):
                dve.wait_ge(S["g_bcast"], hb + 1)
                if hb:
                    dve.wait_ge(S["d_half"], 1)
                for c in range(2):
                    dve.tensor_copy(glast[:, 4 * hb:4 * hb + 4, c], psum[:, 4:8, c * P + P - 1])
                for a in range(8):
                    u = 8 * hb + a
                    g = bank[4 + a // 2][:, a % 2 * P:(a % 2 + 1) * P]
                    dve.tensor_scalar(Cb[:, a, :], g, gcol[:, u:u + 1], 0.0, ALU.subtract, ALU.min)
                    ins = dve.tensor_scalar(Yb[:, a, :], g, gcol[:, u:u + 1], 0.0, ALU.subtract, ALU.max)
                ins.then_inc(S["d_diff"], 1)
                dve.wait_ge(S["d_exp"], hb + 1)
                dve.tensor_tensor(Cb, Cb, cst("upper").unsqueeze(1).broadcast_to((P, H, P)), ALU.mult)
                step(dve.tensor_tensor(Yb, Yb, cst("lower").unsqueeze(1).broadcast_to((P, H, P)), ALU.mult))
                dve.wait_ge(S["kk_mm"], hb + 1)
                flat = lambda ap: ap.rearrange("p (a u) n -> p a (u n)", u=4)
                dve.scalar_tensor_tensor(flat(Ab[:, 8 * hb:8 * hb + 8, :]), psum[:, 2:4, :], SCALE, flat(Cb), ALU.mult, ALU.mult)
                for a in range(8):
                    u = 8 * hb + a
                    ins = dve.scalar_tensor_tensor(Mb[:, u, :], bank[a // 4][:, a % 4 * P:(a % 4 + 1) * P], bcol[:, u:u + 1],
                                                   Yb[:, a, :], ALU.mult, ALU.mult)
                ins.then_inc(S["d_half"], 1)
            step(dve.tensor_tensor(kdec[:], glast[:], cols[:, 0, :, :], ALU.subtract))
            dve.nop().then_inc(S["kdec_diff"], 1)
            dve.memset(Tb, 0.0).then_inc(S["t_zero"], 1)
            step(dve.tensor_copy(Tm.rearrange("p i j -> p (i j)"), cst("ident16")))
            dve.wait_ge(S["m_in"], 16)
            for i in range(1, 16):
                t = dtmp[:, 0:16 * i].rearrange("p (j c) -> p j c", c=16)
                step(dve.tensor_tensor(t, Dm[:, i, 0:i].unsqueeze(2).broadcast_to((P, i, 16)), Tm[:, 0:i, :], ALU.mult))
                step(dve.tensor_reduce(dred, t.rearrange("p j c -> p c j"), AX.X, ALU.add))
                ins = dve.tensor_tensor(Tm[:, i, :], Tm[:, i, :], dred, ALU.subtract)
                if i < 15:
                    step(ins)
            ins.then_inc(S["t_ready"], 1)
            dve.wait_ge(S["t_evac"], 1)
            for n in range(6):
                level, half = n // 2, n % 2
                if n:
                    dve.wait_ge(S["lv_y"], n)
                mask = cst("levels")[:, level * P:(level + 1) * P].unsqueeze(1).broadcast_to((P, H, P))
                dve.tensor_tensor(Cb, Mb[:, 8 * half:8 * half + 8, :], mask, ALU.mult).then_inc(S["lv_c"], 1)
                dve.wait_ge(S["lv_z"], n + 1)
                u = flat(Ub[:, 8 * half:8 * half + 8, :])
                dve.tensor_tensor(u, u, psum[:, 2:4, :], ALU.subtract).then_inc(S["lv_u"], 1)
            banks4 = psum[:, 0:4, :].rearrange("p a (u n) -> p (a u) n", u=4)
            dve.wait_ge(S["vk_tok"], 1)
            dve.tensor_tensor(Tb, banks4, bcol.unsqueeze(2).broadcast_to((P, NU, P)), ALU.mult).then_inc(S["bv_ready"], 1)
            dve.wait_ge(S["kdec_exp"], 1)
            step(dve.tensor_tensor(bge[:], bge[:], cols[:, 1, :, 1], ALU.mult))
            dve.wait_ge(S["vk_tok"], 2)
            dve.tensor_tensor(Mb, banks4, kdec[:].rearrange("p h c -> p (h c)").unsqueeze(2).broadcast_to((P, NU, P)),
                              ALU.mult).then_inc(S["kd_ready"], 1)
            dve.wait_ge(S["zs_mm"], 1)
            odd = lambda ap: ap.rearrange("p (h c) n -> p h c n", c=2)[:, :, 1, :]
            units2 = lambda b: psum[:, b:b + 2, :].rearrange("p a (u n) -> p (a u) n", u=4)
            step(dve.tensor_tensor(Yb, units2(6), bge[:].unsqueeze(2).broadcast_to((P, H, P)), ALU.mult))
            dve.tensor_tensor(Yb, odd(Tb), Yb, ALU.subtract).then_inc(S["rhs_ready"], 1)
            dve.wait_ge(S["qe_exp"], 1)
            dve.scalar_tensor_tensor(Cb, Cb, SCALE, PR[:, T_DNQ:T_DNK, P:SEQ], ALU.mult, ALU.mult).then_inc(S["qe_ready"], 1)
            dve.wait_ge(S["s2_mm"], 1)
            step(dve.tensor_tensor(Yb, S1, egl[:].unsqueeze(2).broadcast_to((P, H, P)), ALU.mult))
            dve.tensor_tensor(Yb, Yb, units2(6), ALU.add).then_inc(S["s2_ready"], 1)
            dve.wait_ge(S["o_evac"], 2)
            hb_view = lambda t: PR[:, t:t + H, SEQ:NT]
            mat = lambda ap: ap.rearrange("p (h b) -> p h b", h=H)
            dve.tensor_copy(kq.rearrange("p (h b) c -> p h b c", h=H)[:, :, :, 0], hb_view(T_DNK))
            dve.tensor_copy(kq.rearrange("p (h b) c -> p h b c", h=H)[:, :, :, 1], hb_view(T_DNQ)).then_inc(S["smp_kq"], 1)
            dve.tensor_copy(mat(smp["kc"]), hb_view(T_DNK))
            dve.tensor_tensor(mat(smp["prod"]), hb_view(T_DNQ), hb_view(T_DNK), ALU.mult).then_inc(S["smp_kq"], 1)
            dve.wait_ge(S["smp_evac"], 2)
            dve.wait_ge(S["smp_rows"], 1)
            sk, sq_ = sks[:, :, 0], sks[:, :, 1]
            step(dve.tensor_tensor(smp["vn"], sk, smp["eg"], ALU.mult))
            step(dve.tensor_tensor(mat(smp["vn"]), hb_view(T_DNV), mat(smp["vn"]), ALU.subtract))
            dve.tensor_tensor(smp["vn"], smp["vn"], smp_g[:, 64:P], ALU.mult).then_inc(S["smp_vn"], 1)
            dve.wait_ge(S["smp_vn"], 1)
            step(dve.tensor_tensor(smp["prod"], sq_, smp["eg"], ALU.mult))
            step(dve.tensor_tensor(smp["qk"], smp["qk"], smp["vn"], ALU.mult))
            step(dve.tensor_tensor(smp["prod"], smp["prod"], smp["qk"], ALU.add))
            step(dve.tensor_scalar(hb_view(T_DNV), mat(smp["prod"]), SCALE, None, ALU.mult))
            dve.wait_ge(S["smp_evac"], 3)
            dve.wait_ge(S["s2_stored"], 16)
            dve.wait_ge(S["smp_mm"], 1)
            for m in range(2):
                s0 = ring[:, m, :].rearrange("p (m n) -> p m n", n=P)
                step(dve.tensor_tensor(s0, s0, smp["eg"][:, 32 * m:32 * m + 32].unsqueeze(2).broadcast_to((P, 32, P)), ALU.mult))
            for n in range(9):
                if n < 8:
                    if n:
                        dve.wait_ge(S["smp_outer"], n)
                    dve.tensor_tensor(vdiag, vtok.unsqueeze(1).broadcast_to((64, 8, P)),
                                      ident[0:64, 8 * n:8 * n + 8].unsqueeze(2).broadcast_to((64, 8, P)),
                                      ALU.mult).then_inc(S["smp_diag"], 1)
                if n:
                    m = n - 1
                    s0 = ring[:, m // 4, m % 4 * 1024:(m % 4 + 1) * 1024].rearrange("p (a n) -> p a n", a=2)
                    dve.wait_ge(S["smp_outer"], n)
                    b = 4 + m % 2 * 2
                    ins = dve.tensor_tensor(s0, s0, psum[:, b:b + 2, :], ALU.add)
                    if m % 4 == 3:
                        ins.then_inc(S["smp_new"], 1)
            dve.wait_ge(S["z_silu"], 1)
            for n in (9, 10):
                t0 = T_DNV + 4 * (n - 9)
                head_norm(n, t0, 4, par("dnw"))
                dve.wait_ge(S["hn_done"], n + 1)
                ins = dve.tensor_tensor(PR[:, t0:t0 + 4, :], PR[:, t0:t0 + 4, :], PR[:, t0 + 8:t0 + 12, :], ALU.mult)
            ins.then_inc(S["dn_out"], 1)
            with dve.Fori(0, 48 - N_ADA1) as i:
                ada_bias(i + N_ADA1, 2 * i + 2 * N_ADA1)
            pairs = lambda b: psum[:, b:b + 2, 0:NT]
            for k in range(0, 2 * H, 4):
                t = k if k < H else T_DNV + k - H
                dve.wait_ge(S["o_top"], k // 4 + 1)
                dve.tensor_tensor(pr_lo[:, t:t + 4, :], PR[:, t:t + 4, :], o_hi[:, k:k + 4, :], ALU.subtract).then_inc(S["o_split"], 1)

            def dense_rest(q):
                for c in range(2):
                    r = slice(c * SLOT // 4, (c + 1) * SLOT // 4)
                    dve.wait_ge(S["split_hi"], 4 * q + c + 1)
                    dve.tensor_tensor(w_lo[:, q % 4, r], ring[:, q % 4, r], dense_hi(q % 2, c), ALU.subtract).then_inc(S["split_lo"], 1)

            dense_rest(0)
            dense_rest(1)
            dve.wait_ge(S["proj_evac"], T_END + N_MERGE + 4)
            for n in range(8):
                b, t = n % 2 * 4, 2 * n
                ga, gb = PR[:, H + t:H + t + 2, :], PR[:, MERGE_B[n]:MERGE_B[n] + 2, :]
                dve.wait_ge(slot_used[n % 4], 28 + n // 4 + 2)
                dve.tensor_tensor(ga, ga, pairs(b), ALU.mult)
                step(dve.tensor_tensor(gb, gb, pairs(b + 2), ALU.mult))
                step(dve.tensor_tensor(hT[:, t:t + 2, :], ga, gb, ALU.add))
                step(dve.tensor_copy(mixed_hi[:, t:t + 2, :], hT[:, t:t + 2, :]))
                dve.tensor_tensor(h2_lo[:, t:t + 2, :], hT[:, t:t + 2, :], mixed_hi[:, t:t + 2, :], ALU.subtract).then_inc(S["br_done"], 1)
                dense_rest(n + 2)
            dve.wait_ge(S["x_again"], 16)
            dve.wait_ge(S["ada_done"], 49)
            for n in range(8):
                b, t = n % 4 * 2, 2 * n
                dve.wait_ge(slot_used[n % 4], 30 + n // 4 + 2)
                x1s = x1tmp[:, n % 2]
                step(dve.tensor_tensor(x1s, psum[:, b:b + 2, SEQ:NT], adaT[:, 2 * KT + t:2 * KT + t + 2, 1:NR], ALU.mult))
                for j in range(2):
                    dve.scalar_tensor_tensor(xT[:, t + j, 0:SEQ], bank[b + j][:, 0:SEQ], adaT[:, 2 * KT + t + j, 0:1],
                                             xT[:, t + j, 0:SEQ], ALU.mult, ALU.add)
                dve.tensor_tensor(xT[:, t:t + 2, SEQ:NT], xT[:, t:t + 2, SEQ:NT], x1s, ALU.add).then_inc(S["x1_done"], 1)
                dense_rest(10 + n)
            dve.wait_ge(S["x_std"], 2)
            step(dve.reciprocal(rstd[:], rstd[:]))
            dve.wait_ge(S["x1_done"], 8)
            modulate(1, xT[:], hT[:], S["h_ready"])
            for k in range(0, KT, 4):
                dve.wait_ge(S["o_top"], k // 4 + 5)
                dve.tensor_tensor(hq_lo[:, k:k + 4, :], hT[:, k:k + 4, :], hq_hi[:, k:k + 4, :], ALU.subtract).then_inc(S["o_split"], 1)
            for q in range(18, N_DENSE):
                dense_rest(q)

            dve.sem_inc(S["acc_added"], 2)
            for a, (t0, n) in enumerate(TOKEN_TILES):
                sc, alt = SC[0:n, a].rearrange("p (t n) -> p t n", n=P), SCr[0:n].rearrange("p (t n) -> p t n", n=P)
                val, idx = kval[0:n], kidx[0:n]
                dve.wait_ge(S["scores_in"], a + 1)

                def top16(src, alt, val, idx, count):
                    for t in range(count):
                        ins = dve.max(val[:, t, 0:8], src[:, t, :])
                    step(ins)
                    for t in range(count):
                        dve.max_index(idx[:, t, 0:8], val[:, t, 0:8], src[:, t, :])
                        ins = dve.match_replace(alt[:, t, :], val[:, t, 0:8], src[:, t, :], LOWEST)
                    step(ins)
                    for t in range(count):
                        ins = dve.max(val[:, t, 8:16], alt[:, t, :])
                    step(ins)
                    for t in range(count):
                        ins = dve.max_index(idx[:, t, 8:16], val[:, t, 8:16], alt[:, t, :])
                    step(ins)

                top16(sc, alt, val, idx, 16)
                step(dve.tensor_copy(kidxf[0:n], idx))
                half = lambda ap, m: ap.rearrange("p (h m) k -> p h m k", m=2)[:, :, m, :]
                step(dve.tensor_tensor(sc.rearrange("p (h a) (b k) -> p h (a b) k", a=2, k=16),
                                       half(val, 0).unsqueeze(3).broadcast_to((n, H, 16, 16)),
                                       half(val, 1).unsqueeze(2).broadcast_to((n, H, 16, 16)), ALU.add))
                wide = lambda ap: ap.rearrange("p (h a) n -> p h (a n)", a=2)
                best = chosen[0:n, 2, :].rearrange("p (h k) -> p h k", h=H)
                if a:
                    dve.wait_ge(S["chosen_turned"], a)
                top16(wide(sc), wide(alt), best, cpos[0:n, 0], H)
                step(dve.tensor_scalar(cpos[0:n, 1], cpos[0:n, 0], 4, None, ALU.logical_shift_right))
                step(dve.tensor_scalar(cpos[0:n, 2], cpos[0:n, 0], 15, None, ALU.bitwise_and))
                step(dve.tensor_copy(cposf[0:n], cpos[0:n, 1:3]))
                step(dve.tensor_copy(btop[0:n], best[:, :, 0:1]))
                dve.tensor_tensor(best, best, btop[0:n].broadcast_to((n, H, 16)), ALU.subtract).then_inc(S["best_sub"], 1)
                for m in range(2):
                    eq = alt.rearrange("p t (a j) -> p (t a) j", j=16)
                    step(dve.tensor_tensor(eq, cst("iota")[0:n, 0:16].unsqueeze(1).broadcast_to((n, P, 16)),
                                           cposf[0:n, m].rearrange("p h k -> p (h k)").unsqueeze(2).broadcast_to((n, P, 16)), ALU.is_equal))
                    eq4 = eq.rearrange("p (h k) j -> p h k j", h=H)
                    step(dve.tensor_tensor(eq4, eq4, half(kidxf[0:n], m).unsqueeze(2).broadcast_to((n, H, 16, 16)), ALU.mult))
                    step(dve.tensor_reduce(chosen[0:n, m, :], eq, AX.X, ALU.add))
                dve.wait_ge(S["best_exp"], a + 1)
                step(dve.tensor_reduce(bsum[0:n], best, AX.X, ALU.add))
                step(dve.reciprocal(bsum[0:n], bsum[0:n]))
                dve.tensor_tensor(best, best, bsum[0:n].unsqueeze(2).broadcast_to((n, H, 16)), ALU.mult).then_inc(S["chosen"], 1)
            dve.sem_inc(S["route_mm"], 2)
            dve.wait_ge(S["chosen_evac"], 3)
            with dve.Fori(0, NT // 8) as i:
                for b in range(2):
                    dve.wait_ge(S["route_mm"], 2 * i + b + 1)
                    for t in range(4):
                        col = 8 * i + 4 * b + t
                        dve.tensor_scalar(O2[:, b, t, :], cst("iota"), IT[:, 1, bass.ds(col, 1)], IT[:, 2, bass.ds(col, 1)],
                                                ALU.is_equal, ALU.mult)
                        ins = dve.tensor_scalar(O1[:, b, t, :], cst("iota"), IT[:, 0, bass.ds(col, 1)], None, ALU.is_equal)
                    ins.then_inc(S["onehot"], 1)
            dve.wait_ge(S["route_stored"], 16 * len(ROUTE_BLOCKS))
            dve.wait_ge(S["gelu_early"], N_EARLY + 2)
            dve.memset(acc, 0.0)

            def lo_chunk(dst, src, top, count):
                dve.wait_ge(S["split_hi"], count)
                dve.tensor_tensor(dst, src, top, ALU.subtract).then_inc(S["split_lo"], 1)

            def lo_part(s, part, split, c):
                r = slice(c * SLOT // 4, (c + 1) * SLOT // 4)
                lo_chunk(w_lo[:, s, r], ring[:, s, r], w_hi[:, part, r], 4 * (split + 1 + N_DENSE) + c + 1)

            def expert_act(b, loaded, g):
                dve.wait_ge(S[f"route_in{b}"], 16 * loaded)
                link = Chain(dve, S["act_chain"], 2 * g)
                link(dve.tensor_tensor(act_x[:, b], act_x[:, b], Wb[:, b], ALU.mult))
                link(dve.tensor_copy(act_hi[:, b], act_x[:, b]))
                dve.tensor_tensor(act_lo[:, b], act_x[:, b], act_hi[:, b], ALU.subtract).then_inc(S["expert_act"], 1)

            def late_act(b, i, g):
                dve.wait_ge(S["expert_gelu"], g + 3)
                expert_act(b, i + 1, g)

            def expert_sum(s, use, g, beside=lambda m: None):
                for m in range(8):
                    if m < 7:
                        dve.wait_ge(S["acc_mm"], 7 * g + m + 1)
                    else:
                        dve.wait_ge(slot_used[s], use + 2)
                    if m == 0:
                        dve.wait_ge(S["acc_added"], 8 * g + 2)
                    dst = acc[:, 2 * m:2 * m + 2, :]
                    v = 4 + m % 2 * 2
                    dve.tensor_tensor(dst, dst, psum[:, v:v + 2, 0:NT], ALU.add).then_inc(S["acc_added"], 1)
                    beside(m)

            def splitting(s, part, split, then=None):
                def beside(m):
                    if m in (1, 4):
                        lo_part(s, part, split, m // 3)
                    if m == 2 and then:
                        then()
                return beside

            for k in range(0, KT, 4):
                lo_chunk(h2_lo[:, k:k + 4, :], hT[:, k:k + 4, :], h2_hi[:, k:k + 4, :], 4 * N_DENSE + k // 4 + 1)
            for s, part, split in ((0, 0, 0), (2, 1, 1), (1, 0, 2)):
                for c in range(2):
                    lo_part(s, part, split, c)
            late_act(0, 0, 0)
            with dve.Fori(0, N_LATE // 2 - 1) as i:
                for m in range(2):
                    expert_sum(2 * m + 1, i + 39, 2 * i + m, splitting(2 * m, 1, 4 * i + 2 * m + 3))
                    for c in range(2):
                        lo_part(3 - 2 * m, 0, 4 * i + 2 * m + 4, c)
                    late_act(1 - m, i + m, 2 * i + m + 1)
            expert_sum(1, V_USE - 1, N_LATE - 2, splitting(3, 1, 2 * N_LATE - 1, lambda: late_act(1, N_LATE // 2 - 1, N_LATE - 1)))

            def early_sum(s, use, e):
                b = (s + 1) % 2
                loaded = (e + 1 - b) + N_LATE // 2 + 2
                expert_sum(s, use, e + N_LATE, splitting((s + 1) % 4, b, e + 1 + 2 * N_LATE, lambda: expert_act(b, loaded, e + 1 + N_LATE)))

            early_sum(3, V_USE - 1, -1)
            with dve.Fori(0, N_EARLY // 4 - 1) as i:
                for s in range(SLOTS):
                    early_sum(s, i + V_USE, 4 * i + s)
            last = V_USE + N_EARLY // 4 - 1
            for s in range(3):
                early_sum(s, last, N_EARLY - 4 + s)
            expert_sum(3, last, N_GROUP - 1)
            dve.wait_ge(S["acc_added"], 8 * N_GROUP + 2)
            gate2 = adaT[:, 5 * KT:6 * KT, :]
            for t in range(KT):
                dve.scalar_tensor_tensor(acc[:, t, 0:SEQ], acc[:, t, 0:SEQ], gate2[:, t, 0:1], xT[:, t, 0:SEQ], ALU.mult, ALU.add)
            step(dve.tensor_tensor(acc[:, :, SEQ:NT], acc[:, :, SEQ:NT], gate2[:, :, 1:NR], ALU.mult))
            dve.tensor_tensor(acc[:, :, SEQ:NT], acc[:, :, SEQ:NT], xT[:, :, SEQ:NT], ALU.add).then_inc(S["y_ready"], 1)


NORM_GROUPS = [(0, 4, 0), (4, 4, 0), (T_KC, 2, 1), (T_KS, 2, 2), (T_KW, 2, 3)]
ROPE_GROUPS = [(0, 4), (4, 4), (T_KS, 2), (T_KW, 2)]


def column_tiles(w, n):
    import numpy as np
    return np.ascontiguousarray(w.reshape(KT, P, n, 256).transpose(2, 1, 0, 3).reshape(n, P, SLOT))


def feature_major(a):
    import numpy as np
    return np.ascontiguousarray(a.T.reshape(KT, P, -1).transpose(1, 0, 2))


def packed(places, width, values):
    import numpy as np
    out = np.zeros((P, width), np.float32)
    for name, v in values.items():
        v = np.asarray(v, np.float32)
        lo, hi = places[name]
        out[:v.shape[0], lo:hi] = v.reshape(v.shape[0], hi - lo)
    return out


def shape_constants():
    import numpy as np
    p = np.arange(P)
    half = P // 2
    perm = np.zeros((P, P))
    perm[np.arange(half) + half, np.arange(half)] = -1
    perm[np.arange(half), np.arange(half) + half] = 1
    sumsel = np.zeros((P, NR))
    for g in range(4):
        sumsel[32 * g + np.arange(NR), np.arange(NR)] = 1
    inv = (10000.0 ** (-np.arange(half, dtype=np.float64) / half)).astype(np.float32)

    def rope(pos):
        ang = (pos[None, :].astype(np.float32) * inv[:, None]).astype(np.float64)
        ang = np.concatenate([ang, ang])
        return np.cos(ang), np.sin(ang)

    cos, sin = rope(np.concatenate([np.arange(SEQ), np.full(NS, PAST)]))
    cosc, sinc = rope(np.arange(N_CMP) * 16 + 31)
    t = np.arange(SEQ).reshape(2, P).T
    end = np.arange(16) * 16 + 31
    seen = end[None, None] <= t[:, :, None]
    return packed(CONSTS, N_CONST, dict(
        ident=np.eye(P), perm=perm, sumsel=sumsel, cos=cos, sin=sin, cosc=cosc, sinc=sinc,
        gsum=(p[:, None] // 32 == p[None] // 32) & (p[:, None] % 32 < REP),
        causal=np.where(np.arange(SEQ)[None, None] <= t[:, :, None], 0, NEG),
        cmpbias=np.where(seen | (t[:, :, None] < 31), 0, NEG), cmp01=seen,
        upper=p[:, None] <= p[None], lower=p[:, None] > p[None],
        levels=np.stack([((p[:, None] // b) % 2 == 1) & (p[None] // b == p[:, None] // b - 1) for b in (16, 32, 64)], 1),
        iota=np.tile(p, (P, 1)), ident16=np.tile(np.eye(16).reshape(1, -1), (P, 1)),
        blockid=np.tile(np.arange(1, 15), (P, 1))))


def lay_out(X):
    import numpy as np
    tile = lambda v: v.reshape(-1, P).T
    c = np.zeros((32, D), np.float32)
    c[0], c[1:NR] = X["c_prompt"][0], X["c_sample"]
    w = X["w_in"][0]
    o = np.cumsum([0, 1024, 1536, 24, 3072, 8, 8, 1024, 4096])
    small = np.zeros((D, SM), np.float32)
    small[:, SM_A:SM_A + H] = w[:, o[4]:o[5]]
    small[:, SM_B:SM_B + H] = w[:, o[5]:o[6]]
    small[:, SM_G:SM_G + 3 * H] = w[:, o[2]:o[3]]
    rows = lambda a: a.transpose(0, 3, 2, 1)
    ck, cv, sk, sv = (X["cache_" + n][0] for n in ("cmp_k", "cmp_v", "slc_k", "slc_v"))
    wk, wv = X["state_win_k"][0], X["state_win_v"][0]
    d = dict(
        c=feature_major(c), x=feature_major(np.concatenate([X["x_prompt"][0], X["x_sample"][:, 0]])),
        consts=shape_constants(),
        params=packed(PARAMS, N_PARAM, dict(
            bada=tile(X["b_ada"][0]), nw=np.stack([tile(X["norm1_w"][0]), tile(X["norm2_w"][0])], 1),
            hw=np.stack([X["q_norm_w"][0], *X["k_norm_w"][0]], 1), wck=X["w_cmp_k"][0].T, wcv=X["w_cmp_v"][0].T,
            bck=X["b_cmp_k"][0][:, None], bcv=X["b_cmp_v"][0][:, None],
            convw=X["dn_conv_w"][0].reshape(4, DNT, P).transpose(2, 1, 0), dnw=X["dn_norm_w"][0][:, None],
            alog=X["dn_A_log"][0][:, None], dt=X["dn_dt_bias"][0][:, None])),
        w_small=small.reshape(KT, P, SM).transpose(1, 0, 2),
        w_ada=column_tiles(X["w_ada"][0], 48),
        w_in=column_tiles(np.concatenate([w[:, o[0]:o[2]], w[:, o[3]:o[4]], w[:, o[6]:o[8]]], 1), 42),
        w_br=column_tiles(np.concatenate([X["w_br_a"][0], X["w_br_b"][0]]), 8), w_out=column_tiles(X["w_out"][0], 8),
        w_peer_q=X["w_peer_q"][0].reshape(H, KT, P, 256).transpose(0, 2, 1, 3).reshape(H, P, SLOT),
        w_keys=X["w_peer_keys"][0].reshape(2 * H, P, P).transpose(2, 0, 1),
        w_peer_u=X["w_peer_u"][0].reshape(N_GROUP, 256, KT, P).transpose(0, 3, 2, 1).reshape(N_GROUP, P, SLOT),
        w_peer_v=X["w_peer_v"][0].reshape(N_GROUP, 2, P, D).transpose(0, 2, 1, 3).reshape(N_GROUP, P, SLOT),
        pages=X["page_table"].reshape(1, NS * PAGES),
        conv_hist=X["state_conv"][0].reshape(NS, 3, DNT, P).transpose(3, 2, 1, 0),
        cache_cmp=np.stack([rows(ck), rows(cv)], 2).reshape(POOL, P, 4 * P),
        cache_slc=np.concatenate([rows(sk).reshape(POOL, P, 2 * P), sv.reshape(POOL, P, 2 * P)], 2),
        win=np.concatenate([wk.transpose(0, 3, 2, 1).reshape(NS, P, G * WIN),
                            wv.reshape(NS, 4, P, G * P).transpose(0, 2, 1, 3).reshape(NS, P, G * WIN)], 2),
        win_k_rows=wk.reshape(NS, -1)[:, G * P:], win_v_rows=wv.reshape(NS, -1)[:, G * P:],
        s_delta0=X["state_delta"][0].transpose(2, 1, 0, 3).reshape(P, 2, SLOT).transpose(1, 0, 2))
    return {k: np.ascontiguousarray(v) for k, v in d.items()}


OUTS = dict(y=(P, KT, NT), kv=(P, 12, NT), p_conv=(P, DNT, 3), p_delta=(P, H, P), s_win_k=(NS, (WIN - 1) * G * P),
            s_win_v=(NS, (WIN - 1) * G * P), s_conv=(P, DNT, 3, NS), s_delta=(2, P, SLOT))


def gather_outputs(r):
    import numpy as np
    y = r["y"].transpose(2, 1, 0).reshape(NT, D)
    kv = r["kv"].reshape(P, 6, G, NT).transpose(1, 3, 2, 0)
    win = [np.concatenate([r[n].reshape(NS, WIN - 1, G, P), kv[i, SEQ:, None]], 1)[None]
           for n, i in (("s_win_k", 4), ("s_win_v", 5))]
    out = (y[None, :SEQ], y[SEQ:, None],
           *(kv[i, :SEQ][None, None] for i in range(6)),
           r["p_conv"].transpose(2, 1, 0).reshape(1, 1, 3, DNT * P),
           r["p_delta"].transpose(1, 0, 2)[None, None],
           *(kv[i, SEQ:][None, :, None] for i in range(4)), *win,
           r["s_conv"].transpose(3, 2, 1, 0).reshape(1, NS, 3, DNT * P),
           r["s_delta"].transpose(1, 0, 2).reshape(P, H, NS, P).transpose(2, 1, 0, 3)[None])
    return tuple(np.ascontiguousarray(a) for a in out)


def kernel(**inputs):
    import numpy as _np
    import concourse.bacc as _bacc
    from concourse import mybir as _mybir
    from concourse.bass_utils import run_bass_kernel_spmd as _run

    nc = _bacc.Bacc("TRN2", target_bir_lowering=False, num_devices=1, dynamic_dma_scratch_size=1024)
    data = lay_out({k: _np.asarray(v) for k, v in inputs.items()})
    I = {k: nc.dram_tensor("in_" + k, a.shape, _mybir.dt.from_np(a.dtype), kind="ExternalInput").ap() for k, a in data.items()}
    O = {k: nc.dram_tensor("out_" + k, s, _mybir.dt.float32, kind="ExternalOutput").ap() for k, s in OUTS.items()}
    build_program(nc, I, O)
    r = _run(nc, [{"in_" + k: a for k, a in data.items()}], core_ids=[0])
    return gather_outputs({k: r.results[0]["out_" + k] for k in OUTS})
```
